# Optimizing a Trainium2 kernel written in Bass

```python
import jax, jax.numpy as jnp
from jax import lax
import numpy as np

D_MODEL = 1024
BATCH = 1
SEQ = 1024
DEPTH = 2
DEC_BATCH = 1
DEC_SEQ = 64
PAST_LEN = 1024

CHUNK = 64
N_MIXERS = 2
N_GLA_LAYERS = (DEPTH + 1) // 2
N_SWA_LAYERS = DEPTH // 2
GLA_HEADS = 4
GLA_DK = D_MODEL // 2 // GLA_HEADS
GLA_DV = D_MODEL // GLA_HEADS
GLA_GATE_RANK = 16
GLA_GATE_NORM = 16.0
SWA_HEAD_DIM = 64
SWA_Q_HEADS = D_MODEL // SWA_HEAD_DIM
SWA_KV_HEADS = 4
SWA_GROUP = SWA_Q_HEADS // SWA_KV_HEADS
WINDOW = 128
WINDOW_CHUNKS = WINDOW // CHUNK
D_FF = 4 * D_MODEL
EPS = 1e-6

kernel_name = "hybrid_gla_swa_sink_streaming_step"

def rms_norm(x, g):
    xf = x.astype(jnp.float32)
    y = xf * lax.rsqrt(jnp.mean(xf * xf, axis=-1, keepdims=True) + EPS)
    return (y * g.astype(jnp.float32)).astype(x.dtype)

def squared_relu_mlp(h, w_up, w_down):
    return jnp.square(jax.nn.relu(h @ w_up)) @ w_down

def gla_chunk(q, k, v, logf, s0):
    L = q.shape[1]
    qf, kf, vf = q.astype(jnp.float32), k.astype(jnp.float32), v.astype(jnp.float32)
    b = jnp.cumsum(logf, axis=1)
    inter = jnp.einsum('blhk,bhkv->blhv', qf * jnp.exp(b), s0)
    causal = jnp.tril(jnp.ones((L, L), dtype=bool))[None, :, :, None, None]
    diff = b[:, :, None] - b[:, None, :]
    decay = jnp.exp(jnp.where(causal, diff, -jnp.inf))
    attn = jnp.einsum('blhk,bmhk,blmhk->bhlm', qf, kf, decay)
    intra = jnp.einsum('bhlm,bmhv->blhv', attn, vf)
    b_last = b[:, -1]
    k_dec = kf * jnp.exp(b_last[:, None] - b)
    s_new = jnp.exp(b_last)[..., None] * s0 + jnp.einsum('blhk,blhv->bhkv', k_dec, vf)
    return inter + intra, s_new

def gla_mixer(h, s0, w_in, w_gate_a, w_gate_b, b_gate, g_onorm, w_out):
    B, T, _ = h.shape
    dqk = GLA_HEADS * GLA_DK
    dv = GLA_HEADS * GLA_DV
    proj = h @ w_in
    q = proj[..., :dqk].reshape(B, T, GLA_HEADS, GLA_DK) * (GLA_DK ** -0.5)
    k = proj[..., dqk:2 * dqk].reshape(B, T, GLA_HEADS, GLA_DK)
    v = proj[..., 2 * dqk:2 * dqk + dv].reshape(B, T, GLA_HEADS, GLA_DV)
    r = proj[..., 2 * dqk + dv:]
    gate_pre = ((h @ w_gate_a) @ w_gate_b + b_gate).astype(jnp.float32)
    logf = (jax.nn.log_sigmoid(gate_pre) / GLA_GATE_NORM).reshape(B, T, GLA_HEADS, GLA_DK)
    lc = min(T, CHUNK)
    n = T // lc

    def to_chunks(a):
        return jnp.moveaxis(a.reshape((B, n, lc) + a.shape[2:]), 1, 0)

    def step(s, xs):
        qc, kc, vc, fc = xs
        o, s = gla_chunk(qc, kc, vc, fc, s)
        return s, o

    s_fin, o = lax.scan(step, s0.astype(jnp.float32),
                        (to_chunks(q), to_chunks(k), to_chunks(v), to_chunks(logf)))
    o = jnp.moveaxis(o, 0, 1).reshape(B, T, GLA_HEADS, GLA_DV)
    o = o * lax.rsqrt(jnp.mean(o * o, axis=-1, keepdims=True) + EPS)
    o = o.reshape(B, T, dv) * g_onorm.astype(jnp.float32)
    o = (o * jax.nn.silu(r.astype(jnp.float32))).astype(h.dtype)
    return o @ w_out, s_fin.astype(h.dtype)

def swa_qkv(h, w_in, b_in):
    B, T, _ = h.shape
    dq = SWA_Q_HEADS * SWA_HEAD_DIM
    dkv = SWA_KV_HEADS * SWA_HEAD_DIM
    proj = h @ w_in + b_in
    q = proj[..., :dq].reshape(B, T, SWA_KV_HEADS, SWA_GROUP, SWA_HEAD_DIM)
    k = proj[..., dq:dq + dkv].reshape(B, T, SWA_KV_HEADS, SWA_HEAD_DIM)
    v = proj[..., dq + dkv:].reshape(B, T, SWA_KV_HEADS, SWA_HEAD_DIM)
    return q, k, v

def sink_attention(q, k, v, mask, sinks):
    s = jnp.einsum('bnqkgd,bnskd->bnkgqs', q, k).astype(jnp.float32) * (SWA_HEAD_DIM ** -0.5)
    s = jnp.where(mask, s, -jnp.inf)
    sink = sinks.astype(jnp.float32).reshape(SWA_KV_HEADS, SWA_GROUP)[:, :, None, None]
    m = jnp.maximum(jnp.max(s, axis=-1, keepdims=True), sink)
    p = jnp.exp(s - m)
    p = p / (jnp.sum(p, axis=-1, keepdims=True) + jnp.exp(sink - m))
    return jnp.einsum('bnkgqs,bnskd->bnqkgd', p.astype(v.dtype), v)

def swa_prompt(h, w_in, b_in, sinks, w_out, b_out):
    B, T, _ = h.shape
    n = T // CHUNK
    q, k, v = swa_qkv(h, w_in, b_in)
    pad = WINDOW_CHUNKS * CHUNK

    def band(a):
        ap = jnp.pad(a, ((0, 0), (pad, 0), (0, 0), (0, 0)))
        ap = ap.reshape(B, n + WINDOW_CHUNKS, CHUNK, SWA_KV_HEADS, SWA_HEAD_DIM)
        return jnp.concatenate([ap[:, j:j + n] for j in range(WINDOW_CHUNKS + 1)], axis=2)

    kb, vb = band(k), band(v)
    key_chunk = jnp.arange(n)[:, None] - WINDOW_CHUNKS + jnp.arange((WINDOW_CHUNKS + 1) * CHUNK)[None, :] // CHUNK
    mask = (key_chunk >= 0)[None, :, None, None, None, :]
    qb = q.reshape(B, n, CHUNK, SWA_KV_HEADS, SWA_GROUP, SWA_HEAD_DIM)
    o = sink_attention(qb, kb, vb, mask, sinks)
    o = o.reshape(B, T, SWA_Q_HEADS * SWA_HEAD_DIM) @ w_out + b_out
    keep = min(WINDOW, T)
    return o, k[:, T - keep:], v[:, T - keep:]

def swa_sample(h, cache_k, cache_v, w_in, b_in, sinks, w_out, b_out):
    B, T, _ = h.shape
    q, k, v = swa_qkv(h, w_in, b_in)
    kf = jnp.concatenate([cache_k.astype(k.dtype), k], axis=1)
    vf = jnp.concatenate([cache_v.astype(v.dtype), v], axis=1)
    o = sink_attention(q[:, None], kf[:, None], vf[:, None], True, sinks)
    o = o.reshape(B, T, SWA_Q_HEADS * SWA_HEAD_DIM) @ w_out + b_out
    keep = cache_k.shape[1]
    return o, kf[:, kf.shape[1] - keep:], vf[:, vf.shape[1] - keep:]

def trunk(x, gla_s0, swa_k0, swa_v0, gla_w_in, gla_w_gate_a, gla_w_gate_b, gla_b_gate, gla_g_onorm,
          gla_w_out, swa_w_in, swa_b_in, swa_sinks, swa_w_out, swa_b_out, norm_g, mlp_w_up, mlp_w_down):
    new_s, new_k, new_v = [], [], []
    for i in range(DEPTH):
        j = i // N_MIXERS
        h = rms_norm(x, norm_g[i, 0])
        if i % N_MIXERS == 0:
            o, s = gla_mixer(h, gla_s0[j], gla_w_in[j], gla_w_gate_a[j], gla_w_gate_b[j], gla_b_gate[j],
                             gla_g_onorm[j], gla_w_out[j])
            new_s.append(s)
        else:
            if swa_k0 is None:
                o, kc, vc = swa_prompt(h, swa_w_in[j], swa_b_in[j], swa_sinks[j], swa_w_out[j], swa_b_out[j])
            else:
                o, kc, vc = swa_sample(h, swa_k0[j], swa_v0[j], swa_w_in[j], swa_b_in[j], swa_sinks[j],
                                       swa_w_out[j], swa_b_out[j])
            new_k.append(kc)
            new_v.append(vc)
        x = x + rms_norm(o, norm_g[i, 1])
        h = rms_norm(x, norm_g[i, 2])
        x = x + rms_norm(squared_relu_mlp(h, mlp_w_up[i], mlp_w_down[i]), norm_g[i, 3])
    return x, jnp.stack(new_s), jnp.stack(new_k), jnp.stack(new_v)

def setup_inputs(seed: int = 0) -> dict:
    key = jax.random.key(seed)
    ks = jax.random.split(key, 20)

    def nrm(k, shape, scale):
        return jax.random.normal(k, shape, jnp.float32) * scale

    dqk = GLA_HEADS * GLA_DK
    dv = GLA_HEADS * GLA_DV
    dq = SWA_Q_HEADS * SWA_HEAD_DIM
    swa_cols = (SWA_Q_HEADS + 2 * SWA_KV_HEADS) * SWA_HEAD_DIM
    cache_len = min(WINDOW, PAST_LEN)
    return {
        "x_prompt": nrm(ks[0], (BATCH, SEQ, D_MODEL), 1.0),
        "x_sample": nrm(ks[1], (DEC_BATCH, DEC_SEQ, D_MODEL), 1.0),
        "state_gla": nrm(ks[2], (N_GLA_LAYERS, DEC_BATCH, GLA_HEADS, GLA_DK, GLA_DV), 0.5),
        "cache_swa_k": nrm(ks[3], (N_SWA_LAYERS, DEC_BATCH, cache_len, SWA_KV_HEADS, SWA_HEAD_DIM), 1.0),
        "cache_swa_v": nrm(ks[4], (N_SWA_LAYERS, DEC_BATCH, cache_len, SWA_KV_HEADS, SWA_HEAD_DIM), 1.0),
        "gla_w_in": nrm(ks[5], (N_GLA_LAYERS, D_MODEL, 2 * dqk + 2 * dv), D_MODEL ** -0.5),
        "gla_w_gate_a": nrm(ks[6], (N_GLA_LAYERS, D_MODEL, GLA_GATE_RANK), D_MODEL ** -0.5),
        "gla_w_gate_b": nrm(ks[7], (N_GLA_LAYERS, GLA_GATE_RANK, dqk), GLA_GATE_RANK ** -0.5),
        "gla_b_gate": nrm(ks[8], (N_GLA_LAYERS, dqk), 0.1),
        "gla_g_onorm": 1.0 + nrm(ks[9], (N_GLA_LAYERS, dv), 0.1),
        "gla_w_out": nrm(ks[10], (N_GLA_LAYERS, dv, D_MODEL), dv ** -0.5),
        "swa_w_in": nrm(ks[11], (N_SWA_LAYERS, D_MODEL, swa_cols), D_MODEL ** -0.5),
        "swa_b_in": nrm(ks[12], (N_SWA_LAYERS, swa_cols), 0.02),
        "swa_sinks": nrm(ks[13], (N_SWA_LAYERS, SWA_Q_HEADS), 1.0),
        "swa_w_out": nrm(ks[14], (N_SWA_LAYERS, dq, D_MODEL), dq ** -0.5),
        "swa_b_out": nrm(ks[15], (N_SWA_LAYERS, D_MODEL), 0.02),
        "norm_g": 1.0 + nrm(ks[16], (DEPTH, 4, D_MODEL), 0.1),
        "mlp_w_up": nrm(ks[17], (DEPTH, D_MODEL, D_FF), D_MODEL ** -0.5),
        "mlp_w_down": nrm(ks[18], (DEPTH, D_FF, D_MODEL), D_FF ** -0.5),
    }

def reference(x_prompt, x_sample, state_gla, cache_swa_k, cache_swa_v, gla_w_in, gla_w_gate_a, gla_w_gate_b,
              gla_b_gate, gla_g_onorm, gla_w_out, swa_w_in, swa_b_in, swa_sinks, swa_w_out, swa_b_out,
              norm_g, mlp_w_up, mlp_w_down):
    gla_zero = jnp.zeros((N_GLA_LAYERS, x_prompt.shape[0], GLA_HEADS, GLA_DK, GLA_DV), x_prompt.dtype)
    y_prompt, state_gla_prompt, cache_swa_k_prompt, cache_swa_v_prompt = trunk(
        x_prompt, gla_zero, None, None, gla_w_in, gla_w_gate_a, gla_w_gate_b, gla_b_gate, gla_g_onorm,
        gla_w_out, swa_w_in, swa_b_in, swa_sinks, swa_w_out, swa_b_out, norm_g, mlp_w_up, mlp_w_down)
    y_sample, state_gla_sample, cache_swa_k_sample, cache_swa_v_sample = trunk(
        x_sample, state_gla, cache_swa_k, cache_swa_v, gla_w_in, gla_w_gate_a, gla_w_gate_b, gla_b_gate,
        gla_g_onorm, gla_w_out, swa_w_in, swa_b_in, swa_sinks, swa_w_out, swa_b_out, norm_g, mlp_w_up,
        mlp_w_down)
    return (y_prompt, y_sample, state_gla_prompt, state_gla_sample, cache_swa_k_prompt, cache_swa_v_prompt,
            cache_swa_k_sample, cache_swa_v_sample)


_drawn_inputs = setup_inputs


def setup_inputs(seed=0):
    import zlib

    import numpy as np

    out = dict(_drawn_inputs(seed))
    spreads = {}
    factors = {'swa_sinks': 8.0}
    for name, (base, spread) in spreads.items():
        noise = np.random.default_rng([zlib.crc32(name.encode()), seed]).standard_normal(out[name].shape)
        drawn = base * np.exp(spread * noise) if base else spread * noise
        out[name] = __import__('jax').numpy.asarray(drawn.astype(out[name].dtype))
    for name, factor in factors.items():
        out[name] = (out[name] * factor).astype(out[name].dtype)
    return out
```

```python
from contextlib import ExitStack

import numpy as np

import concourse.bass as bass
from concourse import mybir

F32 = mybir.dt.float32
F32R = mybir.dt.float32r
ALU = mybir.AluOpType
ACT = mybir.ActivationFunctionType
AX_X = mybir.AxisListType.X

P = 128
D = 1024
KT = D // P
SEQ, DEC = 1024, 64
CHUNK = 64
T = SEQ + DEC
NB = 3
BW = 364
TP = NB * BW
UNIT = KT * P
NCH = T // CHUNK
NPAIR = (NCH + 1) // 2
EPS = 1e-6

GH, DV = 4, 256
GATE_NORM = 16.0
HALVES = (32, 16, 8, 4, 2, 1)
NLEV = len(HALVES)
CW = NLEV
KW = NLEV + 1
RANK = 16

KVP = 2
GROUP = 4
WIN = 3 * CHUNK
CACHE0 = SEQ
NEW0 = SEQ + 128
KCOLS = SEQ + 128 + DEC

FF_GROUPS = 8
FF_TILES = 4


def blocks_of(ap):
    return ap.rearrange("p (b n) -> p b n", b=NB)


class Chip:

    def __init__(self, nc, ctx):
        self.nc, self.ctx = nc, ctx
        self.shared = {}
        sb = self.sbuf
        self.h_hi = sb("h_hi", [P, KT, TP], F32R)
        self.h_lo = sb("h_lo", [P, KT, TP], F32R)
        self.y = sb("y", [P, KT, TP])
        self.w_raw = sb("w_raw", [P, 2, UNIT])
        self.w_hi = sb("w_hi", [P, 2, UNIT], F32R)
        self.w_lo = sb("w_lo", [P, 2, UNIT], F32R)
        self.ident = sb("identity", [P, P])
        self.ones = sb("all_ones", [P, P])
        self.gains = sb("gains", [P, 8, KT])
        self.banks = ctx.enter_context(nc.psum_tensor("banks", [P, 8, 512], F32))
        self.x_dram = nc.dram_tensor("x_scratch", [P, KT, TP], F32, kind="Internal").ap()

    def sbuf(self, name, shape, dtype=F32):
        return self.ctx.enter_context(self.nc.sbuf_tensor(name, shape, dtype))

    def sem(self, name):
        return self.ctx.enter_context(self.nc.semaphore(name))

    def counted(self, name):
        if name not in self.shared:
            self.shared[name] = Counted(self.sem(name))
        return self.shared[name]

    def psum_set(self, s):
        return self.banks[:, 3 * s:3 * s + 3, 0:BW]


class Counted:

    def __init__(self, sem):
        self.sem, self.base = sem, 0

    def at(self, n):
        return self.base + n


class WeightStream:

    def __init__(self, chip, name):
        self.chip = chip
        self.raw_in = [chip.sem(f"{name}_raw_in{s}") for s in range(2)]
        self.hi_done = chip.sem(f"{name}_w_hi_done")
        self.ready = chip.sem(f"{name}_w_ready")
        self.begun = chip.sem(f"{name}_w_begun")


def load_units(sp, ws, units, n_units):
    for s in range(2):
        sp.dma_start(ws.chip.w_raw[:, s], units[s]).then_inc(ws.raw_in[s], 16)
    with sp.Fori(1, n_units // 2) as i:
        for s in range(2):
            sp.wait_ge(ws.ready, 2 * i + s - 1)
            sp.dma_start(ws.chip.w_raw[:, s], units[2 * i + s]).then_inc(ws.raw_in[s], 16)


def split_units(pool, ws, n_units):
    c, nc = ws.chip, ws.chip.nc
    with pool.Fori(0, n_units // 2) as i:
        for s in range(2):
            pool.wait_ge(ws.raw_in[s], 16 * i + 16)
            pool.wait_ge(ws.begun, 2 * i + s + 1)
            raw = c.w_raw[:, s].rearrange("p (k m) -> p k m", k=KT)
            ones = c.ones[:, None, :].to_broadcast([P, KT, P])
            hi = nc.gpsimd.tensor_tensor(c.w_hi[:, s].rearrange("p (k m) -> p k m", k=KT), raw, ones, ALU.mult)
            hi.then_inc(ws.hi_done, 1)
            pool.wait_ge(ws.hi_done, 2 * i + s + 1)
            lo = nc.gpsimd.tensor_tensor(c.w_lo[:, s], c.w_raw[:, s], c.w_hi[:, s].bitcast(F32), ALU.subtract)
            lo.then_inc(ws.ready, 1)


def dense_tile(chip, s, weight_cols, slot, hi, lo, begun=None, before_k=None):
    nc = chip.nc
    n_k = hi.shape[1]
    for k in range(n_k):
        if before_k:
            before_k(k)
        at = weight_cols(k)
        w_hi, w_lo = chip.w_hi[:, slot, at:at + P], chip.w_lo[:, slot, at:at + P]
        for n, (w, x) in enumerate(((w_hi, hi), (w_hi, lo), (w_lo, hi))):
            for b in range(NB):
                mm = nc.tensor.matmul(chip.banks[:, 3 * s + b, 0:BW], w, x[:, k, b * BW:(b + 1) * BW],
                                      start=(k == 0 and n == 0), stop=(k == n_k - 1 and n == 2))
                if begun is not None:
                    mm.then_inc(begun, 1)
                    begun = None
    return mm


def boundary(chip, name, post, pre, x_parts=None, out_parts=None):
    nc = chip.nc
    with ExitStack() as ctx:
        sb = lambda n, shape, dt=F32: ctx.enter_context(nc.sbuf_tensor(f"{name}_{n}", shape, dt))
        sem = lambda n: chip.counted(f"norm_{n}")
        x = sb("x", [P, KT, TP])
        sq = sb("sq", [P, 2, TP])
        tmp = sb("tmp", [P, 2, TP])
        var = sb("var", [P, TP])
        rs = sb("rs", [P, TP])
        x_in = [sem(f"x_in{k}") for k in range(KT)]
        x_new, x_out, pad_zero = sem("x_new"), sem("x_out"), sem("pad_zero")
        sq_done, sq_used, var_done, std_done, rs_done = (
            sem("sq_done"), sem("sq_used"), sem("var_done"), sem("std_done"), sem("rs_done"))
        scaled, hi_done, lo_done = sem("scaled"), sem("hi_done"), sem("lo_done")
        n_norms = (post is not None) + (pre is not None)

        with nc.Block() as block:

            @block.sync
            def _(sp):
                for k in range(KT):
                    if x_parts is None:
                        sp.dma_start(x[:, k], chip.x_dram[:, k]).then_inc(x_in[k].sem, 16)
                    else:
                        sp.dma_start(x[:, k, 0:SEQ], x_parts[0][:, k]).then_inc(x_in[k].sem, 16)
                        sp.dma_start(x[:, k, SEQ:T], x_parts[1][:, k]).then_inc(x_in[k].sem, 16)
                n_out = 0
                for k in range(KT):
                    sp.wait_ge(x_new.sem, x_new.at(k + 1))
                    if out_parts is None:
                        sp.dma_start(chip.x_dram[:, k], x[:, k]).then_inc(x_out.sem, 16)
                        n_out += 1
                    else:
                        sp.dma_start(out_parts[0][:, k], x[:, k, 0:SEQ]).then_inc(x_out.sem, 16)
                        sp.dma_start(out_parts[1][:, k], x[:, k, SEQ:T]).then_inc(x_out.sem, 16)
                        n_out += 2
                sp.wait_ge(x_out.sem, x_out.at(16 * n_out))

            @block.scalar
            def _(act):
                for n in range(n_norms):
                    for k in range(KT):
                        if post is not None and n == 0:
                            src = chip.y[:, k]
                        else:
                            src = x[:, k]
                            act.wait_ge(x_new.sem, x_new.at(k + 1))
                        if KT * n + k >= 2:
                            act.wait_ge(sq_used.sem, sq_used.at(KT * n + k - 1))
                        nc.scalar.activation(sq[:, k % 2], src, ACT.Square).then_inc(sq_done.sem, 1)
                    act.wait_ge(var_done.sem, var_done.at(n + 1))
                    nc.scalar.activation(rs[:], var[:], ACT.Sqrt).then_inc(std_done.sem, 1)
                if pre is not None:
                    for k in range(KT):
                        act.wait_ge(scaled.sem, scaled.at((KT if post is not None else 0) + k + 1))
                        nc.scalar.copy(chip.h_hi[:, k], tmp[:, k % 2]).then_inc(hi_done.sem, 1)

            @block.tensor
            def _(pe):
                for n in range(n_norms):
                    if n:
                        pe.wait_ge(var_done.sem, var_done.at(n))
                    for k in range(KT):
                        pe.wait_ge(sq_done.sem, sq_done.at(KT * n + k + 1))
                        for b in range(NB):
                            mm = nc.tensor.matmul(chip.banks[:, b, 0:BW], chip.ones[:], sq[:, k % 2, b * BW:(b + 1) * BW],
                                                  start=(k == 0), stop=(k == KT - 1))
                        mm.then_inc(sq_used.sem, 1)

            @block.vector
            def _(dve):
                def rsqrt(n):
                    dve.wait_ge(sq_used.sem, sq_used.at(KT * (n + 1)))
                    if n:
                        dve.wait_ge(x_new.sem, x_new.at(KT))
                    nc.vector.tensor_scalar(blocks_of(var[:]), chip.psum_set(0), 1.0 / D, EPS,
                                            ALU.mult, ALU.add).then_inc(var_done.sem, 1)
                    dve.wait_ge(std_done.sem, std_done.at(n + 1))
                    nc.vector.reciprocal(rs[:], rs[:]).then_inc(rs_done.sem, 1)
                    dve.wait_ge(rs_done.sem, rs_done.at(n + 1))

                if x_parts is not None:
                    nc.vector.memset(x[:, :, T:TP], 0.0).then_inc(pad_zero.sem, 1)
                    dve.wait_ge(pad_zero.sem, pad_zero.at(1))
                    for k in range(KT):
                        dve.wait_ge(x_in[k].sem, x_in[k].at(32))
                        dve.sem_inc(x_new.sem, 1)
                n = 0
                if post is not None:
                    rsqrt(0)
                    n = 1
                    for k in range(KT):
                        if k >= 2:
                            dve.wait_ge(x_new.sem, x_new.at(k - 1))
                        nc.vector.scalar_tensor_tensor(out=tmp[:, k % 2], in0=chip.y[:, k],
                                                       scalar=chip.gains[:, post, k:k + 1], in1=rs[:],
                                                       op0=ALU.mult, op1=ALU.mult).then_inc(scaled.sem, 1)
                        dve.wait_ge(x_in[k].sem, x_in[k].at(16))
                        dve.wait_ge(scaled.sem, scaled.at(k + 1))
                        nc.vector.tensor_tensor(x[:, k], x[:, k], tmp[:, k % 2], ALU.add).then_inc(x_new.sem, 1)
                if pre is not None:
                    rsqrt(n)

                    def low_part(k):
                        dve.wait_ge(hi_done.sem, hi_done.at(k + 1))
                        nc.vector.tensor_tensor(chip.h_lo[:, k], tmp[:, k % 2], chip.h_hi[:, k].bitcast(F32), ALU.subtract).then_inc(lo_done.sem, 1)

                    for k in range(KT):
                        if k >= 2:
                            dve.wait_ge(lo_done.sem, lo_done.at(k - 1))
                        nc.vector.scalar_tensor_tensor(out=tmp[:, k % 2], in0=x[:, k],
                                                       scalar=chip.gains[:, pre, k:k + 1], in1=rs[:],
                                                       op0=ALU.mult, op1=ALU.mult).then_inc(scaled.sem, 1)
                        if k >= 1:
                            low_part(k - 1)
                    low_part(KT - 1)

        for k in range(KT):
            x_in[k].base += 16 if x_parts is None else 32
        for s, count in ((x_new, KT), (x_out, 16 * KT * (1 if out_parts is None else 2)),
                         (pad_zero, int(x_parts is not None)), (sq_done, KT * n_norms), (sq_used, KT * n_norms),
                         (var_done, n_norms), (std_done, n_norms), (rs_done, n_norms),
                         (scaled, KT * n_norms), (hi_done, KT * (pre is not None)), (lo_done, KT * (pre is not None))):
            s.base += count


def mlp(chip, name, units):
    nc = chip.nc
    with ExitStack() as ctx:
        sb = lambda n, shape, dt=F32: ctx.enter_context(nc.sbuf_tensor(f"{name}_{n}", shape, dt))
        sem = lambda n: chip.sem(f"{name}_{n}")
        relu = sb("relu", [P, 2, TP])
        act2 = sb("act2", [P, 2, TP])
        a_hi = sb("a_hi", [P, FF_TILES, TP], F32R)
        a_lo = sb("a_lo", [P, FF_TILES, TP], F32R)
        ws = WeightStream(chip, name)
        up_full, up_read, squared, a_hi_done, a_ready = (
            sem("up_full"), sem("up_read"), sem("squared"), sem("a_hi_done"), sem("a_ready"))
        down_full, y_added, y_zero = sem("down_full"), sem("y_added"), sem("y_zero")

        with nc.Block() as block:

            @block.sync
            def _(sp):
                load_units(sp, ws, units, 8 * FF_GROUPS)

            @block.gpsimd
            def _(pool):
                nc.gpsimd.memset(chip.y[:], 0.0).then_inc(y_zero, 1)
                split_units(pool, ws, 8 * FF_GROUPS)

            @block.tensor
            def _(pe):
                pe.sem_inc(ws.begun, 1)
                with pe.Fori(0, FF_GROUPS) as g:
                    for j in range(FF_TILES):
                        pe.wait_ge(ws.ready, 8 * g + j + 1)
                        if j < 2:
                            pe.wait_ge(y_added, 8 * g + j + 1)
                        else:
                            pe.wait_ge(up_read, 4 * g + j - 1)
                        mm = dense_tile(chip, j % 2, lambda k: k * P, j % 2, chip.h_hi, chip.h_lo, ws.begun)
                        mm.then_inc(up_full, 1)
                    for m in range(KT):
                        if m % 2 == 0:
                            pe.wait_ge(ws.ready, 8 * g + FF_TILES + m // 2 + 1)
                        if m < 2:
                            pe.wait_ge(up_read, 4 * g + m + 3)
                        else:
                            pe.wait_ge(y_added, 8 * g + m + 1)

                        def hidden_ready(k, m=m):
                            if m == 0:
                                pe.wait_ge(a_ready, 4 * g + k + 1)

                        mm = dense_tile(chip, m % 2, lambda k: k * 2 * P + (m % 2) * P, (m // 2) % 2, a_hi, a_lo,
                                        ws.begun if m % 2 == 0 else None, hidden_ready)
                        mm.then_inc(down_full, 1)

            @block.scalar
            def _(act):
                with act.Fori(0, FF_GROUPS) as g:

                    def high_part(j):
                        act.wait_ge(squared, 4 * g + j + 1)
                        nc.scalar.copy(a_hi[:, j], act2[:, j % 2]).then_inc(a_hi_done, 1)

                    for j in range(FF_TILES):
                        act.wait_ge(up_full, 4 * g + j + 1)
                        if j >= 2:
                            act.wait_ge(squared, 4 * g + j - 1)
                        nc.scalar.activation(blocks_of(relu[:, j % 2]), chip.psum_set(j % 2), ACT.Relu).then_inc(up_read, 1)
                        high_part(j)

            @block.vector
            def _(dve):
                dve.sem_inc(y_added, 2)
                dve.wait_ge(y_zero, 1)
                with dve.Fori(0, FF_GROUPS) as g:
                    for j in range(FF_TILES):
                        dve.wait_ge(up_read, 4 * g + j + 1)
                        if j >= 2:
                            dve.wait_ge(a_ready, 4 * g + j - 1)
                        nc.vector.tensor_tensor(act2[:, j % 2], relu[:, j % 2], relu[:, j % 2], ALU.mult).then_inc(squared, 1)
                        dve.wait_ge(a_hi_done, 4 * g + j + 1)
                        nc.vector.tensor_tensor(a_lo[:, j], act2[:, j % 2], a_hi[:, j].bitcast(F32),
                                                ALU.subtract).then_inc(a_ready, 1)
                    for m in range(KT):
                        dve.wait_ge(down_full, 8 * g + m + 1)
                        nc.vector.tensor_tensor(blocks_of(chip.y[:, m]), chip.psum_set(m % 2), blocks_of(chip.y[:, m]),
                                                ALU.add).then_inc(y_added, 1)


def gla(chip, name, ins):
    nc = chip.nc
    n_tok = lambda p: min(2 * CHUNK, T - 2 * CHUNK * p)
    n_chunks = lambda p: n_tok(p) // CHUNK
    with ExitStack() as ctx:
        sb = lambda n, shape, dt=F32: ctx.enter_context(nc.sbuf_tensor(f"{name}_{n}", shape, dt))
        sem = lambda n: chip.sem(f"{name}_{n}")
        masks = sb("masks", [P, NLEV + 1, P])
        qk = sb("qk", [P, 2, TP])
        vr = sb("vr", [P, 2, TP])
        b = sb("b", [P, TP])
        rank = sb("rank", [RANK, TP])
        gate_w = sb("gate_w", [RANK, P])
        cols = sb("cols", [P, 3])
        v_tok = sb("v_tok", [P, NPAIR, DV])
        o_hi = sb("o_hi", [P, 2, TP], F32R)
        o_lo = sb("o_lo", [P, 2, TP], F32R)
        work = sb("work", [P, 2 * TP])
        lev = work[:, 0:2 * (NLEV + 2) * P].rearrange("p (b l n) -> p b l n", b=2, l=NLEV + 2)
        flat = work[:, 0:TP]
        prod = sb("prod", [P, NLEV + 1, P])
        att = sb("att", [P, 2, P])
        kdt = sb("kdt", [P, 2, P])
        end_decay = sb("end_decay", [P, NCH])
        state = sb("state", [P, 2, 2, DV])
        s_in = sb("s_in", [P, DV])
        s_out = sb("s_out", [P, 2, DV])
        ws = WeightStream(chip, name)

        masks_in = sem("masks_in")
        const_in, state_in, state_st = sem("const_in"), sem("state_in"), sem("state_st")
        y_zero, rank_raw, rank_hi, rank_split, rank_full, rank_done = (
            sem("y_zero"), sem("rank_raw"), sem("rank_hi"), sem("rank_split"), sem("rank_full"), sem("rank_done"))
        proj_full, proj_read = sem("proj_full"), sem("proj_read")
        gate_step, gate_exp, decay_sum = sem("gate_step"), sem("gate_exp"), sem("decay_sum")
        end_exp = sem("end_exp")
        v_turned, v_copied = sem("v_turned"), sem("v_copied")
        lev_diff, lev_exp, lev_ready = sem("lev_diff"), sem("lev_exp"), sem("lev_ready")
        scores_full, masked, att_ready, kdt_ready = sem("scores_full"), sem("masked"), sem("att_ready"), sem("kdt_ready")
        upd_full, state_new, state_zero = sem("upd_full"), sem("state_new"), sem("state_zero")
        o_full, o_read = sem("o_full"), sem("o_read")
        osq_done, osum_full, ovar_done, ostd_done, ors_done = (
            sem("osq_done"), sem("osum_full"), sem("ovar_done"), sem("ostd_done"), sem("ors_done"))
        o_scaled, o_gated, o_hi_done, o_ready = sem("o_scaled"), sem("o_gated"), sem("o_hi_done"), sem("o_ready")
        out_full, y_added = sem("out_full"), sem("y_added")

        with nc.Block() as block:

            @block.sync
            def _(sp):
                sp.dma_start(masks[:], ins["masks"]).then_inc(masks_in, 16)
                sp.wait_ge(rank_hi, 1)
                raw0 = chip.w_raw[:, 0].rearrange("p (k m) -> p k m", k=KT)
                sp.dma_start(raw0[:, :, 0:RANK], ins["gate_a"]).then_inc(rank_raw, 16)
                sp.wait_ge(rank_split, 1)
                load_units(sp, ws, ins["gla_units"], 8 * GH)

            @block.gpsimd
            def _(pool):
                nc.gpsimd.memset(chip.w_raw[:, 0], 0.0).then_inc(rank_hi, 1)
                pool.wait_ge(rank_raw, 16)
                ones = chip.ones[:, None, :].to_broadcast([P, KT, P])
                view = lambda t: t[:, 0].rearrange("p (k m) -> p k m", k=KT)
                nc.gpsimd.tensor_tensor(view(chip.w_hi), view(chip.w_raw), ones, ALU.mult).then_inc(rank_hi, 1)
                pool.wait_ge(rank_hi, 2)
                nc.gpsimd.tensor_tensor(chip.w_lo[:, 0], chip.w_raw[:, 0], chip.w_hi[:, 0].bitcast(F32),
                                        ALU.subtract).then_inc(rank_split, 1)
                nc.gpsimd.memset(chip.y[:], 0.0).then_inc(y_zero, 1)
                pool.wait_ge(rank_full, 1)
                split_units(pool, ws, 8 * GH)

            @block.tensor
            def _(pe):
                pe.sem_inc(ws.begun, 1)
                pe.wait_ge(rank_split, 1)
                dense_tile(chip, 1, lambda k: k * P, 0, chip.h_hi, chip.h_lo).then_inc(rank_full, 1)
                pe.wait_ge(rank_done, 1)

                with pe.Fori(0, GH) as h:

                    def projection(n, unit):
                        if n < 2:
                            pe.wait_ge(y_added, KT * h + 1)
                        else:
                            pe.wait_ge(proj_read, 7 * h + n - 1)
                        if unit is None:
                            for blk in range(NB):
                                mm = nc.tensor.matmul(chip.banks[:, 3 * (n % 2) + blk, 0:BW], gate_w[:],
                                                      rank[:, blk * BW:(blk + 1) * BW], start=True, stop=True)
                        else:
                            pe.wait_ge(ws.ready, 8 * h + unit + 1)
                            mm = dense_tile(chip, n % 2, lambda k: k * P, unit % 2, chip.h_hi, chip.h_lo, ws.begun)
                        mm.then_inc(proj_full, 1)

                    def turn_v(p):
                        n = n_tok(p)
                        if 2 <= p < NPAIR - 2:
                            pe.wait_ge(v_copied, NPAIR * h + p - 1)
                        if p == NPAIR - 2:
                            pe.wait_ge(v_copied, NPAIR * h + p)
                        for half in range(2):
                            mm = nc.tensor.transpose(chip.banks[0:n, 6 + p % 2, half * P:(half + 1) * P],
                                                     vr[:, half, 2 * CHUNK * p:2 * CHUNK * p + n], chip.ident[:])
                        mm.then_inc(v_turned, 1)

                    def scores(p):
                        n, t0, w = n_tok(p), 2 * CHUNK * p, lev[:, p % 2]
                        pe.wait_ge(lev_ready, NPAIR * h + p + 1)
                        if p >= 2:
                            pe.wait_ge(masked, 2 * NPAIR * h + 2 * p - 2)
                            pe.wait_ge(o_read, NPAIR * h + p - 1)
                        for level in range(NLEV):
                            nc.tensor.matmul(chip.banks[0:n, 2 * (p % 2) + level // 4, (level % 4) * P:(level % 4) * P + n],
                                             w[:, level, 0:n], w[:, level, 0:n], start=True, stop=True)
                        nc.tensor.matmul(chip.banks[0:n, 2 * (p % 2) + 1, 2 * P:2 * P + n],
                                         qk[:, 1, t0:t0 + n], qk[:, 0, t0:t0 + n], start=True, stop=True)
                        nc.tensor.transpose(chip.banks[0:n, 6 + p % 2, 3 * P:4 * P], w[:, KW, 0:n],
                                            chip.ident[:]).then_inc(scores_full, 1)

                    def update(p):
                        pe.wait_ge(kdt_ready, NPAIR * h + p + 1)
                        if p >= 1:
                            pe.wait_ge(state_new, NCH * h + 2 * p)
                        for c in range(n_chunks(p)):
                            rows = slice(c * CHUNK, (c + 1) * CHUNK)
                            mm = nc.tensor.matmul(chip.banks[:, 4 + c, 0:DV], kdt[rows, p % 2, :],
                                                  v_tok[rows, p, :], start=True, stop=True)
                        mm.then_inc(upd_full, 1)

                    def output(p):
                        n = n_tok(p)
                        pe.wait_ge(att_ready, NPAIR * h + p + 1)
                        for half in range(2):
                            f = slice(half * P, (half + 1) * P)
                            out = chip.banks[:, 6 + p % 2, half * P:half * P + n]
                            nc.tensor.matmul(out, v_tok[0:n, p, f], att[0:n, p % 2, 0:n], start=True, stop=False)
                            for c in range(n_chunks(p)):
                                if half == 0:
                                    if p == NPAIR - 1:
                                        pe.wait_ge(state_in, 16 * h + 16)
                                    elif p == 0 and c == 0:
                                        pe.wait_ge(state_zero, h + 1)
                                    else:
                                        pe.wait_ge(state_new, NCH * h + 2 * p + c)
                                s = s_in[:, f] if p == NPAIR - 1 else state[:, p % 2, c, f]
                                mm = nc.tensor.matmul(out[:, c * CHUNK:(c + 1) * CHUNK], s,
                                                      lev[:, p % 2, CW, c * CHUNK:(c + 1) * CHUNK],
                                                      start=False, stop=(c == n_chunks(p) - 1))
                        mm.then_inc(o_full, 1)

                    projection(0, 0)
                    projection(1, 1)
                    pe.wait_ge(const_in, 32 * h + 32)
                    projection(2, None)
                    projection(3, 2)
                    projection(4, 3)
                    pe.wait_ge(proj_read, 7 * h + 5)
                    for p in range(NPAIR):
                        turn_v(p)
                    projection(5, 4)
                    projection(6, 5)
                    pe.wait_ge(proj_read, 7 * h + 7)
                    pe.wait_ge(v_copied, NPAIR * h + NPAIR)
                    scores(0)
                    for p in range(NPAIR):
                        if p + 1 < NPAIR:
                            scores(p + 1)
                        update(p)
                        output(p)
                    pe.wait_ge(masked, 2 * NPAIR * (h + 1))
                    for half in range(2):
                        pe.wait_ge(osq_done, 2 * h + half + 1)
                        for blk in range(NB):
                            mm = nc.tensor.matmul(chip.banks[:, blk, 0:BW], chip.ones[:],
                                                  work[:, half * TP + blk * BW:half * TP + (blk + 1) * BW],
                                                  start=(half == 0), stop=(half == 1))
                    mm.then_inc(osum_full, 1)
                    for m in range(KT):
                        if m == 0:
                            pe.wait_ge(ovar_done, h + 1)
                        if m == 1:
                            pe.wait_ge(state_new, NCH * (h + 1))
                        if m >= 2:
                            pe.wait_ge(y_added, KT * h + m)
                        if m % 4 == 0:
                            pe.wait_ge(ws.ready, 8 * h + 6 + m // 4 + 1)

                        def o_part(k, m=m):
                            if m == 0:
                                pe.wait_ge(o_ready, 2 * h + k + 2)

                        dense_tile(chip, m % 2, lambda k: k * 4 * P + (m % 4) * P, m // 4, o_hi, o_lo,
                                   ws.begun if m % 4 == 0 else None, o_part).then_inc(out_full, 1)

            @block.scalar
            def _(act):
                act.sem_inc(state_st, 16)
                act.wait_ge(rank_full, 1)
                nc.scalar.copy(blocks_of(rank[:]), chip.psum_set(1)[0:RANK]).then_inc(rank_done, 1)

                with act.Fori(0, GH) as h:
                    act.wait_ge(o_ready, 2 * h + 1)
                    act.dma_start(gate_w[:], ins["gate_b"][h]).then_inc(const_in, 16)
                    act.dma_start(cols[:], ins["gla_cols"][h]).then_inc(const_in, 16)
                    act.dma_start(s_in[:], ins["state_gla"][h]).then_inc(state_in, 16)

                    act.wait_ge(proj_full, 7 * h + 1)
                    nc.scalar.copy(blocks_of(qk[:, 1]), chip.psum_set(0)).then_inc(proj_read, 1)
                    act.wait_ge(proj_full, 7 * h + 2)
                    nc.scalar.mul(blocks_of(qk[:, 0]), chip.psum_set(1), float(P) ** -0.5).then_inc(proj_read, 1)
                    act.wait_ge(const_in, 32 * h + 32)
                    act.wait_ge(proj_full, 7 * h + 3)
                    nc.scalar.activation(blocks_of(b[:]), chip.psum_set(0), ACT.Identity,
                                         bias=cols[:, 0:1]).then_inc(proj_read, 1)
                    act.wait_ge(gate_step, 2 * h + 1)
                    nc.scalar.activation(flat, flat, ACT.Exp).then_inc(gate_exp, 1)
                    act.wait_ge(gate_exp, 2 * h + 1)
                    nc.scalar.activation(flat, flat, ACT.Ln, bias=1.0).then_inc(gate_exp, 1)
                    for half in range(2):
                        act.wait_ge(proj_full, 7 * h + 4 + half)
                        nc.scalar.copy(blocks_of(vr[:, half]), chip.psum_set((3 + half) % 2)).then_inc(proj_read, 1)
                    act.wait_ge(decay_sum, NCH * (h + 1))
                    chunk_ends = b[:, 0:T].rearrange("p (c n) -> p c n", n=CHUNK)[:, :, CHUNK - 1]
                    nc.scalar.activation(end_decay[:], chunk_ends, ACT.Exp, scale=1.0 / GATE_NORM).then_inc(end_exp, 1)
                    for p in range(NPAIR):
                        act.wait_ge(v_turned, NPAIR * h + p + 1)
                        nc.scalar.copy(v_tok[0:n_tok(p), p, :],
                                       chip.banks[0:n_tok(p), 6 + p % 2, 0:DV]).then_inc(v_copied, 1)

                    def level_exp(p):
                        n, w = n_tok(p), lev[:, p % 2]
                        act.wait_ge(lev_diff, NPAIR * h + p + 1)
                        nc.scalar.activation(w[:, :, 0:n], w[:, :, 0:n], ACT.Exp, scale=1.0 / GATE_NORM).then_inc(lev_exp, 1)

                    level_exp(0)
                    for half in range(2):
                        act.wait_ge(proj_full, 7 * h + 6 + half)
                        nc.scalar.activation(blocks_of(vr[:, half]), chip.psum_set((5 + half) % 2),
                                             ACT.Silu).then_inc(proj_read, 1)
                    level_exp(1)
                    for p in range(NPAIR):
                        n, t0 = n_tok(p), 2 * CHUNK * p
                        act.wait_ge(scores_full, NPAIR * h + p + 1)
                        if p >= 2:
                            act.wait_ge(upd_full, NPAIR * h + p - 1)
                        nc.scalar.copy(kdt[0:n, p % 2, :], chip.banks[0:n, 6 + p % 2, 3 * P:4 * P]).then_inc(kdt_ready, 1)
                        act.wait_ge(o_full, NPAIR * h + p + 1)
                        o_bank = chip.banks[:, 6 + p % 2, 0:2 * P].rearrange("p (v n) -> p v n", v=2)
                        nc.scalar.copy(qk[:, :, t0:t0 + n], o_bank[:, :, 0:n]).then_inc(o_read, 1)
                        if p + 2 < NPAIR:
                            level_exp(p + 2)
                    act.wait_ge(o_read, NPAIR * (h + 1))
                    act.wait_ge(lev_ready, NPAIR * (h + 1))
                    for half in range(2):
                        nc.scalar.activation(work[:, half * TP:(half + 1) * TP], qk[:, half], ACT.Square).then_inc(osq_done, 1)
                    act.wait_ge(state_new, NCH * (h + 1))
                    act.dma_start(ins["state_prompt"][h], s_out[:, 0]).then_inc(state_st, 16)
                    act.dma_start(ins["state_sample"][h], s_out[:, 1]).then_inc(state_st, 16)
                    act.wait_ge(ovar_done, h + 1)
                    nc.scalar.activation(b[:], b[:], ACT.Sqrt).then_inc(ostd_done, 1)
                    for half in range(2):
                        act.wait_ge(o_gated, 2 * h + half + 1)
                        nc.scalar.copy(o_hi[:, half], work[:, half * TP:(half + 1) * TP]).then_inc(o_hi_done, 1)
                act.wait_ge(state_st, 32 * GH + 16)

            @block.vector
            def _(dve):
                dve.sem_inc(o_ready, 1)
                dve.sem_inc(y_added, 1)
                dve.wait_ge(masks_in, 16)
                dve.wait_ge(y_zero, 1)
                with dve.Fori(0, GH) as h:
                    dve.wait_ge(proj_read, 7 * h + 3)
                    dve.wait_ge(o_ready, 2 * h + 1)
                    nc.vector.scalar_tensor_tensor(out=flat, in0=b[:], scalar=-1.0, in1=b[:], op0=ALU.mult,
                                                   op1=ALU.min).then_inc(gate_step, 1)
                    dve.wait_ge(gate_exp, 2 * h + 2)
                    nc.vector.scalar_tensor_tensor(out=flat, in0=b[:], scalar=0.0, in1=flat, op0=ALU.min,
                                                   op1=ALU.subtract).then_inc(gate_step, 1)
                    dve.wait_ge(gate_step, 2 * h + 2)
                    for c in range(NCH):
                        t = slice(c * CHUNK, (c + 1) * CHUNK)
                        nc.vector.tensor_tensor_scan(b[:, t], chip.ones[:, 0:CHUNK], flat[:, t], 0.0, ALU.mult,
                                                     ALU.add).then_inc(decay_sum, 1)
                    dve.wait_ge(decay_sum, NCH * (h + 1))
                    nc.vector.memset(state[:, 0, 0], 0.0).then_inc(state_zero, 1)

                    def differences(p):
                        n, w = n_tok(p), lev[:, p % 2]
                        bp = b[:, 2 * CHUNK * p:2 * CHUNK * p + n]
                        for level, s in enumerate(HALVES):
                            split = lambda x: x.rearrange("p (n two s) -> p n two s", two=2, s=s)
                            bs, out = split(bp), split(w[:, level, 0:n])
                            ref = bs[:, :, 0, s - 1:s].to_broadcast([P, n // (2 * s), s])
                            nc.vector.tensor_tensor(out[:, :, 1], bs[:, :, 1], ref, ALU.subtract)
                            nc.vector.tensor_tensor(out[:, :, 0], ref, bs[:, :, 0], ALU.subtract)
                        nc.vector.tensor_copy(w[:, CW, 0:n], bp)
                        bc, out = (x.rearrange("p (c n) -> p c n", n=CHUNK) for x in (bp, w[:, KW, 0:n]))
                        ends = bc[:, :, CHUNK - 1:CHUNK].to_broadcast([P, n_chunks(p), CHUNK])
                        nc.vector.tensor_tensor(out, ends, bc, ALU.subtract).then_inc(lev_diff, 1)

                    def decayed(p):
                        n, w = n_tok(p), lev[:, p % 2]
                        t = slice(2 * CHUNK * p, 2 * CHUNK * p + n)
                        q, k = qk[:, 0, t], qk[:, 1, t]
                        dve.wait_ge(lev_exp, NPAIR * h + p + 1)
                        for level, s in enumerate(HALVES):
                            split = lambda x: x.rearrange("p (n two s) -> p n two s", two=2, s=s)
                            out = split(w[:, level, 0:n])
                            nc.vector.tensor_tensor(out[:, :, 1], out[:, :, 1], split(q)[:, :, 1], ALU.mult)
                            nc.vector.tensor_tensor(out[:, :, 0], out[:, :, 0], split(k)[:, :, 0], ALU.mult)
                        nc.vector.tensor_tensor(w[:, CW, 0:n], w[:, CW, 0:n], q, ALU.mult)
                        nc.vector.tensor_tensor(w[:, KW, 0:n], w[:, KW, 0:n], k, ALU.mult).then_inc(lev_ready, 1)

                    def attention(p):
                        n = n_tok(p)
                        dve.wait_ge(scores_full, NPAIR * h + p + 1)
                        if p >= 1:
                            dve.wait_ge(att_ready, NPAIR * h + p)
                        for g, (l0, l1) in enumerate(((0, 4), (4, NLEV + 1))):
                            ps = chip.banks[0:n, 2 * (p % 2) + g].rearrange("p (l n) -> p l n", n=P)
                            nc.vector.tensor_tensor(prod[0:n, l0:l1, 0:n], ps[:, 0:l1 - l0, 0:n], masks[0:n, l0:l1, 0:n],
                                                    ALU.mult).then_inc(masked, 1)
                        dve.wait_ge(masked, 2 * (NPAIR * h + p + 1))
                        if p >= 2:
                            dve.wait_ge(o_full, NPAIR * h + p - 1)
                        nc.vector.tensor_reduce(att[0:n, p % 2, 0:n], prod[0:n, :, 0:n].rearrange("p l n -> p n l"),
                                                AX_X, ALU.add).then_inc(att_ready, 1)

                    def states(p):
                        dve.wait_ge(end_exp, h + 1)
                        dve.wait_ge(upd_full, NPAIR * h + p + 1)
                        if p >= 1:
                            dve.wait_ge(o_full, NPAIR * h + p)
                        for c in range(n_chunks(p)):
                            chunk = 2 * p + c
                            if p == NPAIR - 1:
                                dve.wait_ge(state_in, 16 * h + 16)
                                before, after = s_in[:], s_out[:, 1]
                            else:
                                before = state[:, p % 2, c]
                                if c == 0:
                                    after = state[:, p % 2, 1]
                                else:
                                    after = s_out[:, 0] if p == NPAIR - 2 else state[:, (p + 1) % 2, 0]
                            if chunk:
                                dve.wait_ge(state_new, NCH * h + chunk)
                            else:
                                dve.wait_ge(state_zero, h + 1)
                            if chunk == 2 * NPAIR - 3:
                                dve.wait_ge(state_st, 32 * h + 16)
                            nc.vector.scalar_tensor_tensor(out=after, in0=before, scalar=end_decay[:, chunk:chunk + 1],
                                                           in1=chip.banks[:, 4 + c, 0:DV],
                                                           op0=ALU.mult, op1=ALU.add).then_inc(state_new, 1)

                    differences(0)
                    differences(1)
                    decayed(0)
                    decayed(1)
                    for p in range(NPAIR):
                        attention(p)
                        states(p)
                        if p + 2 < NPAIR:
                            dve.wait_ge(o_full, NPAIR * h + p + 1)
                            differences(p + 2)
                        if p + 2 < NPAIR:
                            decayed(p + 2)

                    dve.wait_ge(osum_full, h + 1)
                    nc.vector.tensor_scalar(blocks_of(b[:]), chip.psum_set(0), 1.0 / DV, EPS, ALU.mult,
                                            ALU.add).then_inc(ovar_done, 1)
                    dve.wait_ge(ostd_done, h + 1)
                    nc.vector.reciprocal(b[:], b[:]).then_inc(ors_done, 1)
                    dve.wait_ge(ors_done, h + 1)
                    for half in range(2):
                        o = work[:, half * TP:(half + 1) * TP]
                        nc.vector.scalar_tensor_tensor(out=o, in0=qk[:, half], scalar=cols[:, 1 + half:2 + half],
                                                       in1=b[:], op0=ALU.mult, op1=ALU.mult).then_inc(o_scaled, 1)
                        dve.wait_ge(o_scaled, 2 * h + half + 1)
                        dve.wait_ge(proj_read, 7 * h + 7)
                        nc.vector.tensor_tensor(o, o, vr[:, half], ALU.mult).then_inc(o_gated, 1)
                    for half in range(2):
                        o = work[:, half * TP:(half + 1) * TP]
                        dve.wait_ge(o_hi_done, 2 * h + half + 1)
                        nc.vector.tensor_tensor(o_lo[:, half], o, o_hi[:, half].bitcast(F32), ALU.subtract).then_inc(o_ready, 1)
                    for m in range(KT):
                        dve.wait_ge(out_full, KT * h + m + 1)
                        nc.vector.tensor_tensor(blocks_of(chip.y[:, m]), chip.psum_set(m % 2), blocks_of(chip.y[:, m]),
                                                ALU.add).then_inc(y_added, 1)



def swa(chip, name, ins):
    nc = chip.nc
    n_tiles = KVP * GROUP
    scale = float(CHUNK) ** -0.5
    SAMPLE = NCH - 1

    def window(c):
        if c == SAMPLE:
            return CACHE0, WIN, ((0, P, SEQ // P), (P, CHUNK, SEQ // P + 1))
        if c == 0:
            return 0, CHUNK, ((0, CHUNK, 0),)
        if c == 1:
            return 0, 2 * CHUNK, ((P, P, 0),)
        first = (c - 2) // 2
        if c % 2 == 0:
            return CHUNK * (c - 2), WIN, ((0, P, first), (P, CHUNK, first + 1))
        return CHUNK * (c - 2), WIN, ((0, P, first), (P, P, first + 1))

    n_full = SEQ // P
    with ExitStack() as ctx:
        sb = lambda n, shape, dt=F32: ctx.enter_context(nc.sbuf_tensor(f"{name}_{n}", shape, dt))
        sem = lambda n: chip.sem(f"{name}_{n}")
        kT = sb("kT", [P, KVP, KCOLS])
        v_fm = sb("v_fm", [P, TP])
        v_tok = sb("v_tok", [P, KVP, n_full + 2, P])
        q_flat = sb("q_flat", [P, TP])
        q2 = sb("q2", [P, NCH, 2, CHUNK])
        prob = sb("prob", [P, 2, 2 * P])
        probT = sb("probT", [P, 2, 2, P])
        o = sb("o", [P, TP])
        o_hi = sb("o_hi", [P, 1, TP], F32R)
        o_lo = sb("o_lo", [P, 1, TP], F32R)
        biases = sb("biases", [P, n_tiles + 2 * KVP])
        out_bias = sb("out_bias", [P, KT])
        sinks = sb("sinks", [P, n_tiles])
        tile_cols = sb("tile_cols", [P, 3])
        s_max, neg_m, p_sum, p_sink, p_den, p_inv = (sb(n, [P, NCH]) for n in
                                                    ("s_max", "neg_m", "p_sum", "p_sink", "p_den", "p_inv"))
        ws = WeightStream(chip, name)

        cache_in, cache_out, const_in, y_zero, y_bias = (
            sem("cache_in"), sem("cache_out"), sem("const_in"), sem("y_zero"), sem("y_bias"))
        pads_zero, cols_ready = sem("pads_zero"), sem("cols_ready")
        kv_full, kv_read, v_turned, v_copied = sem("kv_full"), sem("kv_read"), sem("v_turned"), sem("v_copied")
        q_full, q_read, q_ready = sem("q_full"), sem("q_read"), sem("q_ready")
        scores_full, maxed, shifted = sem("scores_full"), sem("maxed"), sem("shifted")
        exp_done, sink_exp, summed, inverted, normed = (
            sem("exp_done"), sem("sink_exp"), sem("summed"), sem("inverted"), sem("normed"))
        probT_full, probT_ready = sem("probT_full"), sem("probT_ready")
        o_full, o_read, o_hi_done, o_ready = sem("o_full"), sem("o_read"), sem("o_hi_done"), sem("o_ready")
        out_full, y_added = sem("out_full"), sem("y_added")

        with nc.Block() as block:

            @block.sync
            def _(sp):
                sp.dma_start(biases[:], ins["swa_bias"]).then_inc(const_in, 16)
                sp.dma_start(out_bias[:], ins["swa_out_bias"]).then_inc(const_in, 16)
                sp.dma_start(sinks[:], ins["sinks"]).then_inc(const_in, 16)
                sp.dma_start(kT[:, :, CACHE0:NEW0], ins["cache_k"]).then_inc(cache_in, 16)
                sp.dma_start(v_tok[:, :, n_full], ins["cache_v"]).then_inc(cache_in, 16)
                load_units(sp, ws, ins["swa_units"], KVP * (2 + 2 * GROUP))
                sp.wait_ge(kv_read, 4 * KVP)
                sp.wait_ge(v_copied, KVP * NPAIR)
                sp.wait_ge(cache_in, 32)
                sp.dma_start(ins["k_prompt"], kT[:, :, SEQ - P:SEQ]).then_inc(cache_out, 16)
                sp.dma_start(ins["k_sample"], kT[:, :, KCOLS - P:KCOLS]).then_inc(cache_out, 16)
                sp.dma_start(ins["v_prompt"], v_tok[:, :, n_full - 1]).then_inc(cache_out, 16)
                sp.dma_start(ins["v_sample"][0:CHUNK], v_tok[CHUNK:P, :, n_full]).then_inc(cache_out, 16)
                sp.dma_start(ins["v_sample"][CHUNK:P], v_tok[0:CHUNK, :, n_full + 1]).then_inc(cache_out, 16)
                sp.wait_ge(cache_out, 80)

            @block.gpsimd
            def _(pool):
                nc.gpsimd.memset(chip.y[:], 0.0).then_inc(y_zero, 1)
                nc.gpsimd.memset(q2[:], 0.0).then_inc(pads_zero, 1)
                nc.gpsimd.memset(o[:], 0.0).then_inc(pads_zero, 1)
                nc.gpsimd.memset(prob[:], 0.0).then_inc(pads_zero, 1)
                split_units(pool, ws, KVP * (2 + 2 * GROUP))

            @block.tensor
            def _(pe):
                pe.sem_inc(ws.begun, 1)
                for i in range(KVP):
                    for n in range(2):
                        pe.wait_ge(ws.ready, 10 * i + n + 1)
                        if i:
                            pe.wait_ge(y_added, KT * GROUP * i + 1)
                        dense_tile(chip, n, lambda k: k * P, n, chip.h_hi, chip.h_lo, ws.begun).then_inc(kv_full, 1)
                    pe.wait_ge(kv_read, 4 * i + 4)
                    for p in range(NPAIR):
                        n = min(P, T - P * p)
                        if p >= 2:
                            pe.wait_ge(v_copied, NPAIR * i + p - 1)
                        nc.tensor.transpose(chip.banks[0:n, 6 + p % 2, 0:P], v_fm[:, P * p:P * p + n],
                                            chip.ident[:]).then_inc(v_turned, 1)
                    pe.wait_ge(v_copied, NPAIR * (i + 1))
                    pe.wait_ge(cache_in, 32)
                    with pe.Fori(0, GROUP) as g:
                        tile = g + GROUP * i
                        pe.wait_ge(ws.ready, 2 * g + 10 * i + 3)
                        pe.wait_ge(y_added, KT * tile + 1)
                        dense_tile(chip, 0, lambda k: k * P, 0, chip.h_hi, chip.h_lo, ws.begun).then_inc(q_full, 1)
                        pe.wait_ge(q_ready, 2 * tile + 2)

                        def scores(c):
                            first, n, _ = window(c)
                            if c >= 3:
                                pe.wait_ge(exp_done, NCH * tile + c - 2)
                            nc.tensor.matmul(chip.banks[:, c % 3, 0:n], q2[:, c],
                                             kT[:, i, first:first + n], start=True, stop=True).then_inc(scores_full, 1)

                        def turn(c):
                            pe.wait_ge(normed, NCH * tile + c + 1)
                            if c >= 2:
                                pe.wait_ge(probT_ready, NCH * tile + c - 1)
                            for j, (col, n, _) in enumerate(window(c)[2]):
                                n = P if j == 0 else n
                                mm = nc.tensor.transpose(chip.banks[0:n, 3 + c % 2, j * P:(j + 1) * P],
                                                         prob[:, c % 2, col:col + n], chip.ident[:])
                            mm.then_inc(probT_full, 1)

                        def output(c):
                            pe.wait_ge(probT_ready, NCH * tile + c + 1)
                            if c >= 2:
                                pe.wait_ge(o_read, 2 * (NCH * tile + c - 1))
                            parts = window(c)[2]
                            for j, (_, n, v_tile) in enumerate(parts):
                                mm = nc.tensor.matmul(chip.banks[:, 5 + c % 2, 0:P], v_tok[0:n, i, v_tile],
                                                      probT[0:n, c % 2, j], start=(j == 0), stop=(j == len(parts) - 1))
                            mm.then_inc(o_full, 1)

                        for c in range(NCH + 2):
                            if c < NCH:
                                scores(c)
                            if 1 <= c <= NCH:
                                turn(c - 1)
                            if c >= 2:
                                output(c - 2)
                        pe.wait_ge(o_ready, tile + 1)
                        pe.wait_ge(o_read, 2 * NCH * (tile + 1))
                        pe.wait_ge(ws.ready, 2 * g + 10 * i + 4)
                        for m in range(KT):
                            if m >= 2:
                                pe.wait_ge(y_added, KT * tile + m)
                            dense_tile(chip, m % 2, lambda k: m * P, 1, o_hi, o_lo,
                                       ws.begun if m == 0 else None).then_inc(out_full, 1)

            @block.scalar
            def _(act):
                act.sem_inc(o_hi_done, 1)
                act.wait_ge(const_in, 48)
                act.wait_ge(pads_zero, 3)
                for i in range(KVP):
                    act.wait_ge(kv_full, 2 * i + 1)
                    k_bias = biases[:, n_tiles + i:n_tiles + i + 1]
                    for blk in range(NB):
                        lo, hi = blk * BW, min((blk + 1) * BW, SEQ)
                        last = nc.scalar.activation(kT[:, i, lo:hi], chip.banks[:, blk, 0:hi - lo], ACT.Identity, bias=k_bias)
                    last.then_inc(kv_read, 1)
                    nc.scalar.activation(kT[:, i, NEW0:KCOLS], chip.banks[:, NB - 1, SEQ - (NB - 1) * BW:T - (NB - 1) * BW],
                                         ACT.Identity, bias=k_bias).then_inc(kv_read, 2)
                    act.wait_ge(kv_full, 2 * i + 2)
                    if i:
                        act.wait_ge(v_turned, NPAIR * i)
                    nc.scalar.activation(blocks_of(v_fm[:]), chip.psum_set(1), ACT.Identity,
                                         bias=biases[:, n_tiles + KVP + i:n_tiles + KVP + i + 1]).then_inc(kv_read, 1)
                    for p in range(NPAIR):
                        n = min(P, T - P * p)
                        act.wait_ge(v_turned, NPAIR * i + p + 1)
                        nc.scalar.copy(v_tok[0:n, i, p if p < n_full else n_full + 1],
                                       chip.banks[0:n, 6 + p % 2, 0:P]).then_inc(v_copied, 1)
                    with act.Fori(0, GROUP) as g:
                        tile = g + GROUP * i
                        act.wait_ge(q_full, tile + 1)
                        act.wait_ge(cols_ready, 3 * tile + 3)
                        nc.scalar.activation(blocks_of(q_flat[:]), chip.psum_set(0), ACT.Identity,
                                             bias=tile_cols[:, 0:1]).then_inc(q_read, 1)

                        def exps(c):
                            _, n, _ = window(c)
                            col = CHUNK * (c % 2) if n == WIN else P * (c % 2)
                            act.wait_ge(shifted, NCH * tile + c + 1)
                            if c >= 2:
                                act.wait_ge(probT_full, NCH * tile + c - 1)
                            nc.scalar.activation(p_sink[:, c:c + 1], tile_cols[:, 1:2], ACT.Exp,
                                                 bias=neg_m[:, c:c + 1]).then_inc(sink_exp, 1)
                            nc.scalar.activation(prob[:, c % 2, col:col + n], chip.banks[:, c % 3, 0:n], ACT.Exp,
                                                 bias=neg_m[:, c:c + 1], scale=scale,
                                                 accum_out=p_sum[:, c:c + 1]).then_inc(exp_done, 1)

                        def take_output(c):
                            act.wait_ge(o_full, NCH * tile + c + 1)
                            for a in range(2):
                                rows = slice(a * CHUNK, (a + 1) * CHUNK)
                                nc.scalar.copy(o[rows, CHUNK * c:CHUNK * (c + 1)],
                                               chip.banks[rows, 5 + c % 2, rows]).then_inc(o_read, 1)

                        for c in range(NCH + 2):
                            if c < NCH:
                                exps(c)
                            if c >= 2:
                                take_output(c - 2)
                        act.wait_ge(o_read, 2 * NCH * (tile + 1))
                        nc.scalar.copy(o_hi[:, 0], o[:]).then_inc(o_hi_done, 1)

            @block.vector
            def _(dve):
                dve.sem_inc(y_added, 1)
                dve.wait_ge(const_in, 48)
                dve.wait_ge(y_zero, 1)
                for k in range(KT):
                    nc.vector.tensor_scalar(chip.y[:, k], chip.y[:, k], out_bias[:, k:k + 1], None, ALU.add).then_inc(y_bias, 1)
                dve.wait_ge(y_bias, KT)
                dve.wait_ge(pads_zero, 3)
                with dve.Fori(0, n_tiles) as tile:
                    dve.wait_ge(o_hi_done, tile + 1)
                    for n, (src, sign) in enumerate(((biases, 1.0), (sinks, 1.0), (sinks, -1.0))):
                        nc.vector.tensor_scalar(tile_cols[:, n:n + 1], src[:, bass.ds(tile, 1)], sign, None,
                                                ALU.mult).then_inc(cols_ready, 1)
                    dve.wait_ge(cols_ready, 3 * tile + 3)
                    dve.wait_ge(q_read, tile + 1)
                    for a in range(2):
                        rows = slice(a * CHUNK, (a + 1) * CHUNK)
                        nc.vector.tensor_copy(q2[rows, :, a], q_flat[rows, 0:T].rearrange("p (c n) -> p c n", n=CHUNK)
                                              ).then_inc(q_ready, 1)

                    def softmax_head(c):
                        _, n, _ = window(c)
                        dve.wait_ge(scores_full, NCH * tile + c + 1)
                        nc.vector.reduce_max(s_max[:, c:c + 1], chip.banks[:, c % 3, 0:n], AX_X).then_inc(maxed, 1)
                        dve.wait_ge(maxed, NCH * tile + c + 1)
                        nc.vector.tensor_scalar(neg_m[:, c:c + 1], s_max[:, c:c + 1], -scale, tile_cols[:, 2:3],
                                                ALU.mult, ALU.min).then_inc(shifted, 1)

                    def softmax_tail(c):
                        _, n, _ = window(c)
                        col = CHUNK * (c % 2) if n == WIN else P * (c % 2)
                        dve.wait_ge(sink_exp, NCH * tile + c + 1)
                        dve.wait_ge(exp_done, NCH * tile + c + 1)
                        nc.vector.tensor_tensor(p_den[:, c:c + 1], p_sum[:, c:c + 1], p_sink[:, c:c + 1],
                                                ALU.add).then_inc(summed, 1)
                        dve.wait_ge(summed, NCH * tile + c + 1)
                        nc.vector.reciprocal(p_inv[:, c:c + 1], p_den[:, c:c + 1]).then_inc(inverted, 1)
                        dve.wait_ge(inverted, NCH * tile + c + 1)
                        nc.vector.tensor_scalar(prob[:, c % 2, col:col + n], prob[:, c % 2, col:col + n],
                                                p_inv[:, c:c + 1], None, ALU.mult).then_inc(normed, 1)

                    def copy_turned(c):
                        parts = window(c)[2]
                        n = max(k for _, k, _ in parts)
                        dve.wait_ge(probT_full, NCH * tile + c + 1)
                        if c >= 2:
                            dve.wait_ge(o_full, NCH * tile + c - 1)
                        src = chip.banks[:, 3 + c % 2, 0:2 * P].rearrange("p (j n) -> p j n", j=2)
                        if len(parts) == 1 or parts[0][1] == parts[1][1]:
                            nc.vector.tensor_copy(probT[0:n, c % 2, 0:len(parts)], src[0:n, 0:len(parts)]).then_inc(probT_ready, 1)
                        else:
                            nc.vector.tensor_copy(probT[:, c % 2, 0], src[:, 0])
                            nc.vector.tensor_copy(probT[0:CHUNK, c % 2, 1], src[0:CHUNK, 1]).then_inc(probT_ready, 1)

                    for c in range(NCH + 2):
                        if c < NCH:
                            softmax_head(c)
                        if 1 <= c <= NCH:
                            softmax_tail(c - 1)
                        if c >= 2:
                            copy_turned(c - 2)
                    dve.wait_ge(o_hi_done, tile + 2)
                    nc.vector.tensor_tensor(o_lo[:, 0], o[:], o_hi[:, 0].bitcast(F32), ALU.subtract).then_inc(o_ready, 1)
                    for m in range(KT):
                        dve.wait_ge(out_full, KT * tile + m + 1)
                        nc.vector.tensor_tensor(blocks_of(chip.y[:, m]), chip.psum_set(m % 2), blocks_of(chip.y[:, m]),
                                                ALU.add).then_inc(y_added, 1)


def build(nc, ins, outs):
    with ExitStack() as ctx:
        chip = Chip(nc, ctx)
        const_in = chip.sem("const_in")
        with nc.Block() as block:

            @block.sync
            def _(sp):
                sp.dma_start(chip.ones[:], ins["ones"]).then_inc(const_in, 16)
                sp.dma_start(chip.ident[:], ins["ident"]).then_inc(const_in, 16)
                sp.dma_start(chip.gains[:], ins["gains"]).then_inc(const_in, 16)
                sp.wait_ge(const_in, 48)

        everything = dict(ins)
        everything.update(outs)
        boundary(chip, "in", None, 0, x_parts=(ins["x_prompt"], ins["x_sample"]))
        gla(chip, "gla", everything)
        boundary(chip, "mid0", 1, 2)
        mlp(chip, "mlp0", ins["mlp_units"][0])
        boundary(chip, "next", 3, 4)
        swa(chip, "swa", everything)
        boundary(chip, "mid1", 5, 6)
        mlp(chip, "mlp1", ins["mlp_units"][1])
        boundary(chip, "out", 7, None, out_parts=(outs["y_prompt"], outs["y_sample"]))


OUT_SHAPES = {
    "y_prompt": (P, KT, SEQ), "y_sample": (P, KT, DEC),
    "state_prompt": (GH, P, DV), "state_sample": (GH, P, DV),
    "k_prompt": (P, KVP, P), "v_prompt": (P, KVP, P), "k_sample": (P, KVP, P), "v_sample": (P, KVP, P),
}


def features_first(a):
    return np.ascontiguousarray(a.T.reshape(KT, P, -1).transpose(1, 0, 2))


def k_units(w):
    return w.reshape(-1, P, w.shape[1]).transpose(1, 0, 2).reshape(P, -1)


def laid_out(inputs):
    a = {name: np.asarray(value) for name, value in inputs.items()}
    dqk = GH * P
    w_in, w_out = a["gla_w_in"][0], a["gla_w_out"][0]
    gla_units = []
    for h in range(GH):
        q, k = w_in[:, h * P:(h + 1) * P], w_in[:, dqk + h * P:dqk + (h + 1) * P]
        v, r = (w_in[:, s + h * DV:s + (h + 1) * DV] for s in (2 * dqk, 2 * dqk + GH * DV))
        o = w_out[h * DV:(h + 1) * DV]
        gla_units += [k_units(x) for x in (k, q, v[:, :P], v[:, P:], r[:, :P], r[:, P:], o[:, :512], o[:, 512:])]
    per_head = lambda x: x.reshape(GH, -1, P)
    cols = np.concatenate([per_head(a["gla_b_gate"][0]), per_head(a["gla_g_onorm"][0])], 1).transpose(0, 2, 1)

    s_in, s_out, s_b = a["swa_w_in"][0], a["swa_w_out"][0], a["swa_b_in"][0]
    n_q = s_out.shape[0]
    heads = [(8 * i + g, 8 * i + GROUP + g) for i in range(KVP) for g in range(GROUP)]
    rows = [np.concatenate([np.arange(64 * h, 64 * h + 64) for h in pair]) for pair in heads]
    kv = [n_q + np.arange(P * i, P * (i + 1)) for i in range(2 * KVP)]
    swa_units = []
    for i in range(KVP):
        swa_units += [k_units(s_in[:, kv[i]]), k_units(s_in[:, kv[KVP + i]])]
        for g in range(GROUP):
            swa_units += [k_units(s_in[:, rows[GROUP * i + g]]), s_out[rows[GROUP * i + g]]]
    mlp_units = []
    for up, down in zip(a["mlp_w_up"], a["mlp_w_down"]):
        for g in range(FF_GROUPS):
            f = slice(g * FF_TILES * P, (g + 1) * FF_TILES * P)
            mlp_units += [k_units(x) for x in np.split(up[:, f], FF_TILES, 1)]
            mlp_units += [k_units(x) for x in np.split(down[f], KT // 2, 1)]

    m, l = np.arange(P)[:, None], np.arange(P)[None, :]
    masks = [(m // (2 * s) == l // (2 * s)) & (m % (2 * s) < s) & (l % (2 * s) >= s) for s in HALVES] + [m == l]
    pack = lambda x: np.ascontiguousarray(x)
    return {
        "ones": np.ones((P, P), np.float32), "ident": np.eye(P, dtype=np.float32),
        "masks": pack(np.stack(masks, 1).astype(np.float32)),
        "gains": pack(a["norm_g"].reshape(8, KT, P).transpose(2, 0, 1)),
        "x_prompt": features_first(a["x_prompt"][0]), "x_sample": features_first(a["x_sample"][0]),
        "gla_units": np.stack(gla_units), "gate_a": pack(a["gla_w_gate_a"][0].reshape(KT, P, RANK).transpose(1, 0, 2)),
        "gate_b": pack(a["gla_w_gate_b"][0].reshape(RANK, GH, P).transpose(1, 0, 2)),
        "gla_cols": pack(cols), "state_gla": a["state_gla"][0, 0],
        "swa_units": np.stack(swa_units), "swa_bias": pack(s_b[np.stack(rows + kv)].T),
        "swa_out_bias": pack(a["swa_b_out"][0].reshape(KT, P).T),
        "sinks": pack(np.repeat(a["swa_sinks"][0][np.array(heads)], 64, 1).T),
        "cache_k": pack(a["cache_swa_k"][0, 0].reshape(P, KVP, P).transpose(2, 1, 0)),
        "cache_v": pack(a["cache_swa_v"][0, 0].reshape(P, KVP, P)),
        "mlp_units": np.stack(mlp_units).reshape(2, 8 * FF_GROUPS, P, UNIT),
    }


def kernel(**inputs):
    import concourse.bacc as bacc
    from concourse.bass_utils import run_bass_kernel_spmd

    nc = bacc.Bacc("TRN2", target_bir_lowering=False, num_devices=1)
    arrays = {f"in_{name}": array for name, array in laid_out(inputs).items()}
    ins = {name[3:]: nc.dram_tensor(name, array.shape, mybir.dt.from_np(array.dtype), kind="ExternalInput").ap()
           for name, array in arrays.items()}
    outs = {name: nc.dram_tensor(f"out_{name}", shape, F32, kind="ExternalOutput").ap()
            for name, shape in OUT_SHAPES.items()}
    build(nc, ins, outs)
    result = run_bass_kernel_spmd(nc, [arrays], core_ids=[0]).results[0]
    got = {name: np.asarray(result[f"out_{name}"]) for name in OUT_SHAPES}

    tokens_first = lambda x: np.ascontiguousarray(x.transpose(1, 0, 2).reshape(D, -1).T)[None]
    keys_first = lambda x: np.ascontiguousarray(x.transpose(2, 1, 0)).reshape(1, 1, P, 2 * KVP, 64)
    return (tokens_first(got["y_prompt"]), tokens_first(got["y_sample"]),
            got["state_prompt"][None, None], got["state_sample"][None, None],
            keys_first(got["k_prompt"]), got["v_prompt"].reshape(1, 1, P, 2 * KVP, 64),
            keys_first(got["k_sample"]), got["v_sample"].reshape(1, 1, P, 2 * KVP, 64))
```

```python
from contextlib import ExitStack

import numpy as np

import concourse.bass as bass
from concourse import mybir

F32 = mybir.dt.float32
F32R = mybir.dt.float32r
ALU = mybir.AluOpType
ACT = mybir.ActivationFunctionType
AX_X = mybir.AxisListType.X

P = 128
D = 1024
KT = D // P
SEQ, DEC = 1024, 64
CHUNK = 64
T = SEQ + DEC
NB = 3
BW = 364
TP = NB * BW
UNIT = KT * P
NCH = T // CHUNK
NPAIR = (NCH + 1) // 2
EPS = 1e-6

GH, DV = 4, 256
GATE_NORM = 16.0
HALVES = (32, 16, 8, 4, 2, 1)
NLEV = len(HALVES)
CW = NLEV
KW = NLEV + 1
RANK = 16

KVP = 2
GROUP = 4
WIN = 3 * CHUNK
CACHE0 = SEQ
NEW0 = SEQ + 128
KCOLS = SEQ + 128 + DEC

FF_GROUPS = 8
FF_TILES = 4


def blocks_of(ap):
    return ap.rearrange("p (b n) -> p b n", b=NB)


class Chip:

    def __init__(self, nc, ctx):
        self.nc, self.ctx = nc, ctx
        self.shared = {}
        sb = self.sbuf
        self.h_hi = sb("h_hi", [P, KT, TP], F32R)
        self.h_lo = sb("h_lo", [P, KT, TP], F32R)
        self.y = sb("y", [P, KT, TP])
        self.w_raw = sb("w_raw", [P, 2, UNIT])
        self.w_hi = sb("w_hi", [P, 2, UNIT], F32R)
        self.w_lo = sb("w_lo", [P, 2, UNIT], F32R)
        self.ident = sb("identity", [P, P])
        self.ones = sb("all_ones", [P, P])
        self.gains = sb("gains", [P, 8, KT])
        self.banks = ctx.enter_context(nc.psum_tensor("banks", [P, 8, 512], F32))
        self.x_dram = nc.dram_tensor("x_scratch", [P, KT, TP], F32, kind="Internal").ap()

    def sbuf(self, name, shape, dtype=F32):
        return self.ctx.enter_context(self.nc.sbuf_tensor(name, shape, dtype))

    def sem(self, name):
        return self.ctx.enter_context(self.nc.semaphore(name))

    def counted(self, name):
        if name not in self.shared:
            self.shared[name] = Counted(self.sem(name))
        return self.shared[name]

    def psum_set(self, s):
        return self.banks[:, 3 * s:3 * s + 3, 0:BW]


class Counted:

    def __init__(self, sem):
        self.sem, self.base = sem, 0

    def at(self, n):
        return self.base + n


class WeightStream:

    def __init__(self, chip, name):
        self.chip = chip
        self.raw_in = [chip.sem(f"{name}_raw_in{s}") for s in range(2)]
        self.hi_done = chip.sem(f"{name}_w_hi_done")
        self.ready = chip.sem(f"{name}_w_ready")
        self.begun = chip.sem(f"{name}_w_begun")


def load_units(sp, ws, units, n_units):
    for s in range(2):
        sp.dma_start(ws.chip.w_raw[:, s], units[s]).then_inc(ws.raw_in[s], 16)
    with sp.Fori(1, n_units // 2) as i:
        for s in range(2):
            sp.wait_ge(ws.ready, 2 * i + s - 1)
            sp.dma_start(ws.chip.w_raw[:, s], units[2 * i + s]).then_inc(ws.raw_in[s], 16)


def split_units(pool, ws, n_units):
    c, nc = ws.chip, ws.chip.nc
    with pool.Fori(0, n_units // 2) as i:
        for s in range(2):
            pool.wait_ge(ws.raw_in[s], 16 * i + 16)
            pool.wait_ge(ws.begun, 2 * i + s + 1)
            raw = c.w_raw[:, s].rearrange("p (k m) -> p k m", k=KT)
            ones = c.ones[:, None, :].to_broadcast([P, KT, P])
            hi = nc.gpsimd.tensor_tensor(c.w_hi[:, s].rearrange("p (k m) -> p k m", k=KT), raw, ones, ALU.mult)
            hi.then_inc(ws.hi_done, 1)
            pool.wait_ge(ws.hi_done, 2 * i + s + 1)
            lo = nc.gpsimd.tensor_tensor(c.w_lo[:, s], c.w_raw[:, s], c.w_hi[:, s].bitcast(F32), ALU.subtract)
            lo.then_inc(ws.ready, 1)


def dense_part(chip, s, k, n_k, at, slot, hi, lo, begun=None):
    w_hi, w_lo = chip.w_hi[:, slot, at:at + P], chip.w_lo[:, slot, at:at + P]
    for n, (w, x) in enumerate(((w_hi, hi), (w_hi, lo), (w_lo, hi))):
        for b in range(NB):
            mm = chip.nc.tensor.matmul(chip.banks[:, 3 * s + b, 0:BW], w, x[:, k, b * BW:(b + 1) * BW],
                                       start=(k == 0 and n == 0), stop=(k == n_k - 1 and n == 2))
            if begun is not None:
                mm.then_inc(begun, 1)
                begun = None
    return mm


def dense_tile(chip, s, weight_cols, slot, hi, lo, begun=None, before_k=None):
    n_k = hi.shape[1]
    for k in range(n_k):
        if before_k:
            before_k(k)
        mm = dense_part(chip, s, k, n_k, weight_cols(k), slot, hi, lo, begun if k == 0 else None)
    return mm


def boundary(chip, name, post, pre, x_parts=None, out_parts=None):
    nc = chip.nc
    with ExitStack() as ctx:
        sb = lambda n, shape, dt=F32: ctx.enter_context(nc.sbuf_tensor(f"{name}_{n}", shape, dt))
        sem = lambda n: chip.counted(f"norm_{n}")
        x = sb("x", [P, KT, TP])
        sq = sb("sq", [P, 2, TP])
        tmp = sb("tmp", [P, 2, TP])
        var = sb("var", [P, TP])
        rs = sb("rs", [P, TP])
        x_in = [sem(f"x_in{k}") for k in range(KT)]
        x_new, x_out, pad_zero = sem("x_new"), sem("x_out"), sem("pad_zero")
        sq_done, sq_used, var_done, std_done, rs_done = (
            sem("sq_done"), sem("sq_used"), sem("var_done"), sem("std_done"), sem("rs_done"))
        scaled, hi_done, lo_done = sem("scaled"), sem("hi_done"), sem("lo_done")
        n_norms = (post is not None) + (pre is not None)

        with nc.Block() as block:

            @block.sync
            def _(sp):
                for k in range(KT):
                    if x_parts is None:
                        sp.dma_start(x[:, k], chip.x_dram[:, k]).then_inc(x_in[k].sem, 16)
                    else:
                        sp.dma_start(x[:, k, 0:SEQ], x_parts[0][:, k]).then_inc(x_in[k].sem, 16)
                        sp.dma_start(x[:, k, SEQ:T], x_parts[1][:, k]).then_inc(x_in[k].sem, 16)
                n_out = 0
                for k in range(KT):
                    sp.wait_ge(x_new.sem, x_new.at(k + 1))
                    if out_parts is None:
                        sp.dma_start(chip.x_dram[:, k], x[:, k]).then_inc(x_out.sem, 16)
                        n_out += 1
                    else:
                        sp.dma_start(out_parts[0][:, k], x[:, k, 0:SEQ]).then_inc(x_out.sem, 16)
                        sp.dma_start(out_parts[1][:, k], x[:, k, SEQ:T]).then_inc(x_out.sem, 16)
                        n_out += 2
                sp.wait_ge(x_out.sem, x_out.at(16 * n_out))

            @block.scalar
            def _(act):
                for n in range(n_norms):
                    for k in range(KT):
                        if post is not None and n == 0:
                            src = chip.y[:, k]
                        else:
                            src = x[:, k]
                            act.wait_ge(x_new.sem, x_new.at(k + 1))
                        if KT * n + k >= 2:
                            act.wait_ge(sq_used.sem, sq_used.at(KT * n + k - 1))
                        nc.scalar.activation(sq[:, k % 2], src, ACT.Square).then_inc(sq_done.sem, 1)
                    act.wait_ge(var_done.sem, var_done.at(n + 1))
                    nc.scalar.activation(rs[:], var[:], ACT.Sqrt).then_inc(std_done.sem, 1)
                if pre is not None:
                    for k in range(KT):
                        act.wait_ge(scaled.sem, scaled.at((KT if post is not None else 0) + k + 1))
                        nc.scalar.copy(chip.h_hi[:, k], tmp[:, k % 2]).then_inc(hi_done.sem, 1)

            @block.tensor
            def _(pe):
                for n in range(n_norms):
                    if n:
                        pe.wait_ge(var_done.sem, var_done.at(n))
                    for k in range(KT):
                        pe.wait_ge(sq_done.sem, sq_done.at(KT * n + k + 1))
                        for b in range(NB):
                            mm = nc.tensor.matmul(chip.banks[:, b, 0:BW], chip.ones[:], sq[:, k % 2, b * BW:(b + 1) * BW],
                                                  start=(k == 0), stop=(k == KT - 1))
                        mm.then_inc(sq_used.sem, 1)

            @block.vector
            def _(dve):
                def rsqrt(n):
                    dve.wait_ge(sq_used.sem, sq_used.at(KT * (n + 1)))
                    if n:
                        dve.wait_ge(x_new.sem, x_new.at(KT))
                    nc.vector.tensor_scalar(blocks_of(var[:]), chip.psum_set(0), 1.0 / D, EPS,
                                            ALU.mult, ALU.add).then_inc(var_done.sem, 1)
                    dve.wait_ge(std_done.sem, std_done.at(n + 1))
                    nc.vector.reciprocal(rs[:], rs[:]).then_inc(rs_done.sem, 1)
                    dve.wait_ge(rs_done.sem, rs_done.at(n + 1))

                if x_parts is not None:
                    nc.vector.memset(x[:, :, T:TP], 0.0).then_inc(pad_zero.sem, 1)
                    dve.wait_ge(pad_zero.sem, pad_zero.at(1))
                    for k in range(KT):
                        dve.wait_ge(x_in[k].sem, x_in[k].at(32))
                        dve.sem_inc(x_new.sem, 1)
                n = 0
                if post is not None:
                    rsqrt(0)
                    n = 1
                    for k in range(KT):
                        if k >= 2:
                            dve.wait_ge(x_new.sem, x_new.at(k - 1))
                        nc.vector.scalar_tensor_tensor(out=tmp[:, k % 2], in0=chip.y[:, k],
                                                       scalar=chip.gains[:, post, k:k + 1], in1=rs[:],
                                                       op0=ALU.mult, op1=ALU.mult).then_inc(scaled.sem, 1)
                        dve.wait_ge(x_in[k].sem, x_in[k].at(16))
                        dve.wait_ge(scaled.sem, scaled.at(k + 1))
                        nc.vector.tensor_tensor(x[:, k], x[:, k], tmp[:, k % 2], ALU.add).then_inc(x_new.sem, 1)
                if pre is not None:
                    rsqrt(n)

                    def low_part(k):
                        dve.wait_ge(hi_done.sem, hi_done.at(k + 1))
                        nc.vector.tensor_tensor(chip.h_lo[:, k], tmp[:, k % 2], chip.h_hi[:, k].bitcast(F32), ALU.subtract).then_inc(lo_done.sem, 1)

                    for k in range(KT):
                        if k >= 2:
                            dve.wait_ge(lo_done.sem, lo_done.at(k - 1))
                        nc.vector.scalar_tensor_tensor(out=tmp[:, k % 2], in0=x[:, k],
                                                       scalar=chip.gains[:, pre, k:k + 1], in1=rs[:],
                                                       op0=ALU.mult, op1=ALU.mult).then_inc(scaled.sem, 1)
                        if k >= 1:
                            low_part(k - 1)
                    low_part(KT - 1)

        for k in range(KT):
            x_in[k].base += 16 if x_parts is None else 32
        for s, count in ((x_new, KT), (x_out, 16 * KT * (1 if out_parts is None else 2)),
                         (pad_zero, int(x_parts is not None)), (sq_done, KT * n_norms), (sq_used, KT * n_norms),
                         (var_done, n_norms), (std_done, n_norms), (rs_done, n_norms),
                         (scaled, KT * n_norms), (hi_done, KT * (pre is not None)), (lo_done, KT * (pre is not None))):
            s.base += count


def mlp(chip, name, units):
    nc = chip.nc
    with ExitStack() as ctx:
        sb = lambda n, shape, dt=F32: ctx.enter_context(nc.sbuf_tensor(f"{name}_{n}", shape, dt))
        sem = lambda n: chip.sem(f"{name}_{n}")
        relu = sb("relu", [P, 2, TP])
        act2 = sb("act2", [P, 2, TP])
        a_hi = sb("a_hi", [P, FF_TILES, TP], F32R)
        a_lo = sb("a_lo", [P, FF_TILES, TP], F32R)
        ws = WeightStream(chip, name)
        up_full, up_read, squared, a_hi_done, a_ready = (
            sem("up_full"), sem("up_read"), sem("squared"), sem("a_hi_done"), sem("a_ready"))
        down_full, y_added, y_zero = sem("down_full"), sem("y_added"), sem("y_zero")

        with nc.Block() as block:

            @block.sync
            def _(sp):
                load_units(sp, ws, units, 8 * FF_GROUPS)

            @block.gpsimd
            def _(pool):
                nc.gpsimd.memset(chip.y[:], 0.0).then_inc(y_zero, 1)
                split_units(pool, ws, 8 * FF_GROUPS)

            @block.tensor
            def _(pe):
                pe.sem_inc(ws.begun, 1)
                with pe.Fori(0, FF_GROUPS) as g:
                    for j in range(FF_TILES):
                        pe.wait_ge(ws.ready, 8 * g + j + 1)
                        if j < 2:
                            pe.wait_ge(y_added, 8 * g + j + 1)
                        else:
                            pe.wait_ge(up_read, 4 * g + j - 1)
                        mm = dense_tile(chip, j % 2, lambda k: k * P, j % 2, chip.h_hi, chip.h_lo, ws.begun)
                        mm.then_inc(up_full, 1)
                    for m in range(KT):
                        if m % 2 == 0:
                            pe.wait_ge(ws.ready, 8 * g + FF_TILES + m // 2 + 1)
                        if m < 2:
                            pe.wait_ge(up_read, 4 * g + m + 3)
                        else:
                            pe.wait_ge(y_added, 8 * g + m + 1)

                        def hidden_ready(k, m=m):
                            if m == 0:
                                pe.wait_ge(a_ready, 4 * g + k + 1)

                        mm = dense_tile(chip, m % 2, lambda k: k * 2 * P + (m % 2) * P, (m // 2) % 2, a_hi, a_lo,
                                        ws.begun if m % 2 == 0 else None, hidden_ready)
                        mm.then_inc(down_full, 1)

            @block.scalar
            def _(act):
                with act.Fori(0, FF_GROUPS) as g:

                    def high_part(j):
                        act.wait_ge(squared, 4 * g + j + 1)
                        nc.scalar.copy(a_hi[:, j], act2[:, j % 2]).then_inc(a_hi_done, 1)

                    for j in range(FF_TILES):
                        act.wait_ge(up_full, 4 * g + j + 1)
                        if j >= 2:
                            act.wait_ge(squared, 4 * g + j - 1)
                        nc.scalar.activation(blocks_of(relu[:, j % 2]), chip.psum_set(j % 2), ACT.Relu).then_inc(up_read, 1)
                        high_part(j)

            @block.vector
            def _(dve):
                dve.sem_inc(y_added, 2)
                dve.wait_ge(y_zero, 1)
                with dve.Fori(0, FF_GROUPS) as g:
                    for j in range(FF_TILES):
                        dve.wait_ge(up_read, 4 * g + j + 1)
                        if j >= 2:
                            dve.wait_ge(a_ready, 4 * g + j - 1)
                        nc.vector.tensor_tensor(act2[:, j % 2], relu[:, j % 2], relu[:, j % 2], ALU.mult).then_inc(squared, 1)
                        dve.wait_ge(a_hi_done, 4 * g + j + 1)
                        nc.vector.tensor_tensor(a_lo[:, j], act2[:, j % 2], a_hi[:, j].bitcast(F32),
                                                ALU.subtract).then_inc(a_ready, 1)
                    for m in range(KT):
                        dve.wait_ge(down_full, 8 * g + m + 1)
                        nc.vector.tensor_tensor(blocks_of(chip.y[:, m]), chip.psum_set(m % 2), blocks_of(chip.y[:, m]),
                                                ALU.add).then_inc(y_added, 1)


def gla(chip, name, ins):
    nc = chip.nc
    n_tok = lambda p: min(2 * CHUNK, T - 2 * CHUNK * p)
    n_chunks = lambda p: n_tok(p) // CHUNK
    SCORE_BANK, UPDATE_BANK, OUT_BANK = 3, 5, 7
    R_SLOTS = range(0, 8)
    OUT_SLOTS = range(8, 16)
    with ExitStack() as ctx:
        sb = lambda n, shape, dt=F32: ctx.enter_context(nc.sbuf_tensor(f"{name}_{n}", shape, dt))
        sem = lambda n: chip.sem(f"{name}_{n}")
        masks = sb("masks", [P, NLEV + 1, P])
        qk = sb("qk", [P, 2, TP])
        vr = sb("vr", [P, 2, TP])
        b = sb("b", [P, TP])
        rank = sb("rank", [RANK, TP])
        gate_w = sb("gate_w", [RANK, P])
        gate_b = sb("gate_b", [P, 1])
        o_gain = sb("o_gain", [P, 2])
        v_tok = sb("v_tok", [P, NPAIR, DV])
        o_hi = sb("o_hi", [P, 2, TP], F32R)
        o_lo = sb("o_lo", [P, 2, TP], F32R)
        work = sb("work", [P, 2 * TP])
        lev = work[:, 0:2 * (NLEV + 2) * P].rearrange("p (b l n) -> p b l n", b=2, l=NLEV + 2)
        flat = work[:, 0:TP]
        prod = sb("prod", [P, NLEV + 1, P])
        att = sb("att", [P, 2, P])
        kdt = sb("kdt", [P, 2, P])
        end_decay = sb("end_decay", [P, NCH])
        state = sb("state", [P, 2, 2, DV])
        s_in = sb("s_in", [P, DV])
        s_out = sb("s_out", [P, 2, DV])
        ws = WeightStream(chip, name)

        masks_in = sem("masks_in")
        const_in, gain_in, state_in, state_st = sem("const_in"), sem("gain_in"), sem("state_in"), sem("state_st")
        y_zero, rank_raw, rank_hi, rank_split, rank_full, rank_done = (
            sem("y_zero"), sem("rank_raw"), sem("rank_hi"), sem("rank_split"), sem("rank_full"), sem("rank_done"))
        proj_full, proj_read = sem("proj_full"), sem("proj_read")
        gate_step, gate_exp, decay_sum = sem("gate_step"), sem("gate_exp"), sem("decay_sum")
        end_exp = sem("end_exp")
        v_turned, v_copied = sem("v_turned"), sem("v_copied")
        lev_diff, lev_exp, lev_ready = sem("lev_diff"), sem("lev_exp"), sem("lev_ready")
        scores_full, masked, att_ready, kdt_ready = sem("scores_full"), sem("masked"), sem("att_ready"), sem("kdt_ready")
        upd_full, state_new, state_zero = sem("upd_full"), sem("state_new"), sem("state_zero")
        o_full, o_read = sem("o_full"), sem("o_read")
        osq_done, osum_full, ovar_done, ostd_done, ors_done = (
            sem("osq_done"), sem("osum_full"), sem("ovar_done"), sem("ostd_done"), sem("ors_done"))
        o_scaled, o_gated, o_hi_done, o_ready = sem("o_scaled"), sem("o_gated"), sem("o_hi_done"), sem("o_ready")
        out_full, y_added = sem("out_full"), sem("y_added")

        with nc.Block() as block:

            @block.sync
            def _(sp):
                sp.dma_start(masks[:], ins["masks"]).then_inc(masks_in, 16)
                sp.wait_ge(rank_hi, 1)
                raw0 = chip.w_raw[:, 0].rearrange("p (k m) -> p k m", k=KT)
                sp.dma_start(raw0[:, :, 0:RANK], ins["gate_a"]).then_inc(rank_raw, 16)
                sp.wait_ge(rank_split, 1)
                load_units(sp, ws, ins["gla_units"], 8 * GH)

            @block.gpsimd
            def _(pool):
                nc.gpsimd.memset(chip.w_raw[:, 0], 0.0).then_inc(rank_hi, 1)
                pool.wait_ge(rank_raw, 16)
                ones = chip.ones[:, None, :].to_broadcast([P, KT, P])
                view = lambda t: t[:, 0].rearrange("p (k m) -> p k m", k=KT)
                nc.gpsimd.tensor_tensor(view(chip.w_hi), view(chip.w_raw), ones, ALU.mult).then_inc(rank_hi, 1)
                pool.wait_ge(rank_hi, 2)
                nc.gpsimd.tensor_tensor(chip.w_lo[:, 0], chip.w_raw[:, 0], chip.w_hi[:, 0].bitcast(F32),
                                        ALU.subtract).then_inc(rank_split, 1)
                nc.gpsimd.memset(chip.y[:], 0.0).then_inc(y_zero, 1)
                pool.wait_ge(rank_full, 1)
                split_units(pool, ws, 8 * GH)

            @block.tensor
            def _(pe):
                pe.sem_inc(ws.begun, 1)
                pe.wait_ge(rank_split, 1)
                dense_tile(chip, 1, lambda k: k * P, 0, chip.h_hi, chip.h_lo).then_inc(rank_full, 1)
                pe.wait_ge(rank_done, 1)

                def unit_ready(h, unit):
                    pe.wait_ge(ws.ready, (unit if isinstance(h, int) and h == 0 else 8 * h - 2 + unit) + 1)

                def o_square_sums(h):
                    pe.wait_ge(masked, 2 * NPAIR * h)
                    pe.wait_ge(state_new, NCH * h)
                    for half in range(2):
                        pe.wait_ge(osq_done, 2 * h + half - 1)
                        for blk in range(NB):
                            mm = nc.tensor.matmul(chip.banks[:, 3 + blk, 0:BW], chip.ones[:],
                                                  work[:, half * TP + blk * BW:half * TP + (blk + 1) * BW],
                                                  start=(half == 0), stop=(half == 1))
                    mm.then_inc(osum_full, 1)

                def output_tile(h, m, s, stationary_slot):
                    if m == 0:
                        pe.wait_ge(o_ready, 2 * h)
                    dense_tile(chip, s, lambda k: k * 4 * P + (m % 4) * P, stationary_slot, o_hi, o_lo,
                               ws.begun if m % 4 == 0 else None).then_inc(out_full, 1)

                def head(h, is_first):

                    def projection(n, unit, k_tiles=range(KT)):
                        s = n % 2 if n < 5 else 0
                        if 0 in k_tiles and unit is not None:
                            unit_ready(h, unit)
                        if unit is None:
                            for blk in range(NB):
                                mm = nc.tensor.matmul(chip.banks[:, 3 * s + blk, 0:BW], gate_w[:],
                                                      rank[:, blk * BW:(blk + 1) * BW], start=True, stop=True)
                        else:
                            for k in k_tiles:
                                mm = dense_part(chip, s, k, KT, k * P, unit % 2, chip.h_hi, chip.h_lo,
                                                ws.begun if k == 0 else None)
                        if unit is None or KT - 1 in k_tiles:
                            mm.then_inc(proj_full, 1)

                    def turn_v(p):
                        n = n_tok(p)
                        if 2 <= p < NPAIR - 2:
                            pe.wait_ge(v_copied, NPAIR * h + p - 1)
                        if p == NPAIR - 2:
                            pe.wait_ge(v_copied, NPAIR * h + p)
                        for half in range(2):
                            mm = nc.tensor.transpose(chip.banks[0:n, 6 + p % 2, half * P:(half + 1) * P],
                                                     vr[:, half, 2 * CHUNK * p:2 * CHUNK * p + n], chip.ident[:])
                        mm.then_inc(v_turned, 1)

                    def scores(p):
                        n, t0, w = n_tok(p), 2 * CHUNK * p, lev[:, p % 2]
                        pe.wait_ge(lev_ready, NPAIR * h + p + 1)
                        if p >= 1:
                            pe.wait_ge(masked, 2 * (NPAIR * h + p))
                        for level in range(NLEV):
                            nc.tensor.matmul(chip.banks[0:n, SCORE_BANK + level // 4, (level % 4) * P:(level % 4) * P + n],
                                             w[:, level, 0:n], w[:, level, 0:n], start=True, stop=True)
                        if p >= 1:
                            pe.wait_ge(o_read, NPAIR * h + p)
                        nc.tensor.matmul(chip.banks[0:n, SCORE_BANK + 1, 2 * P:2 * P + n],
                                         qk[:, 1, t0:t0 + n], qk[:, 0, t0:t0 + n], start=True, stop=True)
                        nc.tensor.transpose(chip.banks[0:n, OUT_BANK, 3 * P:4 * P], w[:, KW, 0:n],
                                            chip.ident[:]).then_inc(scores_full, 1)

                    def update(p):
                        pe.wait_ge(kdt_ready, NPAIR * h + p + 1)
                        if p >= 1:
                            pe.wait_ge(state_new, NCH * h + 2 * p)
                        for c in range(n_chunks(p)):
                            rows = slice(c * CHUNK, (c + 1) * CHUNK)
                            mm = nc.tensor.matmul(chip.banks[:, UPDATE_BANK + c, 0:DV], kdt[rows, p % 2, :],
                                                  v_tok[rows, p, :], start=True, stop=True)
                        mm.then_inc(upd_full, 1)

                    def output(p):
                        n = n_tok(p)
                        pe.wait_ge(att_ready, NPAIR * h + p + 1)
                        for half in range(2):
                            f = slice(half * P, (half + 1) * P)
                            out = chip.banks[:, OUT_BANK, half * P:half * P + n]
                            nc.tensor.matmul(out, v_tok[0:n, p, f], att[0:n, p % 2, 0:n], start=True, stop=False)
                            for c in range(n_chunks(p)):
                                if half == 0:
                                    if p == NPAIR - 1:
                                        pe.wait_ge(state_in, 16 * h + 16)
                                    elif p == 0 and c == 0:
                                        pe.wait_ge(state_zero, h + 1)
                                    else:
                                        pe.wait_ge(state_new, NCH * h + 2 * p + c)
                                s = s_in[:, f] if p == NPAIR - 1 else state[:, p % 2, c, f]
                                mm = nc.tensor.matmul(out[:, c * CHUNK:(c + 1) * CHUNK], s,
                                                      lev[:, p % 2, CW, c * CHUNK:(c + 1) * CHUNK],
                                                      start=False, stop=(c == n_chunks(p) - 1))
                        mm.then_inc(o_full, 1)

                    def dense_slot(n):
                        if n in R_SLOTS:
                            if n == 4:
                                pe.wait_ge(proj_read, 7 * h + 6)
                            projection(5 + n // 4, 4 + n // 4, range(2 * (n % 4), 2 * (n % 4) + 2))
                        if n in OUT_SLOTS and not is_first:
                            m = n - OUT_SLOTS.start
                            if m == 0:
                                pe.wait_ge(proj_read, 7 * h + 7)
                            else:
                                pe.wait_ge(y_added, KT * (h - 1) + m + 1)
                            if m % 4 == 0:
                                unit_ready(h, 6 + m // 4)
                            output_tile(h, m, 0, m // 4)

                    if is_first:
                        projection(0, 0)
                    else:
                        pe.wait_ge(y_added, KT * (h - 1) + 1)
                        projection(0, 0, range(0, 3))
                        o_square_sums(h)
                        projection(0, 0, range(3, KT))
                        pe.wait_ge(ovar_done, h)
                    projection(1, 1)
                    pe.wait_ge(const_in, 32 * h + 32)
                    pe.wait_ge(proj_read, 7 * h + 1)
                    projection(2, None)
                    pe.wait_ge(proj_read, 7 * h + 2)
                    projection(3, 2)
                    pe.wait_ge(proj_read, 7 * h + 3)
                    projection(4, 3)
                    pe.wait_ge(proj_read, 7 * h + 5)
                    for p in range(NPAIR):
                        turn_v(p)
                    pe.wait_ge(v_copied, NPAIR * h + NPAIR)
                    for p in range(NPAIR):
                        scores(p)
                        dense_slot(2 * p)
                        update(p)
                        output(p)
                        dense_slot(2 * p + 1)

                head(0, True)
                with pe.Fori(1, GH) as h:
                    head(h, False)
                o_square_sums(GH)
                for m in range(KT):
                    if m == 0:
                        pe.wait_ge(y_added, KT * (GH - 1) + 1)
                    if m == 1:
                        pe.wait_ge(ovar_done, GH)
                    if m >= 2:
                        pe.wait_ge(y_added, KT * (GH - 1) + m)
                    if m % 4 == 0:
                        unit_ready(GH, m // 4)
                    output_tile(GH, m, m % 2, m // 4)

            @block.scalar
            def _(act):
                act.sem_inc(state_st, 16)
                act.wait_ge(rank_full, 1)
                nc.scalar.copy(blocks_of(rank[:]), chip.psum_set(1)[0:RANK]).then_inc(rank_done, 1)

                def squares(h):
                    act.wait_ge(o_read, NPAIR * h)
                    act.wait_ge(lev_ready, NPAIR * h)
                    for half in range(2):
                        nc.scalar.activation(work[:, half * TP:(half + 1) * TP], qk[:, half], ACT.Square).then_inc(osq_done, 1)
                    act.wait_ge(state_new, NCH * h)
                    act.dma_start(ins["state_prompt"][bass.ds(h - 1, 1)], s_out[:, 0]).then_inc(state_st, 16)
                    act.dma_start(ins["state_sample"][bass.ds(h - 1, 1)], s_out[:, 1]).then_inc(state_st, 16)

                def high_parts(h):
                    for half in range(2):
                        act.wait_ge(o_gated, 2 * h + half - 1)
                        nc.scalar.copy(o_hi[:, half], work[:, half * TP:(half + 1) * TP]).then_inc(o_hi_done, 1)

                def head(h, is_first):
                    if not is_first:
                        squares(h)
                    act.dma_start(gate_w[:], ins["gate_b"][h]).then_inc(const_in, 16)
                    act.dma_start(gate_b[:], ins["gate_bias"][h]).then_inc(const_in, 16)
                    act.dma_start(s_in[:], ins["state_gla"][h]).then_inc(state_in, 16)
                    if not is_first:
                        act.wait_ge(ovar_done, h)
                        nc.scalar.activation(b[:], b[:], ACT.Sqrt).then_inc(ostd_done, 1)
                        act.wait_ge(o_scaled, 2 * h)
                    act.dma_start(o_gain[:], ins["gla_gain"][h]).then_inc(gain_in, 16)
                    act.wait_ge(proj_full, 7 * h + 1)
                    nc.scalar.copy(blocks_of(qk[:, 1]), chip.psum_set(0)).then_inc(proj_read, 1)
                    if not is_first:
                        high_parts(h)
                    act.wait_ge(proj_full, 7 * h + 2)
                    nc.scalar.mul(blocks_of(qk[:, 0]), chip.psum_set(1), float(P) ** -0.5).then_inc(proj_read, 1)
                    act.wait_ge(const_in, 32 * h + 32)
                    act.wait_ge(proj_full, 7 * h + 3)
                    nc.scalar.activation(blocks_of(b[:]), chip.psum_set(0), ACT.Identity,
                                         bias=gate_b[:]).then_inc(proj_read, 1)
                    act.wait_ge(gate_step, 2 * h + 1)
                    nc.scalar.activation(flat, flat, ACT.Exp).then_inc(gate_exp, 1)
                    act.wait_ge(gate_exp, 2 * h + 1)
                    nc.scalar.activation(flat, flat, ACT.Ln, bias=1.0).then_inc(gate_exp, 1)
                    for half in range(2):
                        act.wait_ge(proj_full, 7 * h + 4 + half)
                        nc.scalar.copy(blocks_of(vr[:, half]), chip.psum_set((3 + half) % 2)).then_inc(proj_read, 1)
                    act.wait_ge(decay_sum, NCH * (h + 1))
                    chunk_ends = b[:, 0:T].rearrange("p (c n) -> p c n", n=CHUNK)[:, :, CHUNK - 1]
                    nc.scalar.activation(end_decay[:], chunk_ends, ACT.Exp, scale=1.0 / GATE_NORM).then_inc(end_exp, 1)

                    def level_exp(p):
                        n, w = n_tok(p), lev[:, p % 2]
                        act.wait_ge(lev_diff, NPAIR * h + p + 1)
                        nc.scalar.activation(w[:, :, 0:n], w[:, :, 0:n], ACT.Exp, scale=1.0 / GATE_NORM).then_inc(lev_exp, 1)

                    level_exp(0)
                    level_exp(1)
                    for p in range(NPAIR):
                        act.wait_ge(v_turned, NPAIR * h + p + 1)
                        nc.scalar.copy(v_tok[0:n_tok(p), p, :],
                                       chip.banks[0:n_tok(p), 6 + p % 2, 0:DV]).then_inc(v_copied, 1)
                    for p in range(NPAIR):
                        n, t0 = n_tok(p), 2 * CHUNK * p
                        if p in (2, 4):
                            half = p // 2 - 1
                            act.wait_ge(proj_full, 7 * h + 6 + half)
                            nc.scalar.activation(blocks_of(vr[:, half]), chip.psum_set(0), ACT.Silu).then_inc(proj_read, 1)
                        act.wait_ge(scores_full, NPAIR * h + p + 1)
                        if p >= 2:
                            act.wait_ge(upd_full, NPAIR * h + p - 1)
                        nc.scalar.copy(kdt[0:n, p % 2, :], chip.banks[0:n, OUT_BANK, 3 * P:4 * P]).then_inc(kdt_ready, 1)
                        act.wait_ge(o_full, NPAIR * h + p + 1)
                        o_bank = chip.banks[:, OUT_BANK, 0:2 * P].rearrange("p (v n) -> p v n", v=2)
                        nc.scalar.copy(qk[:, :, t0:t0 + n], o_bank[:, :, 0:n]).then_inc(o_read, 1)
                        if p + 2 < NPAIR:
                            level_exp(p + 2)

                head(0, True)
                with act.Fori(1, GH) as h:
                    head(h, False)
                squares(GH)
                act.wait_ge(ovar_done, GH)
                nc.scalar.activation(b[:], b[:], ACT.Sqrt).then_inc(ostd_done, 1)
                high_parts(GH)
                act.wait_ge(state_st, 32 * GH + 16)

            @block.vector
            def _(dve):
                dve.sem_inc(y_added, 1)
                dve.wait_ge(masks_in, 16)
                dve.wait_ge(y_zero, 1)

                def norm_and_gate(h):
                    dve.wait_ge(lev_diff, NPAIR * h)
                    dve.wait_ge(osum_full, h)
                    nc.vector.tensor_scalar(blocks_of(b[:]), chip.psum_set(1), 1.0 / DV, EPS, ALU.mult,
                                            ALU.add).then_inc(ovar_done, 1)
                    dve.wait_ge(ostd_done, h)
                    nc.vector.reciprocal(b[:], b[:]).then_inc(ors_done, 1)
                    dve.wait_ge(ors_done, h)
                    dve.wait_ge(gain_in, 16 * h)
                    for half in range(2):
                        o = work[:, half * TP:(half + 1) * TP]
                        nc.vector.scalar_tensor_tensor(out=o, in0=qk[:, half], scalar=o_gain[:, half:half + 1],
                                                       in1=b[:], op0=ALU.mult, op1=ALU.mult).then_inc(o_scaled, 1)
                    dve.wait_ge(proj_read, 7 * h)
                    dve.wait_ge(o_scaled, 2 * h)
                    for half in range(2):
                        o = work[:, half * TP:(half + 1) * TP]
                        nc.vector.tensor_tensor(o, o, vr[:, half], ALU.mult).then_inc(o_gated, 1)
                    for half in range(2):
                        o = work[:, half * TP:(half + 1) * TP]
                        dve.wait_ge(o_hi_done, 2 * h + half - 1)
                        nc.vector.tensor_tensor(o_lo[:, half], o, o_hi[:, half].bitcast(F32), ALU.subtract).then_inc(o_ready, 1)

                def add_output(h, m, s):
                    dve.wait_ge(out_full, KT * (h - 1) + m + 1)
                    nc.vector.tensor_tensor(blocks_of(chip.y[:, m]), chip.psum_set(s), blocks_of(chip.y[:, m]),
                                            ALU.add).then_inc(y_added, 1)

                def head(h, is_first):
                    if not is_first:
                        norm_and_gate(h)
                        dve.wait_ge(o_ready, 2 * h)
                    dve.wait_ge(proj_read, 7 * h + 3)
                    nc.vector.scalar_tensor_tensor(out=flat, in0=b[:], scalar=-1.0, in1=b[:], op0=ALU.mult,
                                                   op1=ALU.min).then_inc(gate_step, 1)
                    dve.wait_ge(gate_exp, 2 * h + 2)
                    nc.vector.scalar_tensor_tensor(out=flat, in0=b[:], scalar=0.0, in1=flat, op0=ALU.min,
                                                   op1=ALU.subtract).then_inc(gate_step, 1)
                    dve.wait_ge(gate_step, 2 * h + 2)
                    for c in range(NCH):
                        t = slice(c * CHUNK, (c + 1) * CHUNK)
                        nc.vector.tensor_tensor_scan(b[:, t], chip.ones[:, 0:CHUNK], flat[:, t], 0.0, ALU.mult,
                                                     ALU.add).then_inc(decay_sum, 1)
                    dve.wait_ge(decay_sum, NCH * (h + 1))
                    nc.vector.memset(state[:, 0, 0], 0.0).then_inc(state_zero, 1)

                    def differences(p):
                        n, w = n_tok(p), lev[:, p % 2]
                        bp = b[:, 2 * CHUNK * p:2 * CHUNK * p + n]
                        for level, s in enumerate(HALVES):
                            split = lambda x: x.rearrange("p (n two s) -> p n two s", two=2, s=s)
                            bs, out = split(bp), split(w[:, level, 0:n])
                            ref = bs[:, :, 0, s - 1:s].to_broadcast([P, n // (2 * s), s])
                            nc.vector.tensor_tensor(out[:, :, 1], bs[:, :, 1], ref, ALU.subtract)
                            nc.vector.tensor_tensor(out[:, :, 0], ref, bs[:, :, 0], ALU.subtract)
                        nc.vector.tensor_copy(w[:, CW, 0:n], bp)
                        bc, out = (x.rearrange("p (c n) -> p c n", n=CHUNK) for x in (bp, w[:, KW, 0:n]))
                        ends = bc[:, :, CHUNK - 1:CHUNK].to_broadcast([P, n_chunks(p), CHUNK])
                        nc.vector.tensor_tensor(out, ends, bc, ALU.subtract).then_inc(lev_diff, 1)

                    def decayed(p):
                        n, w = n_tok(p), lev[:, p % 2]
                        t = slice(2 * CHUNK * p, 2 * CHUNK * p + n)
                        q, k = qk[:, 0, t], qk[:, 1, t]
                        dve.wait_ge(lev_exp, NPAIR * h + p + 1)
                        for level, s in enumerate(HALVES):
                            split = lambda x: x.rearrange("p (n two s) -> p n two s", two=2, s=s)
                            out = split(w[:, level, 0:n])
                            nc.vector.tensor_tensor(out[:, :, 1], out[:, :, 1], split(q)[:, :, 1], ALU.mult)
                            nc.vector.tensor_tensor(out[:, :, 0], out[:, :, 0], split(k)[:, :, 0], ALU.mult)
                        nc.vector.tensor_tensor(w[:, CW, 0:n], w[:, CW, 0:n], q, ALU.mult)
                        nc.vector.tensor_tensor(w[:, KW, 0:n], w[:, KW, 0:n], k, ALU.mult).then_inc(lev_ready, 1)

                    def attention(p):
                        n = n_tok(p)
                        dve.wait_ge(scores_full, NPAIR * h + p + 1)
                        if p >= 1:
                            dve.wait_ge(att_ready, NPAIR * h + p)
                        for g, (l0, l1) in enumerate(((0, 4), (4, NLEV + 1))):
                            ps = chip.banks[0:n, SCORE_BANK + g].rearrange("p (l n) -> p l n", n=P)
                            nc.vector.tensor_tensor(prod[0:n, l0:l1, 0:n], ps[:, 0:l1 - l0, 0:n], masks[0:n, l0:l1, 0:n],
                                                    ALU.mult).then_inc(masked, 1)
                        dve.wait_ge(masked, 2 * (NPAIR * h + p + 1))
                        if p >= 2:
                            dve.wait_ge(o_full, NPAIR * h + p - 1)
                        nc.vector.tensor_reduce(att[0:n, p % 2, 0:n], prod[0:n, :, 0:n].rearrange("p l n -> p n l"),
                                                AX_X, ALU.add).then_inc(att_ready, 1)

                    def states(p):
                        dve.wait_ge(end_exp, h + 1)
                        dve.wait_ge(upd_full, NPAIR * h + p + 1)
                        if p >= 1:
                            dve.wait_ge(o_full, NPAIR * h + p)
                        for c in range(n_chunks(p)):
                            chunk = 2 * p + c
                            if p == NPAIR - 1:
                                dve.wait_ge(state_in, 16 * h + 16)
                                before, after = s_in[:], s_out[:, 1]
                            else:
                                before = state[:, p % 2, c]
                                if c == 0:
                                    after = state[:, p % 2, 1]
                                else:
                                    after = s_out[:, 0] if p == NPAIR - 2 else state[:, (p + 1) % 2, 0]
                            if chunk:
                                dve.wait_ge(state_new, NCH * h + chunk)
                            else:
                                dve.wait_ge(state_zero, h + 1)
                            if chunk == 2 * NPAIR - 3:
                                dve.wait_ge(state_st, 32 * h + 16)
                            nc.vector.scalar_tensor_tensor(out=after, in0=before, scalar=end_decay[:, chunk:chunk + 1],
                                                           in1=chip.banks[:, UPDATE_BANK + c, 0:DV],
                                                           op0=ALU.mult, op1=ALU.add).then_inc(state_new, 1)

                    differences(0)
                    differences(1)
                    decayed(0)
                    for p in range(NPAIR):
                        attention(p)
                        if p + 1 < NPAIR:
                            decayed(p + 1)
                        if 2 * p in OUT_SLOTS and not is_first:
                            add_output(h, 2 * p - OUT_SLOTS.start, 0)
                        states(p)
                        if p + 2 < NPAIR:
                            dve.wait_ge(o_full, NPAIR * h + p + 1)
                            differences(p + 2)
                        if 2 * p + 1 in OUT_SLOTS and not is_first:
                            add_output(h, 2 * p + 1 - OUT_SLOTS.start, 0)

                head(0, True)
                with dve.Fori(1, GH) as h:
                    head(h, False)
                norm_and_gate(GH)
                for m in range(KT):
                    add_output(GH, m, m % 2)


def swa(chip, name, ins):
    nc = chip.nc
    n_tiles = KVP * GROUP
    scale = float(CHUNK) ** -0.5
    SAMPLE = NCH - 1
    n_full = SEQ // P
    OUT_FROM = 8
    SCORE_BANK, TURN_BANK, OUT_BANK = 3, 5, 7

    def window(c):
        if c == SAMPLE:
            return CACHE0, WIN, ((0, P, n_full), (P, CHUNK, n_full + 1))
        if c == 0:
            return 0, CHUNK, ((0, CHUNK, 0),)
        if c == 1:
            return 0, 2 * CHUNK, ((P, P, 0),)
        first = (c - 2) // 2
        return CHUNK * (c - 2), WIN, ((0, P, first), (P, P if c % 2 else CHUNK, first + 1))

    def prob_cols(c):
        n = window(c)[1]
        first = 0 if c % 2 == 0 else (CHUNK if n == WIN else P)
        return slice(first, first + n + 1)

    with ExitStack() as ctx:
        sb = lambda n, shape, dt=F32: ctx.enter_context(nc.sbuf_tensor(f"{name}_{n}", shape, dt))
        sem = lambda n: chip.sem(f"{name}_{n}")
        kT = sb("kT", [P, KVP, KCOLS])
        v_fm = sb("v_fm", [P, KVP, TP])
        v_tok = sb("v_tok", [P, KVP, n_full + 2, P])
        q_flat = sb("q_flat", [P, TP])
        q2 = sb("q2", [P, NCH, 2, CHUNK])
        prob = sb("prob", [P, 2, 2 * P + 2])
        probT = sb("probT", [P, 2, 2, P])
        o = sb("o", [P, TP])
        o_hi = sb("o_hi", [P, 1, TP], F32R)
        o_lo = sb("o_lo", [P, 1, TP], F32R)
        biases = sb("biases", [P, n_tiles + 2 * KVP])
        q_bias = sb("q_bias", [P, 1])
        sink_col = sb("sink_col", [P, 1])
        out_bias = sb("out_bias", [P, KT])
        sinks = sb("sinks", [P, n_tiles])
        neg_max, p_sum, p_inv = (sb(n, [P, NCH]) for n in ("neg_max", "p_sum", "p_inv"))
        ws = WeightStream(chip, name)

        cache_in, cache_out, const_in, y_zero, y_bias = (
            sem("cache_in"), sem("cache_out"), sem("const_in"), sem("y_zero"), sem("y_bias"))
        pads_zero, bias_ready, sink_ready = sem("pads_zero"), sem("bias_ready"), sem("sink_ready")
        kv_full, kv_read, v_turned, v_copied = sem("kv_full"), sem("kv_read"), sem("v_turned"), sem("v_copied")
        q_full, q_read, q_ready = sem("q_full"), sem("q_read"), sem("q_ready")
        scores_full, maxed = sem("scores_full"), sem("maxed")
        exp_done, inverted, normed = sem("exp_done"), sem("inverted"), sem("normed")
        probT_full, probT_ready = sem("probT_full"), sem("probT_ready")
        o_full, o_read, o_hi_done, o_ready = sem("o_full"), sem("o_read"), sem("o_hi_done"), sem("o_ready")
        out_full, y_added = sem("out_full"), sem("y_added")

        with nc.Block() as block:

            @block.sync
            def _(sp):
                sp.dma_start(biases[:], ins["swa_bias"]).then_inc(const_in, 16)
                sp.dma_start(out_bias[:], ins["swa_out_bias"]).then_inc(const_in, 16)
                sp.dma_start(sinks[:], ins["sinks"]).then_inc(const_in, 16)
                sp.dma_start(kT[:, :, CACHE0:NEW0], ins["cache_k"]).then_inc(cache_in, 16)
                sp.dma_start(v_tok[:, :, n_full], ins["cache_v"]).then_inc(cache_in, 16)
                load_units(sp, ws, ins["swa_units"], 2 * KVP + 2 * n_tiles)
                sp.wait_ge(kv_read, 4 * KVP)
                sp.wait_ge(v_copied, KVP * NPAIR)
                sp.wait_ge(cache_in, 32)
                sp.dma_start(ins["k_prompt"], kT[:, :, SEQ - P:SEQ]).then_inc(cache_out, 16)
                sp.dma_start(ins["k_sample"], kT[:, :, KCOLS - P:KCOLS]).then_inc(cache_out, 16)
                sp.dma_start(ins["v_prompt"], v_tok[:, :, n_full - 1]).then_inc(cache_out, 16)
                sp.dma_start(ins["v_sample"][0:CHUNK], v_tok[CHUNK:P, :, n_full]).then_inc(cache_out, 16)
                sp.dma_start(ins["v_sample"][CHUNK:P], v_tok[0:CHUNK, :, n_full + 1]).then_inc(cache_out, 16)
                sp.wait_ge(cache_out, 80)

            @block.gpsimd
            def _(pool):
                nc.gpsimd.memset(chip.y[:], 0.0).then_inc(y_zero, 1)
                nc.gpsimd.memset(q2[:], 0.0).then_inc(pads_zero, 1)
                nc.gpsimd.memset(o[:], 0.0).then_inc(pads_zero, 1)
                nc.gpsimd.memset(prob[:], 0.0).then_inc(pads_zero, 1)
                split_units(pool, ws, 2 * KVP + 2 * n_tiles)

            @block.tensor
            def _(pe):
                pe.sem_inc(ws.begun, 1)
                for i in range(KVP):
                    for n in range(2):
                        pe.wait_ge(ws.ready, 2 * i + n + 1)
                        if i:
                            pe.wait_ge(kv_read, 3 if n == 0 else 4)
                        dense_tile(chip, n, lambda k: k * P, n, chip.h_hi, chip.h_lo, ws.begun).then_inc(kv_full, 1)

                def queries(t, slot, ready, k):
                    if k == 0:
                        pe.wait_ge(ws.ready, ready)
                        pe.wait_ge(y_added, KT * (t - 2) + 1) if not isinstance(t, int) or t > 1 else None
                    mm = dense_part(chip, 0, k, KT, k * P, slot, chip.h_hi, chip.h_lo, ws.begun if k == 0 else None)
                    if k == KT - 1:
                        mm.then_inc(q_full, 1)

                def out_tile(t, slot, ready, m):
                    if m == 0:
                        pe.wait_ge(o_ready, t + 1)
                        pe.wait_ge(ws.ready, ready)
                        pe.wait_ge(q_read, t + 3 if not isinstance(t, int) or t < n_tiles - 2 else n_tiles)
                    if not isinstance(t, int) or t > 0 or m > 0:
                        pe.wait_ge(y_added, KT * t + m + 1)
                    dense_part(chip, 0, 0, 1, m * P, slot, o_hi, o_lo, ws.begun if m == 0 else None).then_inc(out_full, 1)

                pe.wait_ge(kv_read, 7)
                for k in range(KT):
                    queries(0, 0, 2 * KVP + 1, k)
                pe.wait_ge(kv_read, 4 * KVP)
                for i in range(KVP):
                    for p in range(NPAIR):
                        n = min(P, T - P * p)
                        if i or p >= 2:
                            pe.wait_ge(v_copied, NPAIR * i + p - 1)
                        nc.tensor.transpose(chip.banks[0:n, 6 + (NPAIR * i + p) % 2, 0:P], v_fm[:, i, P * p:P * p + n],
                                            chip.ident[:]).then_inc(v_turned, 1)
                pe.wait_ge(v_copied, NPAIR * KVP)
                pe.wait_ge(cache_in, 32)

                def chunks(t, i, q_unit=None, out_unit=None):
                    pe.wait_ge(q_ready, 2 * t + 2)
                    pe.wait_ge(sink_ready, t + 1)

                    def scores(c):
                        first, n, _ = window(c)
                        if c >= 2:
                            pe.wait_ge(exp_done, NCH * t + c - 1)
                        nc.tensor.matmul(chip.banks[:, SCORE_BANK + c % 2, 0:n], q2[:, c],
                                         kT[:, i, first:first + n], start=True, stop=True)
                        nc.tensor.matmul(chip.banks[:, SCORE_BANK + c % 2, n:n + 1], chip.ident[:], sink_col[:],
                                         start=True, stop=True).then_inc(scores_full, 1)

                    def turn(c):
                        pe.wait_ge(normed, NCH * t + c + 1)
                        if c >= 2:
                            pe.wait_ge(probT_ready, NCH * t + c - 1)
                        for j, (col, n, _) in enumerate(window(c)[2]):
                            n = P if j == 0 else n
                            mm = nc.tensor.transpose(chip.banks[0:n, TURN_BANK + c % 2, j * P:(j + 1) * P],
                                                     prob[:, c % 2, col:col + n], chip.ident[:])
                        mm.then_inc(probT_full, 1)

                    def output(c):
                        pe.wait_ge(probT_ready, NCH * t + c + 1)
                        if c >= 1:
                            pe.wait_ge(o_read, 2 * (NCH * t + c))
                        parts = window(c)[2]
                        for j, (_, n, v_tile) in enumerate(parts):
                            mm = nc.tensor.matmul(chip.banks[:, OUT_BANK, 0:P], v_tok[0:n, i, v_tile],
                                                  probT[0:n, c % 2, j], start=(j == 0), stop=(j == len(parts) - 1))
                        mm.then_inc(o_full, 1)

                    for c in range(NCH + 2):
                        if c < NCH:
                            scores(c)
                        if c < KT and q_unit is not None:
                            queries(t + 1, *q_unit, c)
                        if OUT_FROM <= c < OUT_FROM + KT and out_unit is not None:
                            out_tile(t - 1, *out_unit, c - OUT_FROM)
                        if 1 <= c <= NCH:
                            turn(c - 1)
                        if c >= 2:
                            output(c - 2)

                q_of = lambda t: (0, 2 * t + 2 * KVP + 1)
                out_of = lambda t: (1, 2 * t + 2 * KVP + 2)
                chunks(0, 0, q_unit=(1, 2 * KVP + 2))
                with pe.Fori(1, GROUP) as t:
                    chunks(t, 0, q_of(t), out_of(t))
                with pe.Fori(GROUP, n_tiles - 1) as t:
                    chunks(t, 1, q_of(t), out_of(t))
                chunks(n_tiles - 1, 1, out_unit=(0, 2 * KVP + 2 * n_tiles - 1))
                for m in range(KT):
                    out_tile(n_tiles - 1, 1, 2 * KVP + 2 * n_tiles, m)

            @block.scalar
            def _(act):
                act.sem_inc(o_hi_done, 1)
                act.wait_ge(const_in, 48)
                act.wait_ge(pads_zero, 3)

                def take_queries(t):
                    act.wait_ge(q_full, t + 1)
                    act.wait_ge(bias_ready, t + 1)
                    nc.scalar.activation(blocks_of(q_flat[:]), chip.psum_set(0), ACT.Identity,
                                         bias=q_bias[:], scale=scale).then_inc(q_read, 1)

                for i in range(KVP):
                    act.wait_ge(kv_full, 2 * i + 1)
                    k_bias = biases[:, n_tiles + i:n_tiles + i + 1]
                    for blk in range(NB):
                        lo, hi = blk * BW, min((blk + 1) * BW, SEQ)
                        last = nc.scalar.activation(kT[:, i, lo:hi], chip.banks[:, blk, 0:hi - lo], ACT.Identity, bias=k_bias)
                    last.then_inc(kv_read, 1)
                    nc.scalar.activation(kT[:, i, NEW0:KCOLS], chip.banks[:, NB - 1, SEQ - (NB - 1) * BW:T - (NB - 1) * BW],
                                         ACT.Identity, bias=k_bias).then_inc(kv_read, 2)
                    act.wait_ge(kv_full, 2 * i + 2)
                    nc.scalar.activation(blocks_of(v_fm[:, i]), chip.psum_set(1), ACT.Identity,
                                         bias=biases[:, n_tiles + KVP + i:n_tiles + KVP + i + 1]).then_inc(kv_read, 1)
                take_queries(0)
                for i in range(KVP):
                    for p in range(NPAIR):
                        n = min(P, T - P * p)
                        act.wait_ge(v_turned, NPAIR * i + p + 1)
                        nc.scalar.copy(v_tok[0:n, i, p if p < n_full else n_full + 1],
                                       chip.banks[0:n, 6 + (NPAIR * i + p) % 2, 0:P]).then_inc(v_copied, 1)

                def chunks(t, next_queries):

                    def exps(c):
                        act.wait_ge(maxed, NCH * t + c + 1)
                        if c >= 2:
                            act.wait_ge(probT_full, NCH * t + c - 1)
                        cols = prob_cols(c)
                        nc.scalar.activation(prob[:, c % 2, cols], chip.banks[:, SCORE_BANK + c % 2, 0:cols.stop - cols.start],
                                             ACT.Exp, bias=neg_max[:, c:c + 1],
                                             accum_out=p_sum[:, c:c + 1]).then_inc(exp_done, 1)

                    def take_output(c):
                        act.wait_ge(o_full, NCH * t + c + 1)
                        if c == 0 and (not isinstance(t, int) or t > 0):
                            act.wait_ge(o_ready, t)
                        for a in range(2):
                            rows = slice(a * CHUNK, (a + 1) * CHUNK)
                            nc.scalar.copy(o[rows, CHUNK * c:CHUNK * (c + 1)],
                                           chip.banks[rows, OUT_BANK, rows]).then_inc(o_read, 1)

                    for c in range(NCH + 2):
                        if c == KT and next_queries:
                            take_queries(t + 1)
                        if c < NCH:
                            exps(c)
                        if c >= 2:
                            take_output(c - 2)
                    act.wait_ge(o_read, 2 * NCH * (t + 1))
                    if not isinstance(t, int) or t > 0:
                        act.wait_ge(out_full, KT * t)
                    nc.scalar.copy(o_hi[:, 0], o[:]).then_inc(o_hi_done, 1)

                chunks(0, True)
                with act.Fori(1, n_tiles - 1) as t:
                    chunks(t, True)
                chunks(n_tiles - 1, False)

            @block.vector
            def _(dve):
                dve.sem_inc(y_added, 1)
                dve.wait_ge(const_in, 48)
                dve.wait_ge(y_zero, 1)
                dve.wait_ge(pads_zero, 3)

                def tile_bias(t):
                    at = bass.ds(t, 1) if not isinstance(t, int) else slice(t, t + 1)
                    nc.vector.tensor_scalar(q_bias[:], biases[:, at], scale, None, ALU.mult).then_inc(bias_ready, 1)

                def place_queries(t):
                    dve.wait_ge(q_read, t + 1)
                    if not isinstance(t, int) or t > 0:
                        dve.wait_ge(scores_full, NCH * t)
                    for a in range(2):
                        rows = slice(a * CHUNK, (a + 1) * CHUNK)
                        nc.vector.tensor_copy(q2[rows, :, a], q_flat[rows, 0:T].rearrange("p (c n) -> p c n", n=CHUNK)
                                              ).then_inc(q_ready, 1)
                    at = bass.ds(t, 1) if not isinstance(t, int) else slice(t, t + 1)
                    nc.vector.tensor_scalar(sink_col[:], sinks[:, at], 1.0, None, ALU.mult).then_inc(sink_ready, 1)

                tile_bias(0)
                for k in range(KT):
                    nc.vector.tensor_scalar(chip.y[:, k], chip.y[:, k], out_bias[:, k:k + 1], None, ALU.add).then_inc(y_bias, 1)
                dve.wait_ge(y_bias, KT)
                place_queries(0)

                def add_output(t, m):
                    dve.wait_ge(out_full, KT * t + m + 1)
                    nc.vector.tensor_tensor(blocks_of(chip.y[:, m]), chip.psum_set(0), blocks_of(chip.y[:, m]),
                                            ALU.add).then_inc(y_added, 1)

                def chunks(t, has_next, has_last):

                    def row_max(c):
                        n = window(c)[1] + 1
                        dve.wait_ge(scores_full, NCH * t + c + 1)
                        nc.vector.tensor_reduce(neg_max[:, c:c + 1], chip.banks[:, SCORE_BANK + c % 2, 0:n], AX_X, ALU.max,
                                                negate=True).then_inc(maxed, 1)

                    def normalize(c):
                        cols = prob_cols(c)
                        keys = slice(cols.start, cols.stop - 1)
                        dve.wait_ge(exp_done, NCH * t + c + 1)
                        nc.vector.reciprocal(p_inv[:, c:c + 1], p_sum[:, c:c + 1]).then_inc(inverted, 1)
                        dve.wait_ge(inverted, NCH * t + c + 1)
                        nc.vector.tensor_scalar(prob[:, c % 2, keys], prob[:, c % 2, keys], p_inv[:, c:c + 1], None,
                                                ALU.mult).then_inc(normed, 1)

                    def copy_turned(c):
                        parts = window(c)[2]
                        dve.wait_ge(probT_full, NCH * t + c + 1)
                        if c >= 2:
                            dve.wait_ge(o_full, NCH * t + c - 1)
                        src = chip.banks[:, TURN_BANK + c % 2, 0:2 * P].rearrange("p (j n) -> p j n", j=2)
                        if len(parts) == 1 or parts[0][1] == parts[1][1]:
                            n = parts[0][1]
                            nc.vector.tensor_copy(probT[0:n, c % 2, 0:len(parts)], src[0:n, 0:len(parts)]).then_inc(probT_ready, 1)
                        else:
                            nc.vector.tensor_copy(probT[:, c % 2, 0], src[:, 0])
                            nc.vector.tensor_copy(probT[0:CHUNK, c % 2, 1], src[0:CHUNK, 1]).then_inc(probT_ready, 1)

                    for c in range(NCH + 2):
                        if OUT_FROM < c <= OUT_FROM + KT and has_last:
                            add_output(t - 1, c - OUT_FROM - 1)
                        if c < NCH:
                            row_max(c)
                        if 1 <= c <= NCH:
                            normalize(c - 1)
                        if c >= 2:
                            copy_turned(c - 2)
                        if c == 0 and has_last:
                            dve.wait_ge(o_hi_done, t + 1)
                            nc.vector.tensor_tensor(o_lo[:, 0], o[:], o_hi[:, 0].bitcast(F32), ALU.subtract).then_inc(o_ready, 1)
                        if c == 1 and has_next:
                            dve.wait_ge(q_read, t + 1)
                            tile_bias(t + 1)
                        if c == NCH and has_next:
                            place_queries(t + 1)

                chunks(0, True, False)
                with dve.Fori(1, n_tiles - 1) as t:
                    chunks(t, True, True)
                chunks(n_tiles - 1, False, True)
                dve.wait_ge(o_hi_done, n_tiles + 1)
                nc.vector.tensor_tensor(o_lo[:, 0], o[:], o_hi[:, 0].bitcast(F32), ALU.subtract).then_inc(o_ready, 1)
                for m in range(KT):
                    add_output(n_tiles - 1, m)


def build(nc, ins, outs):
    with ExitStack() as ctx:
        chip = Chip(nc, ctx)
        const_in = chip.sem("const_in")
        with nc.Block() as block:

            @block.sync
            def _(sp):
                sp.dma_start(chip.ones[:], ins["ones"]).then_inc(const_in, 16)
                sp.dma_start(chip.ident[:], ins["ident"]).then_inc(const_in, 16)
                sp.dma_start(chip.gains[:], ins["gains"]).then_inc(const_in, 16)
                sp.wait_ge(const_in, 48)

        everything = dict(ins)
        everything.update(outs)
        boundary(chip, "in", None, 0, x_parts=(ins["x_prompt"], ins["x_sample"]))
        gla(chip, "gla", everything)
        boundary(chip, "mid0", 1, 2)
        mlp(chip, "mlp0", ins["mlp_units"][0])
        boundary(chip, "next", 3, 4)
        swa(chip, "swa", everything)
        boundary(chip, "mid1", 5, 6)
        mlp(chip, "mlp1", ins["mlp_units"][1])
        boundary(chip, "out", 7, None, out_parts=(outs["y_prompt"], outs["y_sample"]))


OUT_SHAPES = {
    "y_prompt": (P, KT, SEQ), "y_sample": (P, KT, DEC),
    "state_prompt": (GH, P, DV), "state_sample": (GH, P, DV),
    "k_prompt": (P, KVP, P), "v_prompt": (P, KVP, P), "k_sample": (P, KVP, P), "v_sample": (P, KVP, P),
}


def features_first(a):
    return np.ascontiguousarray(a.T.reshape(KT, P, -1).transpose(1, 0, 2))


def k_units(w):
    return w.reshape(-1, P, w.shape[1]).transpose(1, 0, 2).reshape(P, -1)


def laid_out(inputs):
    a = {name: np.asarray(value) for name, value in inputs.items()}
    dqk = GH * P
    w_in, w_out = a["gla_w_in"][0], a["gla_w_out"][0]
    gla_units = []
    for h in range(GH):
        q, k = w_in[:, h * P:(h + 1) * P], w_in[:, dqk + h * P:dqk + (h + 1) * P]
        v, r = (w_in[:, s + h * DV:s + (h + 1) * DV] for s in (2 * dqk, 2 * dqk + GH * DV))
        o = w_out[h * DV:(h + 1) * DV]
        gla_units += [k_units(x) for x in (k, q, v[:, :P], v[:, P:], r[:, :P], r[:, P:])]
        gla_units += [k_units(x) for x in (before[:, :512], before[:, 512:])] if h else []
        before = o
    gla_units += [k_units(x) for x in (o[:, :512], o[:, 512:])]

    s_in, s_out, s_b = a["swa_w_in"][0], a["swa_w_out"][0], a["swa_b_in"][0]
    n_q = s_out.shape[0]
    heads = [(8 * i + g, 8 * i + GROUP + g) for i in range(KVP) for g in range(GROUP)]
    rows = [np.concatenate([np.arange(64 * h, 64 * h + 64) for h in pair]) for pair in heads]
    kv = [n_q + np.arange(P * i, P * (i + 1)) for i in range(2 * KVP)]
    q_unit = lambda t: k_units(s_in[:, rows[t]])
    out_unit = lambda t: s_out[rows[t]]
    swa_units = [k_units(s_in[:, kv[n]]) for n in (0, KVP, 1, KVP + 1)] + [q_unit(0), q_unit(1)]
    n_tiles = len(heads)
    for t in range(1, n_tiles - 1):
        swa_units += [q_unit(t + 1), out_unit(t - 1)]
    swa_units += [out_unit(n_tiles - 2), out_unit(n_tiles - 1)]
    mlp_units = []
    for up, down in zip(a["mlp_w_up"], a["mlp_w_down"]):
        for g in range(FF_GROUPS):
            f = slice(g * FF_TILES * P, (g + 1) * FF_TILES * P)
            mlp_units += [k_units(x) for x in np.split(up[:, f], FF_TILES, 1)]
            mlp_units += [k_units(x) for x in np.split(down[f], KT // 2, 1)]

    m, l = np.arange(P)[:, None], np.arange(P)[None, :]
    masks = [(m // (2 * s) == l // (2 * s)) & (m % (2 * s) < s) & (l % (2 * s) >= s) for s in HALVES] + [m == l]
    pack = lambda x: np.ascontiguousarray(x)
    return {
        "ones": np.ones((P, P), np.float32), "ident": np.eye(P, dtype=np.float32),
        "masks": pack(np.stack(masks, 1).astype(np.float32)),
        "gains": pack(a["norm_g"].reshape(8, KT, P).transpose(2, 0, 1)),
        "x_prompt": features_first(a["x_prompt"][0]), "x_sample": features_first(a["x_sample"][0]),
        "gla_units": np.stack(gla_units), "gate_a": pack(a["gla_w_gate_a"][0].reshape(KT, P, RANK).transpose(1, 0, 2)),
        "gate_b": pack(a["gla_w_gate_b"][0].reshape(RANK, GH, P).transpose(1, 0, 2)),
        "gate_bias": pack(a["gla_b_gate"][0].reshape(GH, P, 1)),
        "gla_gain": pack(a["gla_g_onorm"][0].reshape(GH, 2, P).transpose(0, 2, 1)), "state_gla": a["state_gla"][0, 0],
        "swa_units": np.stack(swa_units), "swa_bias": pack(s_b[np.stack(rows + kv)].T),
        "swa_out_bias": pack(a["swa_b_out"][0].reshape(KT, P).T),
        "sinks": pack(np.repeat(a["swa_sinks"][0][np.array(heads)], 64, 1).T),
        "cache_k": pack(a["cache_swa_k"][0, 0].reshape(P, KVP, P).transpose(2, 1, 0)),
        "cache_v": pack(a["cache_swa_v"][0, 0].reshape(P, KVP, P)),
        "mlp_units": np.stack(mlp_units).reshape(2, 8 * FF_GROUPS, P, UNIT),
    }


def kernel(**inputs):
    import concourse.bacc as bacc
    from concourse.bass_utils import run_bass_kernel_spmd

    nc = bacc.Bacc("TRN2", target_bir_lowering=False, num_devices=1)
    arrays = {f"in_{name}": array for name, array in laid_out(inputs).items()}
    ins = {name[3:]: nc.dram_tensor(name, array.shape, mybir.dt.from_np(array.dtype), kind="ExternalInput").ap()
           for name, array in arrays.items()}
    outs = {name: nc.dram_tensor(f"out_{name}", shape, F32, kind="ExternalOutput").ap()
            for name, shape in OUT_SHAPES.items()}
    build(nc, ins, outs)
    result = run_bass_kernel_spmd(nc, [arrays], core_ids=[0]).results[0]
    got = {name: np.asarray(result[f"out_{name}"]) for name in OUT_SHAPES}

    tokens_first = lambda x: np.ascontiguousarray(x.transpose(1, 0, 2).reshape(D, -1).T)[None]
    keys_first = lambda x: np.ascontiguousarray(x.transpose(2, 1, 0)).reshape(1, 1, P, 2 * KVP, 64)
    return (tokens_first(got["y_prompt"]), tokens_first(got["y_sample"]),
            got["state_prompt"][None, None], got["state_sample"][None, None],
            keys_first(got["k_prompt"]), got["v_prompt"].reshape(1, 1, P, 2 * KVP, 64),
            keys_first(got["k_sample"]), got["v_sample"].reshape(1, 1, P, 2 * KVP, 64))
```

```python
from contextlib import ExitStack

import numpy as np

import concourse.bass as bass
from concourse import mybir

F32 = mybir.dt.float32
F32R = mybir.dt.float32r
ALU = mybir.AluOpType
ACT = mybir.ActivationFunctionType
AX_X = mybir.AxisListType.X

P = 128
D = 1024
KT = D // P
SEQ, DEC = 1024, 64
CHUNK = 64
T = SEQ + DEC
NB = 3
BW = 364
TP = NB * BW
UNIT = KT * P
NCH = T // CHUNK
NPAIR = (NCH + 1) // 2
EPS = 1e-6

GH, DV = 4, 256
GATE_NORM = 16.0
HALVES = (32, 16, 8, 4, 2, 1)
NLEV = len(HALVES)
CW = NLEV
KW = NLEV + 1
RANK = 16

KVP = 2
GROUP = 4
WIN = 3 * CHUNK
CACHE0 = SEQ
NEW0 = SEQ + 128
KCOLS = SEQ + 128 + DEC

FF_GROUPS = 8
FF_TILES = 4


def blocks_of(ap):
    return ap.rearrange("p (b n) -> p b n", b=NB)


class Chip:

    def __init__(self, nc, ctx, units):
        self.nc, self.ctx = nc, ctx
        self.shared = {}
        sb = self.sbuf
        self.h_hi = sb("h_hi", [P, KT, TP], F32R)
        self.h_lo = sb("h_lo", [P, KT, TP], F32R)
        self.y = sb("y", [P, KT, TP])
        self.w_raw = sb("w_raw", [P, 2, UNIT])
        self.w_hi = sb("w_hi", [P, 2, UNIT], F32R)
        self.w_lo = sb("w_lo", [P, 2, UNIT], F32R)
        self.ident = sb("identity", [P, P])
        self.ones = sb("all_ones", [P, P])
        self.gains = sb("gains", [P, 8, KT])
        self.banks = ctx.enter_context(nc.psum_tensor("banks", [P, 8, 512], F32))
        self.stream = WeightStream(self, units)
        self.x_dram = nc.dram_tensor("x_scratch", [P, KT, TP], F32, kind="Internal").ap()

    def sbuf(self, name, shape, dtype=F32):
        return self.ctx.enter_context(self.nc.sbuf_tensor(name, shape, dtype))

    def sem(self, name):
        return self.ctx.enter_context(self.nc.semaphore(name))

    def counted(self, name):
        if name not in self.shared:
            self.shared[name] = Counted(self.sem(name))
        return self.shared[name]

    def psum_set(self, s):
        return self.banks[:, 3 * s:3 * s + 3, 0:BW]


class Counted:

    def __init__(self, sem):
        self.sem, self.base = sem, 0

    def at(self, n):
        return self.base + n


class WeightStream:

    def __init__(self, chip, units):
        self.chip, self.units, self.base = chip, units, 0
        self.raw_in = [chip.sem(f"w_raw_in{s}") for s in range(2)]
        self.hi_done, self.ready, self.begun = chip.sem("w_hi_done"), chip.sem("w_ready"), chip.sem("w_begun")

    def load_first(self, sp):
        for s in range(2):
            sp.dma_start(self.chip.w_raw[:, s], self.units[s]).then_inc(self.raw_in[s], 16)

    def load_one(self, sp, i, s):
        unit = 2 * i + (self.base + s)
        sp.wait_ge(self.ready, unit - 1)
        sp.dma_start(self.chip.w_raw[:, s], self.units[unit]).then_inc(self.raw_in[s], 16)

    def load(self, sp, n_units, is_last=False, first=2):
        with sp.Fori(first, n_units // 2 + (0 if is_last else 1)) as i:
            for s in range(2):
                self.load_one(sp, i, s)

    def split(self, pool, i, s):
        c, nc = self.chip, self.chip.nc
        pool.wait_ge(self.raw_in[s], 16 * i + (8 * self.base + 16))
        raw = c.w_raw[:, s].rearrange("p (k m) -> p k m", k=KT)
        ones = c.ones[:, None, :].to_broadcast([P, KT, P])
        hi = nc.gpsimd.tensor_tensor(c.w_hi[:, s].rearrange("p (k m) -> p k m", k=KT), raw, ones, ALU.mult)
        hi.then_inc(self.hi_done, 1)
        pool.wait_ge(self.hi_done, 2 * i + (self.base + s + 1))
        lo = nc.gpsimd.tensor_tensor(c.w_lo[:, s], c.w_raw[:, s], c.w_hi[:, s].bitcast(F32), ALU.subtract)
        lo.then_inc(self.ready, 1)

    def split_when_free(self, pool, i, s):
        pool.wait_ge(self.begun, 2 * i + (self.base + s))
        self.split(pool, i, s)

    def split_from(self, pool, first, n_units):
        with pool.Fori(first, n_units // 2) as i:
            for s in range(2):
                self.split_when_free(pool, i, s)

    def wait_ready(self, pe, n):
        pe.wait_ge(self.ready, n + self.base)


def dense_part(chip, s, k, n_k, at, slot, hi, lo, begun=None, before_bank=None):
    w_hi, w_lo = chip.w_hi[:, slot, at:at + P], chip.w_lo[:, slot, at:at + P]
    passes = ((w_hi, hi), (w_hi, lo), (w_lo, hi))
    order = [(n, b) for n in range(3) for b in range(NB)]
    if before_bank:
        order = [(n, b) for b in range(NB) for n in range(3)]
    for n, b in order:
        w, x = passes[n]
        if n == 0 and before_bank:
            before_bank(b)
        mm = chip.nc.tensor.matmul(chip.banks[:, 3 * s + b, 0:BW], w, x[:, k, b * BW:(b + 1) * BW],
                                   start=(k == 0 and n == 0), stop=(k == n_k - 1 and n == 2))
        if begun is not None:
            mm.then_inc(begun, 1)
            begun = None
    return mm


def dense_tile(chip, s, weight_cols, slot, hi, lo, begun=None, before_k=None):
    n_k = hi.shape[1]
    for k in range(n_k):
        if before_k:
            before_k(k)
        mm = dense_part(chip, s, k, n_k, weight_cols(k), slot, hi, lo, begun if k == 0 else None)
    return mm


class Norm:

    SLOTS = 4
    SUM_BANK, RS_BANK, KEEP_BANKS = 6, 3, (7, 6, 7)
    SUM_AT = {2: 0, 3: 1}
    SPREAD_AT = {6: (0,), 7: (1, 2)}
    TOK = [P * j for j in range(SEQ // P)] + [TP - P]
    N_TOK = len(TOK)

    def __init__(self, chip, name, post, pre, x_parts=None, out_parts=None):
        self.chip, self.post, self.pre = chip, post, pre
        self.x_parts, self.out_parts = x_parts, out_parts
        self.first, self.last = post is None, pre is None
        self.middle = not self.first and not self.last
        self.kept = ExitStack()
        kept = lambda n, shape, dt=F32: self.kept.enter_context(chip.nc.sbuf_tensor(f"{name}_{n}", shape, dt))
        if self.middle:
            self.keep = kept("keep", [P, TP])
        with ExitStack() as ctx:
            sb = lambda n, shape, dt=F32: ctx.enter_context(chip.nc.sbuf_tensor(f"{name}_{n}", shape, dt))
            small = kept if self.middle else sb
            self.diag = small("diag", [P, self.N_TOK, P])
            self.var = small("var", [P, self.N_TOK])
            self.rs = small("rs", [P, self.N_TOK])
            self.x = sb("x", [P, KT, TP])
            self.work = sb("work", [P, KT, TP])
        if self.first:
            self.adds, self.totals = [(k, k - 1) for k in range(1, KT)], [(KT - 1, KT - 1)]
        else:
            self.adds, self.totals = [(1, 0), (3, 2), (3, 1), (5, 4), (7, 6), (7, 5)], [(3, 3), (7, 6)]
        sem = lambda n: chip.counted(f"norm_{n}")
        self.x_in = [sem(f"x_in{k}") for k in range(KT)]
        self.x_out, self.pad_zero = sem("x_out"), sem("pad_zero")
        self.x_new = [sem("x_new_even"), sem("x_new_odd")]
        self.sq_done, self.kept_done = sem("sq_done"), sem("kept_done")
        self.sq_added, self.sq_used, self.var_done, self.std_done, self.inverted = (
            sem("sq_added"), sem("sq_used"), sem("var_done"), sem("std_done"), sem("inverted"))
        self.diag_done, self.rs_full = sem("diag_done"), sem("rs_full")
        self.scaled, self.hi_done = sem("scaled"), sem("hi_done")
        self.lo_done = [sem("lo_done_even"), sem("lo_done_odd")]
        self.n_norms = 2 if self.middle else 1

    def x_ready(self, engine, k):
        if self.first:
            engine.wait_ge(self.x_in[k].sem, self.x_in[k].at(32))
            engine.wait_ge(self.pad_zero.sem, self.pad_zero.at(1))
        else:
            engine.wait_ge(self.x_new[k % 2].sem, self.x_new[k % 2].at(k // 2 + 1))

    def x_landed(self, engine, k):
        engine.wait_ge(self.x_in[k].sem, self.x_in[k].at(32 if self.x_parts else 16))

    def h_ready(self, engine, k):
        engine.wait_ge(self.lo_done[k % 2].sem, self.lo_done[k % 2].at(k // 2 + 1))

    def free(self, engine):
        for parity in range(2):
            engine.wait_ge(self.lo_done[parity].sem, self.lo_done[parity].at(KT // 2))
        self.sums_read(engine)
        if self.middle:
            engine.wait_ge(self.x_out.sem, self.x_out.at(16 * KT))

    def sums_read(self, engine):
        engine.wait_ge(self.sq_used.sem, self.sq_used.at(len(self.totals)))

    def load_x(self, sp):
        for k in range(KT):
            if self.x_parts is None:
                sp.dma_start(self.x[:, k], self.chip.x_dram[:, k]).then_inc(self.x_in[k].sem, 16)
            else:
                sp.dma_start(self.x[:, k, 0:SEQ], self.x_parts[0][:, k]).then_inc(self.x_in[k].sem, 16)
                sp.dma_start(self.x[:, k, SEQ:T], self.x_parts[1][:, k]).then_inc(self.x_in[k].sem, 16)

    def store_x(self, sp):
        if self.middle:
            for k in range(KT):
                self.x_ready(sp, k)
                sp.dma_start(self.chip.x_dram[:, k], self.x[:, k]).then_inc(self.x_out.sem, 16)
        if self.out_parts is not None:
            for k in range(KT):
                self.x_ready(sp, k)
                sp.dma_start(self.out_parts[0][:, k], self.x[:, k, 0:SEQ]).then_inc(self.x_out.sem, 16)
                sp.dma_start(self.out_parts[1][:, k], self.x[:, k, SEQ:T]).then_inc(self.x_out.sem, 16)
            sp.wait_ge(self.x_out.sem, self.x_out.at(32 * KT))

    def scalar(self, act):
        nc = self.chip.nc
        if self.first:
            for k in range(KT):
                self.x_ready(act, k)
                nc.scalar.activation(self.work[:, k], self.x[:, k], ACT.Square).then_inc(self.sq_done.sem, 1)
        act.wait_ge(self.var_done.sem, self.var_done.at(1))
        nc.scalar.activation(self.rs[:], self.var[:], ACT.Sqrt).then_inc(self.std_done.sem, 1)
        if self.first:
            for k in range(KT):
                act.wait_ge(self.scaled.sem, self.scaled.at(k + 1))
                nc.scalar.copy(self.chip.h_hi[:, k], self.work[:, k % self.SLOTS]).then_inc(self.hi_done.sem, 1)
        if self.middle:
            for k in range(KT):
                self.x_ready(act, k)
                nc.scalar.activation(self.chip.h_hi[:, k], self.x[:, k], ACT.Copy,
                                     scale=self.chip.gains[:, self.pre, k:k + 1]).then_inc(self.hi_done.sem, 1)
                nc.scalar.activation(self.work[:, k], self.x[:, k], ACT.Square).then_inc(self.sq_done.sem, 1)
            act.wait_ge(self.var_done.sem, self.var_done.at(2))
            nc.scalar.activation(self.rs[:], self.var[:], ACT.Sqrt).then_inc(self.std_done.sem, 1)
            for piece, (t0, t1) in enumerate(((0, 512), (512, SEQ), (SEQ, TP))):
                act.wait_ge(self.rs_full.sem, self.rs_full.at(NB + piece + 1))
                nc.scalar.copy(self.keep[:, t0:t1], self.chip.banks[:, self.KEEP_BANKS[piece], 0:t1 - t0]
                               ).then_inc(self.kept_done.sem, 1)

    def kept_ready(self, engine):
        engine.wait_ge(self.kept_done.sem, self.kept_done.at(NB))

    def add_squares(self, dve):
        for n, (to, tile) in enumerate(self.adds):
            dve.wait_ge(self.sq_done.sem, self.sq_done.at(to + 1))
            if self.first or n % 3 == 2:
                if n:
                    dve.wait_ge(self.sq_added.sem, self.sq_added.at(n))
            self.chip.nc.vector.tensor_tensor(self.work[:, to], self.work[:, to], self.work[:, tile],
                                              ALU.add).then_inc(self.sq_added.sem, 1)

    def sum_squares(self, pe, n):
        tile, n_adds = self.totals[n]
        pe.wait_ge(self.sq_added.sem, self.sq_added.at(n_adds))
        for j, t in enumerate(self.TOK):
            mm = self.chip.nc.tensor.matmul(self.chip.banks[:, self.SUM_BANK, j:j + 1], self.work[:, tile, t:t + P],
                                            self.chip.ones[:, 0:1], start=(n == 0 and j == 0),
                                            stop=(n == len(self.totals) - 1 and j == self.N_TOK - 1))
        mm.then_inc(self.sq_used.sem, 1)

    def spread(self, pe, n, piece, bank):
        pe.wait_ge(self.diag_done.sem, self.diag_done.at(NB * n + piece + 1))
        if piece < 2:
            width, rhs = 4 * P, self.diag[:, 4 * piece:4 * piece + 4]
        else:
            width, rhs = TP - SEQ, self.diag[:, 8, P - (TP - SEQ):P]
        self.chip.nc.tensor.matmul(self.chip.banks[:, bank, 0:width], self.chip.ones[:], rhs,
                                   start=True, stop=True).then_inc(self.rs_full.sem, 1)

    def tensor(self, pe):
        if self.first:
            self.sum_squares(pe, 0)
        for piece in range(NB):
            self.spread(pe, 0, piece, self.RS_BANK + piece)

    def before_second_tile(self, pe, k):
        if k in self.SUM_AT:
            self.sum_squares(pe, self.SUM_AT[k])
        for piece in self.SPREAD_AT.get(k, ()):
            if piece == 2:
                pe.wait_ge(self.kept_done.sem, self.kept_done.at(1))
            self.spread(pe, 1, piece, self.KEEP_BANKS[piece])

    def inverse_rms(self, dve, n):
        nc, c = self.chip.nc, self.chip
        if self.first or n:
            self.sums_read(dve)
        nc.vector.tensor_scalar(self.var[:], c.banks[:, self.SUM_BANK, 0:self.N_TOK], 1.0 / D, EPS,
                                ALU.mult, ALU.add).then_inc(self.var_done.sem, 1)
        dve.wait_ge(self.std_done.sem, self.std_done.at(n + 1))
        nc.vector.reciprocal(self.rs[:], self.rs[:]).then_inc(self.inverted.sem, 1)
        dve.wait_ge(self.inverted.sem, self.inverted.at(n + 1))
        for j0, j1 in ((0, 4), (4, 8), (8, 9)):
            shape = [P, j1 - j0, P]
            nc.vector.tensor_tensor(self.diag[:, j0:j1], c.ident[:, None, :].to_broadcast(shape),
                                    self.rs[:, j0:j1, None].to_broadcast(shape), ALU.mult).then_inc(self.diag_done.sem, 1)

    def scale(self, out, source, gain, k):
        rs = self.chip.banks[:, self.RS_BANK:self.RS_BANK + NB].rearrange("p b n -> p (b n)")[:, 0:TP]
        self.chip.nc.vector.scalar_tensor_tensor(
            out=out, in0=source[:, k], scalar=self.chip.gains[:, gain, k:k + 1],
            in1=rs, op0=ALU.mult, op1=ALU.mult).then_inc(self.scaled.sem, 1)

    def add_to_x(self, engine, ns, k):
        self.x_landed(engine, k)
        engine.wait_ge(self.scaled.sem, self.scaled.at(k + 1))
        ns.tensor_tensor(self.x[:, k], self.x[:, k], self.work[:, k], ALU.add).then_inc(self.x_new[k % 2].sem, 1)

    def low_part(self, engine, ns, k):
        engine.wait_ge(self.hi_done.sem, self.hi_done.at(k + 1))
        ns.tensor_tensor(self.chip.h_lo[:, k], self.work[:, k % self.SLOTS], self.chip.h_hi[:, k].bitcast(F32),
                         ALU.subtract).then_inc(self.lo_done[k % 2].sem, 1)

    def vector(self, dve):
        nc = self.chip.nc
        if self.x_parts is not None:
            nc.vector.memset(self.x[:, :, T:TP], 0.0).then_inc(self.pad_zero.sem, 1)
        if self.first:
            self.add_squares(dve)
        self.inverse_rms(dve, 0)
        dve.wait_ge(self.rs_full.sem, self.rs_full.at(NB))
        if self.first:
            for k in range(0, KT, 2):
                for j in (k, k + 1):
                    if j >= self.SLOTS:
                        self.h_ready(dve, j - self.SLOTS)
                    self.scale(self.work[:, j % self.SLOTS], self.x, self.pre, j)
                self.low_part(dve, nc.vector, k)
        if self.middle:
            for k in range(KT + 2):
                if k < KT:
                    self.scale(self.work[:, k], self.chip.y, self.post, k)
                if k == 0:
                    if self.x_parts is not None:
                        dve.wait_ge(self.pad_zero.sem, self.pad_zero.at(1))
                    self.add_to_x(dve, nc.vector, 0)
                if k >= 2:
                    j = k - 2
                    dve.wait_ge(self.hi_done.sem, self.hi_done.at(j + 1))
                    nc.vector.scalar_tensor_tensor(out=self.chip.h_lo[:, j], in0=self.x[:, j],
                                                   scalar=self.chip.gains[:, self.pre, j:j + 1],
                                                   in1=self.chip.h_hi[:, j].bitcast(F32), op0=ALU.mult,
                                                   op1=ALU.subtract).then_inc(self.lo_done[j % 2].sem, 1)
            self.add_squares(dve)
            self.inverse_rms(dve, 1)
        if self.last:
            for k in range(0, KT, 2):
                for j in (k, k + 1):
                    self.scale(self.work[:, j], self.chip.y, self.post, j)
                self.add_to_x(dve, nc.vector, k)

    def gpsimd(self, pool):
        nc = self.chip.nc
        if self.first:
            for k in range(1, KT, 2):
                self.low_part(pool, nc.gpsimd, k)
        else:
            if self.x_parts is not None:
                pool.wait_ge(self.pad_zero.sem, self.pad_zero.at(1))
            for k in range(1, KT, 1 if self.middle else 2):
                self.add_to_x(pool, nc.gpsimd, k)

    def y_read(self, engine):
        if not self.first:
            engine.wait_ge(self.scaled.sem, self.scaled.at(KT))

    def close(self):
        self.kept.close()
        for k in range(KT):
            self.x_in[k].base += 16 if self.x_parts is None else 32
        squares = KT * (not self.last)
        counts = [(self.x_out, 16 * KT * self.middle), (self.pad_zero, self.x_parts is not None),
                  (self.sq_used, len(self.totals) if squares else 0), (self.sq_done, squares),
                  (self.sq_added, len(self.adds) if squares else 0), (self.kept_done, NB * self.middle),
                  (self.diag_done, NB * self.n_norms), (self.rs_full, NB * self.n_norms),
                  (self.scaled, KT), (self.hi_done, KT)]
        counts += [(s, self.n_norms) for s in (self.var_done, self.std_done, self.inverted)]
        counts += [(s, KT // 2 * (not self.first)) for s in self.x_new] + [(s, KT // 2) for s in self.lo_done]
        for s, count in counts:
            s.base += int(count)


class SquareSums:

    def __init__(self, chip, squares, gpsimd_adds, vector_adds, y_final):
        self.chip, self.squares, self.y_final = chip, squares, y_final
        self.gpsimd_adds, self.vector_adds = gpsimd_adds, vector_adds
        self.sq_done, self.added = chip.counted("tail_sq_done"), chip.counted("tail_added")
        self.total_done = chip.counted("tail_total_done")

    def scalar(self, act):
        for m in range(KT):
            self.y_final(act, m)
            self.chip.nc.scalar.activation(self.squares[m], self.chip.y[:, m], ACT.Square).then_inc(self.sq_done.sem, 1)

    def gpsimd(self, pool):
        for n, (to, tile) in enumerate(self.gpsimd_adds):
            pool.wait_ge(self.sq_done.sem, self.sq_done.at(to + 1))
            if n:
                pool.wait_ge(self.added.sem, self.added.at(n))
            self.chip.nc.gpsimd.tensor_tensor(self.squares[to], self.squares[to], self.squares[tile],
                                              ALU.add).then_inc(self.added.sem, 1)

    def vector(self, dve):
        for n, (to, tile) in enumerate(self.vector_adds):
            dve.wait_ge(self.sq_done.sem, self.sq_done.at(to + 1))
            if tile == self.gpsimd_adds[-1][0]:
                dve.wait_ge(self.added.sem, self.added.at(len(self.gpsimd_adds)))
            if n:
                dve.wait_ge(self.total_done.sem, self.total_done.at(n))
            self.chip.nc.vector.tensor_tensor(self.squares[to], self.squares[to], self.squares[tile],
                                              ALU.add).then_inc(self.total_done.sem, 1)

    def tensor(self, pe):
        pe.wait_ge(self.total_done.sem, self.total_done.at(len(self.vector_adds)))
        for j, t in enumerate(Norm.TOK):
            self.chip.nc.tensor.matmul(self.chip.banks[:, Norm.SUM_BANK, j:j + 1], self.squares[KT - 1][:, t:t + P],
                                       self.chip.ones[:, 0:1], start=(j == 0), stop=(j == Norm.N_TOK - 1))

    def close(self):
        self.sq_done.base += KT
        self.added.base += len(self.gpsimd_adds)
        self.total_done.base += len(self.vector_adds)


def result(chip, name, out_parts):
    norm = Norm(chip, name, 7, None, out_parts=out_parts)
    with chip.nc.Block() as block:

        @block.sync
        def _(sp):
            norm.load_x(sp)
            norm.store_x(sp)

        @block.gpsimd
        def _(pool):
            norm.gpsimd(pool)

        @block.tensor
        def _(pe):
            norm.tensor(pe)

        @block.scalar
        def _(act):
            norm.scalar(act)

        @block.vector
        def _(dve):
            norm.vector(dve)


def mlp(chip, name, norm, is_last):
    nc = chip.nc
    with ExitStack() as ctx:
        sb = lambda n, shape, dt=F32: ctx.enter_context(nc.sbuf_tensor(f"{name}_{n}", shape, dt))
        sem = lambda n: chip.sem(f"{name}_{n}")
        relu = sb("relu", [P, 2, TP])
        act2 = sb("act2", [P, 2, TP])
        more = sb("more_squares", [P, KT - 4, TP])
        squares = [relu[:, 0], relu[:, 1], act2[:, 0], act2[:, 1]] + [more[:, i] for i in range(KT - 4)]
        a_hi = sb("a_hi", [P, FF_TILES, TP], F32R)
        a_lo = sb("a_lo", [P, FF_TILES, TP], F32R)
        ws = chip.stream
        up_full, up_read, squared, a_hi_done, a_ready = (
            sem("up_full"), sem("up_read"), sem("squared"), sem("a_hi_done"), sem("a_ready"))
        down_full, y_added, y_zero = sem("down_full"), sem("y_added"), sem("y_zero")
        tail = SquareSums(chip, squares, [(m, m - 1) for m in range(1, KT - 1)], [(KT - 1, KT - 2)],
                          lambda engine, m: engine.wait_ge(y_added, 2 + KT * (FF_GROUPS - 1) + m + 1))

        with nc.Block() as block:

            @block.sync
            def _(sp):
                norm.load_x(sp)
                ws.load_one(sp, 1, 0)
                norm.store_x(sp)
                ws.load_one(sp, 1, 1)
                ws.load(sp, 8 * FF_GROUPS, is_last)

            @block.gpsimd
            def _(pool):
                ws.split(pool, 0, 0)
                norm.gpsimd(pool)
                ws.split(pool, 0, 1)
                norm.y_read(pool)
                ws.split_when_free(pool, 1, 0)
                nc.gpsimd.memset(chip.y[:], 0.0).then_inc(y_zero, 1)
                ws.split_when_free(pool, 1, 1)
                ws.split_from(pool, 2, 8 * FF_GROUPS)
                tail.gpsimd(pool)

            @block.tensor
            def _(pe):
                norm.tensor(pe)

                def group(g, is_first):
                    for j in range(FF_TILES):
                        ws.wait_ready(pe, 8 * g + j + 1)
                        if j >= 2:
                            pe.wait_ge(up_read, 4 * g + j - 1)
                        elif not is_first:
                            pe.wait_ge(y_added, 8 * g + j + 1)
                        before_k = None
                        if is_first and j < 2:
                            before_k = lambda k, j=j: (norm.h_ready if j == 0 else norm.before_second_tile)(pe, k)
                        mm = dense_tile(chip, j % 2, lambda k: k * P, j % 2, chip.h_hi, chip.h_lo, ws.begun, before_k)
                        mm.then_inc(up_full, 1)

                    def down_part(m, k):
                        return dense_part(chip, m % 2, k, FF_TILES, k * 2 * P + (m % 2) * P, (m // 2) % 2, a_hi, a_lo,
                                          ws.begun if m % 2 == 0 and k == 0 else None)

                    ws.wait_ready(pe, 8 * g + FF_TILES + 1)
                    for m in range(2):
                        pe.wait_ge(up_read, 4 * g + m + 3)
                        for k in range(FF_TILES - 1):
                            if m == 0:
                                pe.wait_ge(a_ready, 4 * g + k + 1)
                            down_part(m, k)
                    pe.wait_ge(a_ready, 4 * g + FF_TILES)
                    for m in range(2):
                        down_part(m, FF_TILES - 1).then_inc(down_full, 1)
                    for m in range(2, KT):
                        if m % 2 == 0:
                            ws.wait_ready(pe, 8 * g + FF_TILES + m // 2 + 1)
                        pe.wait_ge(y_added, 8 * g + m + 1)
                        for k in range(FF_TILES):
                            mm = down_part(m, k)
                        mm.then_inc(down_full, 1)

                group(0, True)
                with pe.Fori(1, FF_GROUPS) as g:
                    group(g, False)
                tail.tensor(pe)

            @block.scalar
            def _(act):
                norm.scalar(act)
                norm.free(act)
                with act.Fori(0, FF_GROUPS) as g:

                    for j in range(FF_TILES):
                        act.wait_ge(up_read, 4 * g + j + 1)
                        if j >= 2:
                            act.wait_ge(a_ready, 4 * g + j - 1)
                        nc.scalar.activation(act2[:, j % 2], relu[:, j % 2], ACT.Square).then_inc(squared, 1)
                        act.wait_ge(squared, 4 * g + j + 1)
                        nc.scalar.copy(a_hi[:, j], act2[:, j % 2]).then_inc(a_hi_done, 1)
                tail.scalar(act)

            @block.vector
            def _(dve):
                dve.sem_inc(y_added, 2)
                norm.vector(dve)
                norm.free(dve)
                norm.kept_ready(dve)
                dve.wait_ge(y_zero, 1)
                with dve.Fori(0, FF_GROUPS) as g:
                    for j in range(FF_TILES):
                        dve.wait_ge(up_full, 4 * g + j + 1)
                        if j >= 2:
                            dve.wait_ge(squared, 4 * g + j - 1)
                        nc.vector.scalar_tensor_tensor(out=blocks_of(relu[:, j % 2]), in0=chip.psum_set(j % 2), scalar=0.0,
                                                       in1=blocks_of(norm.keep[:]), op0=ALU.max,
                                                       op1=ALU.mult).then_inc(up_read, 1)
                        dve.wait_ge(a_hi_done, 4 * g + j + 1)
                        nc.vector.tensor_tensor(a_lo[:, j], act2[:, j % 2], a_hi[:, j].bitcast(F32),
                                                ALU.subtract).then_inc(a_ready, 1)
                    for m in range(KT):
                        dve.wait_ge(down_full, 8 * g + m + 1)
                        nc.vector.tensor_tensor(blocks_of(chip.y[:, m]), chip.psum_set(m % 2), blocks_of(chip.y[:, m]),
                                                ALU.add).then_inc(y_added, 1)
                tail.vector(dve)
    tail.close()
    ws.base += 8 * FF_GROUPS


def gla(chip, name, ins, norm):
    nc = chip.nc
    n_tok = lambda p: min(2 * CHUNK, T - 2 * CHUNK * p)
    n_chunks = lambda p: n_tok(p) // CHUNK
    SCORE_BANK, UPDATE_BANK, OUT_BANK = 3, 5, 7
    R_SLOTS = range(0, 8)
    OUT_SLOTS = range(8, 16)
    with ExitStack() as ctx:
        sb = lambda n, shape, dt=F32: ctx.enter_context(nc.sbuf_tensor(f"{name}_{n}", shape, dt))
        sem = lambda n: chip.sem(f"{name}_{n}")
        masks = sb("masks", [P, NLEV + 1, P])
        qk = sb("qk", [P, 2, TP])
        vr = sb("vr", [P, 2, TP])
        b = sb("b", [P, TP])
        rank = sb("rank", [RANK, TP])
        rank_w = sb("rank_w", [P, KT * RANK])
        rank_w_hi = sb("rank_w_hi", [P, KT * RANK], F32R)
        rank_w_lo = sb("rank_w_lo", [P, KT * RANK], F32R)
        gate_w = sb("gate_w", [RANK, P])
        gate_b = sb("gate_b", [P, 1])
        o_gain = sb("o_gain", [P, 2])
        v_tok = sb("v_tok", [P, NPAIR, DV])
        o_hi = sb("o_hi", [P, 2, TP], F32R)
        o_lo = sb("o_lo", [P, 2, TP], F32R)
        work = sb("work", [P, 2 * TP])
        lev = work[:, 0:2 * (NLEV + 2) * P].rearrange("p (b l n) -> p b l n", b=2, l=NLEV + 2)
        flat = work[:, 0:TP]
        o_diag = work[:, 0:Norm.N_TOK * P].rearrange("p (j n) -> p j n", n=P)
        o_var = sb("o_var", [P, Norm.N_TOK])
        o_rs = sb("o_rs", [P, Norm.N_TOK])
        prod = sb("prod", [P, NLEV + 1, P])
        att = sb("att", [P, 2, P])
        kdt = sb("kdt", [P, 2, P])
        end_decay = sb("end_decay", [P, NCH])
        state = sb("state", [P, 2, 2, DV])
        s_in = sb("s_in", [P, DV])
        s_out = sb("s_out", [P, 2, DV])
        ws = chip.stream

        masks_in = sem("masks_in")
        const_in, gain_in, state_in, state_st = sem("const_in"), sem("gain_in"), sem("state_in"), sem("state_st")
        y_zero, rank_raw, rank_hi, rank_split, rank_full, rank_done = (
            sem("y_zero"), sem("rank_raw"), sem("rank_hi"), sem("rank_split"), sem("rank_full"), sem("rank_done"))
        proj_full, proj_read = sem("proj_full"), sem("proj_read")
        gate_step, gate_exp, decay_sum = sem("gate_step"), sem("gate_exp"), sem("decay_sum")
        end_exp = sem("end_exp")
        v_turned, v_copied = sem("v_turned"), sem("v_copied")
        lev_diff, lev_exp, lev_ready = sem("lev_diff"), sem("lev_exp"), sem("lev_ready")
        scores_full, masked, att_ready, kdt_ready = sem("scores_full"), sem("masked"), sem("att_ready"), sem("kdt_ready")
        upd_full, state_new, state_zero = sem("upd_full"), sem("state_new"), sem("state_zero")
        o_full, o_read = sem("o_full"), sem("o_read")
        osq_done, osum_full, ovar_done, ostd_done, ors_done = (
            sem("osq_done"), sem("osum_full"), sem("ovar_done"), sem("ostd_done"), sem("ors_done"))
        odiag_done, orms_full = sem("odiag_done"), sem("orms_full")
        o_scaled, o_gated, o_hi_done, o_ready = sem("o_scaled"), sem("o_gated"), sem("o_hi_done"), sem("o_ready")
        out_full, y_added = sem("out_full"), sem("y_added")
        v_flat = v_tok[:].rearrange("p n d -> p (n d)")
        squares = [qk[:, 0], qk[:, 1], vr[:, 0], vr[:, 1], work[:, 0:TP], work[:, TP:2 * TP],
                   v_flat[:, 0:TP], v_flat[:, TP:2 * TP]]
        tail = SquareSums(chip, squares, [(m, m - 1) for m in range(1, KT - 1)], [(KT - 1, KT - 2)],
                          lambda engine, m: engine.wait_ge(y_added, 1 + NB * (KT * (GH - 1) + m + 1)))

        with nc.Block() as block:

            @block.sync
            def _(sp):
                norm.load_x(sp)
                ws.load_first(sp)
                for s in range(2):
                    ws.load_one(sp, 1, s)
                norm.free(sp)
                sp.dma_start(rank_w[:], ins["gate_a"]).then_inc(rank_raw, 16)
                sp.dma_start(masks[:], ins["masks"]).then_inc(masks_in, 16)
                ws.load(sp, 8 * GH)

            @block.gpsimd
            def _(pool):
                for s in range(2):
                    ws.split(pool, 0, s)
                norm.gpsimd(pool)
                norm.free(pool)
                pool.wait_ge(rank_raw, 16)
                nc.gpsimd.tensor_tensor(rank_w_hi[:], rank_w[:], chip.ones[:, 0:KT * RANK], ALU.mult).then_inc(rank_hi, 1)
                pool.wait_ge(rank_hi, 1)
                nc.gpsimd.tensor_tensor(rank_w_lo[:], rank_w[:], rank_w_hi[:].bitcast(F32),
                                        ALU.subtract).then_inc(rank_split, 1)
                nc.gpsimd.memset(chip.y[:], 0.0).then_inc(y_zero, 1)
                ws.split_from(pool, 1, 8 * GH)
                tail.gpsimd(pool)

            @block.tensor
            def _(pe):
                norm.tensor(pe)

                def rank_tile():
                    pe.wait_ge(rank_split, 1)
                    for k in range(KT):
                        w_hi, w_lo = rank_w_hi[:, k * RANK:(k + 1) * RANK], rank_w_lo[:, k * RANK:(k + 1) * RANK]
                        for n, (w, x) in enumerate(((w_hi, chip.h_hi), (w_hi, chip.h_lo), (w_lo, chip.h_hi))):
                            for blk in range(NB):
                                mm = nc.tensor.matmul(chip.banks[0:RANK, 3 + blk, 0:BW], w, x[:, k, blk * BW:(blk + 1) * BW],
                                                      start=(k == 0 and n == 0), stop=(k == KT - 1 and n == 2))
                    mm.then_inc(rank_full, 1)

                def unit_ready(h, unit):
                    ws.wait_ready(pe, (unit if isinstance(h, int) and h == 0 else 8 * h - 2 + unit) + 1)

                def o_square_sums(h):
                    for half in range(2):
                        pe.wait_ge(osq_done, 2 * h + half - 1)
                        for j, t in enumerate(Norm.TOK):
                            mm = nc.tensor.matmul(chip.banks[:, Norm.SUM_BANK, j:j + 1],
                                                  work[:, half * TP + t:half * TP + t + P], chip.ones[:, 0:1],
                                                  start=(half == 0 and j == 0), stop=(half == 1 and j == Norm.N_TOK - 1))
                    mm.then_inc(osum_full, 1)

                def spread_o_rms(h):
                    pe.wait_ge(masked, 2 * NPAIR * h)
                    pe.wait_ge(state_new, NCH * h)
                    for piece in range(NB):
                        pe.wait_ge(odiag_done, NB * (h - 1) + piece + 1)
                        if piece < 2:
                            width, rhs = 4 * P, o_diag[:, 4 * piece:4 * piece + 4]
                        else:
                            width, rhs = TP - SEQ, o_diag[:, 8, P - (TP - SEQ):P]
                        nc.tensor.matmul(chip.banks[:, 3 + piece, 0:width], chip.ones[:], rhs,
                                         start=True, stop=True).then_inc(orms_full, 1)

                def output_tile(h, m, s, stationary_slot, before_bank=None):
                    if m == 0:
                        pe.wait_ge(o_ready, 2 * h)
                    for k in range(2):
                        mm = dense_part(chip, s, k, 2, k * 4 * P + (m % 4) * P, stationary_slot, o_hi, o_lo,
                                        ws.begun if m % 4 == 0 and k == 0 else None, before_bank if k == 0 else None)
                    mm.then_inc(out_full, 1)

                def head(h, is_first):

                    def projection(n, unit, k_tiles=range(KT)):
                        s = n % 2 if n < 5 else 0
                        if 0 in k_tiles and unit is not None:
                            unit_ready(h, unit)
                        if unit is None:
                            for blk in range(NB):
                                mm = nc.tensor.matmul(chip.banks[:, 3 * s + blk, 0:BW], gate_w[:],
                                                      rank[:, blk * BW:(blk + 1) * BW], start=True, stop=True)
                        else:
                            for k in k_tiles:
                                if is_first and n == 0:
                                    norm.h_ready(pe, k)
                                mm = dense_part(chip, s, k, KT, k * P, unit % 2, chip.h_hi, chip.h_lo,
                                                ws.begun if k == 0 else None)
                        if unit is None or KT - 1 in k_tiles:
                            mm.then_inc(proj_full, 1)

                    def turn_v(p):
                        n = n_tok(p)
                        if 2 <= p < NPAIR - 2:
                            pe.wait_ge(v_copied, NPAIR * h + p - 1)
                        if p == NPAIR - 2:
                            pe.wait_ge(v_copied, NPAIR * h + p)
                        for half in range(2):
                            mm = nc.tensor.transpose(chip.banks[0:n, 6 + p % 2, half * P:(half + 1) * P],
                                                     vr[:, half, 2 * CHUNK * p:2 * CHUNK * p + n], chip.ident[:])
                        mm.then_inc(v_turned, 1)

                    def scores(p):
                        n, t0, w = n_tok(p), 2 * CHUNK * p, lev[:, p % 2]
                        pe.wait_ge(lev_ready, NPAIR * h + p + 1)
                        if p >= 1:
                            pe.wait_ge(masked, 2 * (NPAIR * h + p))
                        for level in range(NLEV):
                            nc.tensor.matmul(chip.banks[0:n, SCORE_BANK + level // 4, (level % 4) * P:(level % 4) * P + n],
                                             w[:, level, 0:n], w[:, level, 0:n], start=True, stop=True)
                        if p >= 1:
                            pe.wait_ge(o_read, NPAIR * h + p)
                        nc.tensor.matmul(chip.banks[0:n, SCORE_BANK + 1, 2 * P:2 * P + n],
                                         qk[:, 1, t0:t0 + n], qk[:, 0, t0:t0 + n], start=True, stop=True)
                        nc.tensor.transpose(chip.banks[0:n, OUT_BANK, 3 * P:4 * P], w[:, KW, 0:n],
                                            chip.ident[:]).then_inc(scores_full, 1)

                    def update(p):
                        pe.wait_ge(kdt_ready, NPAIR * h + p + 1)
                        if p >= 1:
                            pe.wait_ge(state_new, NCH * h + 2 * p)
                        for c in range(n_chunks(p)):
                            rows = slice(c * CHUNK, (c + 1) * CHUNK)
                            mm = nc.tensor.matmul(chip.banks[:, UPDATE_BANK + c, 0:DV], kdt[rows, p % 2, :],
                                                  v_tok[rows, p, :], start=True, stop=True)
                        mm.then_inc(upd_full, 1)

                    def output(p):
                        n = n_tok(p)
                        pe.wait_ge(att_ready, NPAIR * h + p + 1)
                        halves = [(half == 0, slice(half * P, (half + 1) * P),
                                   chip.banks[:, OUT_BANK, half * P:half * P + n]) for half in range(2)]
                        for is_start, f, out in halves:
                            nc.tensor.matmul(out, v_tok[0:n, p, f], att[0:n, p % 2, 0:n], start=is_start, stop=False)
                        for c in range(n_chunks(p)):
                            if p == NPAIR - 1:
                                pe.wait_ge(state_in, 16 * h + 16)
                            elif p == 0 and c == 0:
                                pe.wait_ge(state_zero, h + 1)
                            else:
                                pe.wait_ge(state_new, NCH * h + 2 * p + c)
                            for is_start, f, out in halves:
                                s = s_in[:, f] if p == NPAIR - 1 else state[:, p % 2, c, f]
                                mm = nc.tensor.matmul(out[:, c * CHUNK:(c + 1) * CHUNK], s,
                                                      lev[:, p % 2, CW, c * CHUNK:(c + 1) * CHUNK],
                                                      start=False, stop=(c == n_chunks(p) - 1 and not is_start))
                        mm.then_inc(o_full, 1)

                    def dense_slot(n):
                        if is_first:
                            n = n // 2 if n % 2 == 0 and n < 2 * len(R_SLOTS) else -1
                        if n in R_SLOTS:
                            if n == 4:
                                pe.wait_ge(proj_read, 7 * h + 6)
                            projection(5 + n // 4, 4 + n // 4, range(2 * (n % 4), 2 * (n % 4) + 2))
                        if n in OUT_SLOTS and not is_first:
                            m = n - OUT_SLOTS.start
                            if m == 0:
                                pe.wait_ge(proj_read, 7 * h + 7)
                            if m % 4 == 0:
                                unit_ready(h, 6 + m // 4)

                            def bank_read(b):
                                pe.wait_ge(y_added, NB * KT * (h - 1) + (NB * m + b - 1))

                            output_tile(h, m, 0, m // 4, bank_read if m else None)

                    if is_first:
                        projection(0, 0)
                        rank_tile()
                        pe.wait_ge(rank_done, 1)
                    else:
                        pe.wait_ge(y_added, NB * KT * (h - 1) + 1)
                        projection(0, 0, range(0, 3))
                        o_square_sums(h)
                        projection(0, 0, range(3, 5))
                        spread_o_rms(h)
                        projection(0, 0, range(5, KT))
                        pe.wait_ge(o_scaled, 2 * h)
                    projection(1, 1)
                    pe.wait_ge(const_in, 32 * h + 32)
                    pe.wait_ge(proj_read, 7 * h + 1)
                    projection(2, None)
                    pe.wait_ge(proj_read, 7 * h + 2)
                    projection(3, 2)
                    pe.wait_ge(proj_read, 7 * h + 3)
                    projection(4, 3)
                    pe.wait_ge(proj_read, 7 * h + 5)
                    for p in range(NPAIR):
                        turn_v(p)
                    pe.wait_ge(v_copied, NPAIR * h + NPAIR)
                    for p in range(NPAIR):
                        scores(p)
                        dense_slot(2 * p)
                        update(p)
                        output(p)
                        dense_slot(2 * p + 1)

                head(0, True)
                with pe.Fori(1, GH) as h:
                    head(h, False)
                o_square_sums(GH)
                spread_o_rms(GH)
                for m in range(KT):
                    if m == 0:
                        pe.wait_ge(y_added, NB * KT * (GH - 1) + 1)
                    if m == 1:
                        pe.wait_ge(o_scaled, 2 * GH)
                    if m >= 2:
                        pe.wait_ge(y_added, NB * (KT * (GH - 1) + m - 1) + 1)
                    if m % 4 == 0:
                        unit_ready(GH, m // 4)
                    output_tile(GH, m, m % 2, m // 4)
                tail.tensor(pe)

            @block.scalar
            def _(act):
                act.sem_inc(state_st, 16)
                norm.scalar(act)
                norm.free(act)

                def squares(h):
                    act.wait_ge(o_read, NPAIR * h)
                    act.wait_ge(lev_ready, NPAIR * h)
                    for half in range(2):
                        nc.scalar.activation(work[:, half * TP:(half + 1) * TP], qk[:, half], ACT.Square).then_inc(osq_done, 1)
                    act.wait_ge(state_new, NCH * h)
                    act.dma_start(ins["state_prompt"][bass.ds(h - 1, 1)], s_out[:, 0]).then_inc(state_st, 16)
                    act.dma_start(ins["state_sample"][bass.ds(h - 1, 1)], s_out[:, 1]).then_inc(state_st, 16)

                def high_parts(h):
                    for half in range(2):
                        act.wait_ge(o_gated, 2 * h + half - 1)
                        nc.scalar.copy(o_hi[:, half], work[:, half * TP:(half + 1) * TP]).then_inc(o_hi_done, 1)

                def head(h, is_first):
                    if not is_first:
                        squares(h)
                    act.dma_start(gate_w[:], ins["gate_b"][h]).then_inc(const_in, 16)
                    act.dma_start(gate_b[:], ins["gate_bias"][h]).then_inc(const_in, 16)
                    act.dma_start(s_in[:], ins["state_gla"][h]).then_inc(state_in, 16)
                    if not is_first:
                        act.wait_ge(ovar_done, h)
                        nc.scalar.activation(o_rs[:], o_var[:], ACT.Sqrt).then_inc(ostd_done, 1)
                        act.wait_ge(o_scaled, 2 * h)
                    else:
                        act.wait_ge(rank_full, 1)
                        nc.scalar.copy(blocks_of(rank[:]), chip.psum_set(1)[0:RANK]).then_inc(rank_done, 1)
                    act.dma_start(o_gain[:], ins["gla_gain"][h]).then_inc(gain_in, 16)
                    act.wait_ge(proj_full, 7 * h + 1)
                    nc.scalar.copy(blocks_of(qk[:, 1]), chip.psum_set(0)).then_inc(proj_read, 1)
                    if not is_first:
                        high_parts(h)
                    act.wait_ge(proj_full, 7 * h + 2)
                    nc.scalar.mul(blocks_of(qk[:, 0]), chip.psum_set(1), float(P) ** -0.5).then_inc(proj_read, 1)
                    act.wait_ge(const_in, 32 * h + 32)
                    act.wait_ge(proj_full, 7 * h + 3)
                    nc.scalar.activation(blocks_of(b[:]), chip.psum_set(0), ACT.Identity,
                                         bias=gate_b[:]).then_inc(proj_read, 1)
                    act.wait_ge(gate_step, 2 * h + 1)
                    nc.scalar.activation(flat, flat, ACT.Exp).then_inc(gate_exp, 1)
                    act.wait_ge(gate_exp, 2 * h + 1)
                    nc.scalar.activation(flat, flat, ACT.Ln, bias=1.0).then_inc(gate_exp, 1)

                    def take_v(half):
                        act.wait_ge(proj_full, 7 * h + 4 + half)
                        nc.scalar.copy(blocks_of(vr[:, half]), chip.psum_set((3 + half) % 2)).then_inc(proj_read, 1)

                    take_v(0)
                    act.wait_ge(decay_sum, NCH * (h + 1))
                    chunk_ends = b[:, 0:T].rearrange("p (c n) -> p c n", n=CHUNK)[:, :, CHUNK - 1]
                    nc.scalar.activation(end_decay[:], chunk_ends, ACT.Exp, scale=1.0 / GATE_NORM).then_inc(end_exp, 1)

                    def level_exp(p):
                        n, w = n_tok(p), lev[:, p % 2]
                        act.wait_ge(lev_diff, NPAIR * h + p + 1)
                        nc.scalar.activation(w[:, :, 0:n], w[:, :, 0:n], ACT.Exp, scale=1.0 / GATE_NORM).then_inc(lev_exp, 1)

                    level_exp(0)
                    level_exp(1)
                    take_v(1)
                    for p in range(NPAIR):
                        act.wait_ge(v_turned, NPAIR * h + p + 1)
                        nc.scalar.copy(v_tok[0:n_tok(p), p, :],
                                       chip.banks[0:n_tok(p), 6 + p % 2, 0:DV]).then_inc(v_copied, 1)
                    for p in range(NPAIR):
                        n, t0 = n_tok(p), 2 * CHUNK * p
                        act.wait_ge(scores_full, NPAIR * h + p + 1)
                        if p >= 2:
                            act.wait_ge(upd_full, NPAIR * h + p - 1)
                        nc.scalar.copy(kdt[0:n, p % 2, :], chip.banks[0:n, OUT_BANK, 3 * P:4 * P]).then_inc(kdt_ready, 1)
                        act.wait_ge(o_full, NPAIR * h + p + 1)
                        o_bank = chip.banks[:, OUT_BANK, 0:2 * P].rearrange("p (v n) -> p v n", v=2)
                        nc.scalar.copy(qk[:, :, t0:t0 + n], o_bank[:, :, 0:n]).then_inc(o_read, 1)
                        if p in ((3, 7) if is_first else (1, 3)):
                            half = p // 4 if is_first else p // 2
                            act.wait_ge(proj_full, 7 * h + 6 + half)
                            nc.scalar.activation(blocks_of(vr[:, half]), chip.psum_set(0), ACT.Silu).then_inc(proj_read, 1)
                        if p + 2 < NPAIR:
                            level_exp(p + 2)

                head(0, True)
                with act.Fori(1, GH) as h:
                    head(h, False)
                squares(GH)
                act.wait_ge(ovar_done, GH)
                nc.scalar.activation(o_rs[:], o_var[:], ACT.Sqrt).then_inc(ostd_done, 1)
                high_parts(GH)
                tail.scalar(act)
                act.wait_ge(state_st, 32 * GH + 16)

            @block.vector
            def _(dve):
                dve.sem_inc(y_added, 1)
                norm.vector(dve)
                norm.free(dve)
                dve.wait_ge(masks_in, 16)
                dve.wait_ge(y_zero, 1)

                def norm_and_gate(h):
                    dve.wait_ge(osum_full, h)
                    nc.vector.tensor_scalar(o_var[:], chip.banks[:, Norm.SUM_BANK, 0:Norm.N_TOK], 1.0 / DV, EPS, ALU.mult,
                                            ALU.add).then_inc(ovar_done, 1)
                    dve.wait_ge(ostd_done, h)
                    nc.vector.reciprocal(o_rs[:], o_rs[:]).then_inc(ors_done, 1)
                    dve.wait_ge(ors_done, h)
                    for j0, j1 in ((0, 4), (4, 8), (8, 9)):
                        shape = [P, j1 - j0, P]
                        nc.vector.tensor_tensor(o_diag[:, j0:j1], chip.ident[:, None, :].to_broadcast(shape),
                                                o_rs[:, j0:j1, None].to_broadcast(shape), ALU.mult).then_inc(odiag_done, 1)
                    dve.wait_ge(orms_full, NB * h)
                    o_rms = chip.banks[:, 3:3 + NB].rearrange("p b n -> p (b n)")[:, 0:TP]
                    dve.wait_ge(gain_in, 16 * h)
                    for half in range(2):
                        o = work[:, half * TP:(half + 1) * TP]
                        nc.vector.scalar_tensor_tensor(out=o, in0=qk[:, half], scalar=o_gain[:, half:half + 1],
                                                       in1=o_rms, op0=ALU.mult, op1=ALU.mult).then_inc(o_scaled, 1)
                    dve.wait_ge(proj_read, 7 * h)
                    dve.wait_ge(o_scaled, 2 * h)
                    for half in range(2):
                        o = work[:, half * TP:(half + 1) * TP]
                        nc.vector.tensor_tensor(o, o, vr[:, half], ALU.mult).then_inc(o_gated, 1)
                    for half in range(2):
                        o = work[:, half * TP:(half + 1) * TP]
                        dve.wait_ge(o_hi_done, 2 * h + half - 1)
                        nc.vector.tensor_tensor(o_lo[:, half], o, o_hi[:, half].bitcast(F32), ALU.subtract).then_inc(o_ready, 1)

                def add_output(h, m, s):
                    dve.wait_ge(out_full, KT * (h - 1) + m + 1)
                    for blk in range(NB):
                        cols = slice(blk * BW, (blk + 1) * BW)
                        nc.vector.tensor_tensor(chip.y[:, m, cols], chip.banks[:, 3 * s + blk, 0:BW], chip.y[:, m, cols],
                                                ALU.add).then_inc(y_added, 1)

                def head(h, is_first):
                    if not is_first:
                        norm_and_gate(h)
                        dve.wait_ge(o_ready, 2 * h)
                    dve.wait_ge(proj_read, 7 * h + 3)
                    nc.vector.scalar_tensor_tensor(out=flat, in0=b[:], scalar=-1.0, in1=b[:], op0=ALU.mult,
                                                   op1=ALU.min).then_inc(gate_step, 1)
                    dve.wait_ge(gate_exp, 2 * h + 2)
                    nc.vector.scalar_tensor_tensor(out=flat, in0=b[:], scalar=0.0, in1=flat, op0=ALU.min,
                                                   op1=ALU.subtract).then_inc(gate_step, 1)
                    dve.wait_ge(gate_step, 2 * h + 2)
                    for c in range(NCH):
                        t = slice(c * CHUNK, (c + 1) * CHUNK)
                        nc.vector.tensor_tensor_scan(b[:, t], chip.ones[:, 0:CHUNK], flat[:, t], 0.0, ALU.mult,
                                                     ALU.add).then_inc(decay_sum, 1)
                    dve.wait_ge(decay_sum, NCH * (h + 1))
                    nc.vector.memset(state[:, 0, 0], 0.0).then_inc(state_zero, 1)

                    def differences(p):
                        n, w = n_tok(p), lev[:, p % 2]
                        bp = b[:, 2 * CHUNK * p:2 * CHUNK * p + n]
                        for level, s in enumerate(HALVES):
                            split = lambda x: x.rearrange("p (n two s) -> p n two s", two=2, s=s)
                            bs, out = split(bp), split(w[:, level, 0:n])
                            ref = bs[:, :, 0, s - 1:s].to_broadcast([P, n // (2 * s), s])
                            nc.vector.tensor_tensor(out[:, :, 1], bs[:, :, 1], ref, ALU.subtract)
                            nc.vector.tensor_tensor(out[:, :, 0], ref, bs[:, :, 0], ALU.subtract)
                        nc.vector.tensor_copy(w[:, CW, 0:n], bp)
                        bc, out = (x.rearrange("p (c n) -> p c n", n=CHUNK) for x in (bp, w[:, KW, 0:n]))
                        ends = bc[:, :, CHUNK - 1:CHUNK].to_broadcast([P, n_chunks(p), CHUNK])
                        nc.vector.tensor_tensor(out, ends, bc, ALU.subtract).then_inc(lev_diff, 1)

                    def decayed(p, levels):
                        n, w = n_tok(p), lev[:, p % 2]
                        t = slice(2 * CHUNK * p, 2 * CHUNK * p + n)
                        q, k = qk[:, 0, t], qk[:, 1, t]
                        dve.wait_ge(lev_exp, NPAIR * h + p + 1)
                        for level in levels:
                            s = HALVES[level]
                            split = lambda x: x.rearrange("p (n two s) -> p n two s", two=2, s=s)
                            out = split(w[:, level, 0:n])
                            nc.vector.tensor_tensor(out[:, :, 1], out[:, :, 1], split(q)[:, :, 1], ALU.mult)
                            nc.vector.tensor_tensor(out[:, :, 0], out[:, :, 0], split(k)[:, :, 0], ALU.mult)
                        if NLEV - 1 in levels:
                            nc.vector.tensor_tensor(w[:, CW, 0:n], w[:, CW, 0:n], q, ALU.mult)
                            nc.vector.tensor_tensor(w[:, KW, 0:n], w[:, KW, 0:n], k, ALU.mult).then_inc(lev_ready, 1)

                    def attention(p):
                        n = n_tok(p)
                        dve.wait_ge(scores_full, NPAIR * h + p + 1)
                        if p >= 1:
                            dve.wait_ge(att_ready, NPAIR * h + p)
                        for g, (l0, l1) in enumerate(((0, 4), (4, NLEV + 1))):
                            ps = chip.banks[0:n, SCORE_BANK + g].rearrange("p (l n) -> p l n", n=P)
                            nc.vector.tensor_tensor(prod[0:n, l0:l1, 0:n], ps[:, 0:l1 - l0, 0:n], masks[0:n, l0:l1, 0:n],
                                                    ALU.mult).then_inc(masked, 1)
                        dve.wait_ge(masked, 2 * (NPAIR * h + p + 1))
                        if p >= 2:
                            dve.wait_ge(o_full, NPAIR * h + p - 1)
                        nc.vector.tensor_reduce(att[0:n, p % 2, 0:n], prod[0:n, :, 0:n].rearrange("p l n -> p n l"),
                                                AX_X, ALU.add).then_inc(att_ready, 1)

                    def states(p):
                        dve.wait_ge(end_exp, h + 1)
                        dve.wait_ge(upd_full, NPAIR * h + p + 1)
                        if p >= 1:
                            dve.wait_ge(o_full, NPAIR * h + p)
                        for c in range(n_chunks(p)):
                            chunk = 2 * p + c
                            if p == NPAIR - 1:
                                dve.wait_ge(state_in, 16 * h + 16)
                                before, after = s_in[:], s_out[:, 1]
                            else:
                                before = state[:, p % 2, c]
                                if c == 0:
                                    after = state[:, p % 2, 1]
                                else:
                                    after = s_out[:, 0] if p == NPAIR - 2 else state[:, (p + 1) % 2, 0]
                            if chunk:
                                dve.wait_ge(state_new, NCH * h + chunk)
                            else:
                                dve.wait_ge(state_zero, h + 1)
                            if chunk == 2 * NPAIR - 3:
                                dve.wait_ge(state_st, 32 * h + 16)
                            nc.vector.scalar_tensor_tensor(out=after, in0=before, scalar=end_decay[:, chunk:chunk + 1],
                                                           in1=chip.banks[:, UPDATE_BANK + c, 0:DV],
                                                           op0=ALU.mult, op1=ALU.add).then_inc(state_new, 1)

                    differences(0)
                    differences(1)
                    decayed(0, range(NLEV))
                    for p in range(NPAIR):
                        attention(p)
                        if p + 1 < NPAIR:
                            decayed(p + 1, range(NLEV - 1))
                        states(p)
                        if 2 * p in OUT_SLOTS and not is_first:
                            add_output(h, 2 * p - OUT_SLOTS.start, 0)
                        if p + 1 < NPAIR:
                            decayed(p + 1, (NLEV - 1,))
                        if p + 2 < NPAIR:
                            dve.wait_ge(o_full, NPAIR * h + p + 1)
                            differences(p + 2)
                        if 2 * p + 1 in OUT_SLOTS and not is_first:
                            add_output(h, 2 * p + 1 - OUT_SLOTS.start, 0)

                head(0, True)
                with dve.Fori(1, GH) as h:
                    head(h, False)
                norm_and_gate(GH)
                for m in range(KT):
                    add_output(GH, m, m % 2)
                tail.vector(dve)
    tail.close()
    ws.base += 8 * GH


def swa(chip, name, ins, norm):
    nc = chip.nc
    n_tiles = KVP * GROUP
    scale = float(CHUNK) ** -0.5
    SAMPLE = NCH - 1
    n_full = SEQ // P
    OUT_FROM = 9
    SCORE_BANK, TURN_BANK, OUT_BANK = 3, 5, 7

    def window(c):
        if c == SAMPLE:
            return CACHE0, WIN, ((0, P, n_full), (P, CHUNK, n_full + 1))
        if c == 0:
            return 0, CHUNK, ((0, CHUNK, 0),)
        if c == 1:
            return 0, 2 * CHUNK, ((P, P, 0),)
        first = (c - 2) // 2
        return CHUNK * (c - 2), WIN, ((0, P, first), (P, P if c % 2 else CHUNK, first + 1))

    def prob_cols(c):
        n = window(c)[1]
        first = 0 if c % 2 == 0 else (CHUNK if n == WIN else P)
        return slice(first, first + n + 1)

    with ExitStack() as ctx:
        sb = lambda n, shape, dt=F32: ctx.enter_context(nc.sbuf_tensor(f"{name}_{n}", shape, dt))
        sem = lambda n: chip.sem(f"{name}_{n}")
        kT = sb("kT", [P, KVP, KCOLS])
        v_fm = sb("v_fm", [P, KVP, TP])
        v_tok = sb("v_tok", [P, KVP, n_full + 2, P])
        q_flat = sb("q_flat", [P, TP])
        q2 = sb("q2", [P, NCH, 2, CHUNK])
        prob = sb("prob", [P, 2, 2 * P + 2])
        probT = sb("probT", [P, 2, 2, P])
        o = sb("o", [P, TP])
        o_hi = sb("o_hi", [P, 1, TP], F32R)
        o_lo = sb("o_lo", [P, 1, TP], F32R)
        biases = sb("biases", [P, n_tiles + 2 * KVP])
        q_bias = sb("q_bias", [P, 1])
        sink_col = sb("sink_col", [P, 1])
        out_bias = sb("out_bias", [P, KT])
        sinks = sb("sinks", [P, n_tiles])
        neg_max, p_sum, p_inv = (sb(n, [P, NCH]) for n in ("neg_max", "p_sum", "p_inv"))
        ws = chip.stream

        cache_in, cache_out, const_in, y_zero, y_bias = (
            sem("cache_in"), sem("cache_out"), sem("const_in"), sem("y_zero"), sem("y_bias"))
        pads_zero, bias_ready, sink_ready = sem("pads_zero"), sem("bias_ready"), sem("sink_ready")
        kv_scaled = sem("kv_scaled")
        kv_full, kv_read, v_turned, v_copied = sem("kv_full"), sem("kv_read"), sem("v_turned"), sem("v_copied")
        q_full, q_read, q_ready = sem("q_full"), sem("q_read"), sem("q_ready")
        scores_full, maxed = sem("scores_full"), sem("maxed")
        exp_done, inverted, normed = sem("exp_done"), sem("inverted"), sem("normed")
        probT_full, probT_ready = sem("probT_full"), sem("probT_ready")
        o_full, o_read, o_hi_done, o_ready = sem("o_full"), sem("o_read"), sem("o_hi_done"), sem("o_ready")
        out_full, y_added = sem("out_full"), sem("y_added")
        more = sb("more_squares", [P, 3, TP])
        squares = [v_fm[:, 0], v_fm[:, 1], q_flat[:], o[:], q2[:].rearrange("p c a n -> p (c a n)")[:, 0:TP],
                   more[:, 0], more[:, 1], more[:, 2]]
        tail = SquareSums(chip, squares, [(1, 0), (2, 1), (3, 2)], [(5, 4), (6, 5), (6, 3), (7, 6)],
                          lambda engine, m: engine.wait_ge(y_added, 1 + NB * (KT * (n_tiles - 1) + m + 1)))

        with nc.Block() as block:

            @block.sync
            def _(sp):
                norm.load_x(sp)
                ws.load_one(sp, 1, 0)
                norm.store_x(sp)
                ws.load_one(sp, 1, 1)
                ws.load_one(sp, 2, 0)
                norm.free(sp)
                sp.dma_start(biases[:], ins["swa_bias"]).then_inc(const_in, 16)
                sp.dma_start(out_bias[:], ins["swa_out_bias"]).then_inc(const_in, 16)
                sp.dma_start(sinks[:], ins["sinks"]).then_inc(const_in, 16)
                sp.dma_start(kT[:, :, CACHE0:NEW0], ins["cache_k"]).then_inc(cache_in, 16)
                sp.dma_start(v_tok[:, :, n_full], ins["cache_v"]).then_inc(cache_in, 16)
                ws.load_one(sp, 2, 1)
                ws.load(sp, 2 * KVP + 2 * n_tiles, first=3)
                sp.wait_ge(kv_read, 4 * KVP)
                sp.wait_ge(v_copied, KVP * NPAIR)
                sp.wait_ge(cache_in, 32)
                sp.dma_start(ins["k_prompt"], kT[:, :, SEQ - P:SEQ]).then_inc(cache_out, 16)
                sp.dma_start(ins["k_sample"], kT[:, :, KCOLS - P:KCOLS]).then_inc(cache_out, 16)
                sp.dma_start(ins["v_prompt"], v_tok[:, :, n_full - 1]).then_inc(cache_out, 16)
                sp.dma_start(ins["v_sample"][0:CHUNK], v_tok[CHUNK:P, :, n_full]).then_inc(cache_out, 16)
                sp.dma_start(ins["v_sample"][CHUNK:P], v_tok[0:CHUNK, :, n_full + 1]).then_inc(cache_out, 16)
                sp.wait_ge(cache_out, 80)

            @block.gpsimd
            def _(pool):
                ws.split(pool, 0, 0)
                norm.gpsimd(pool)
                ws.split(pool, 0, 1)
                norm.y_read(pool)
                ws.split_when_free(pool, 1, 0)
                nc.gpsimd.memset(chip.y[:], 0.0).then_inc(y_zero, 1)
                ws.split_when_free(pool, 1, 1)
                norm.free(pool)
                nc.gpsimd.memset(q2[:], 0.0).then_inc(pads_zero, 1)
                nc.gpsimd.memset(o[:], 0.0).then_inc(pads_zero, 1)
                nc.gpsimd.memset(prob[:], 0.0).then_inc(pads_zero, 1)
                ws.split_from(pool, 2, 2 * KVP + 2 * n_tiles)
                tail.gpsimd(pool)

            @block.tensor
            def _(pe):
                norm.tensor(pe)
                for i in range(KVP):
                    for n in range(2):
                        ws.wait_ready(pe, 2 * i + n + 1)
                        if i:
                            pe.wait_ge(kv_scaled, n + 1)
                        before_k = None
                        if i == 0:
                            before_k = lambda k, n=n: (norm.before_second_tile if n else norm.h_ready)(pe, k)
                        dense_tile(chip, n, lambda k: k * P, n, chip.h_hi, chip.h_lo, ws.begun, before_k).then_inc(kv_full, 1)

                def queries(t, slot, ready, k):
                    if k == 0:
                        ws.wait_ready(pe, ready)
                        if not isinstance(t, int) or t > 1:
                            pe.wait_ge(y_added, NB * KT * (t - 2) + 1)
                    mm = dense_part(chip, 0, k, KT, k * P, slot, chip.h_hi, chip.h_lo, ws.begun if k == 0 else None)
                    if k == KT - 1:
                        mm.then_inc(q_full, 1)

                def out_tile(t, slot, ready, m, is_last=False):
                    if m == 0:
                        pe.wait_ge(o_ready, t + 1)
                        ws.wait_ready(pe, ready)
                        pe.wait_ge(q_read, t + 3 if not isinstance(t, int) or t < n_tiles - 2 else n_tiles)

                    def bank_read(b):
                        if is_last and m != 1:
                            pe.wait_ge(y_added, NB * KT * t + (NB * (m - 1 if m else 0) + b - 1))
                        if not is_last and m > 0:
                            pe.wait_ge(y_added, NB * KT * t + (NB * m + b - 1))

                    dense_part(chip, m % 2 if is_last else 0, 0, 1, m * P, slot, o_hi, o_lo, ws.begun if m == 0 else None,
                               bank_read).then_inc(out_full, 1)

                pe.wait_ge(kv_scaled, 3)

                def turn_v(i, p):
                    n = min(P, T - P * p)
                    if i or p >= 2:
                        pe.wait_ge(v_copied, NPAIR * i + p - 1)
                    nc.tensor.transpose(chip.banks[0:n, 6 + (NPAIR * i + p) % 2, 0:P], v_fm[:, i, P * p:P * p + n],
                                        chip.ident[:]).then_inc(v_turned, 1)

                turns = [(i, p) for i in range(KVP) for p in range(NPAIR)]
                for k in range(KT):
                    queries(0, 0, 2 * KVP + 1, k)
                    for i, p in turns[3 * k - 3:3 * k] if k else ():
                        if p == 0:
                            pe.wait_ge(kv_read, 4 * i + 4)
                        turn_v(i, p)
                pe.wait_ge(v_copied, NPAIR * KVP)
                pe.wait_ge(cache_in, 32)

                def chunks(t, i, q_unit=None, out_unit=None):
                    pe.wait_ge(q_ready, 2 * t + 2)
                    pe.wait_ge(sink_ready, t + 1)
                    for b in range(2):
                        nc.tensor.matmul(chip.banks[:, SCORE_BANK + b, WIN:WIN + 1], chip.ident[:], sink_col[:],
                                         start=True, stop=True)

                    def scores(c):
                        first, n, _ = window(c)
                        if c >= 2:
                            pe.wait_ge(exp_done, NCH * t + c - 1)
                        nc.tensor.matmul(chip.banks[:, SCORE_BANK + c % 2, WIN - n:WIN], q2[:, c],
                                         kT[:, i, first:first + n], start=True, stop=True).then_inc(scores_full, 1)

                    def turn(c):
                        pe.wait_ge(normed, NCH * t + c + 1)
                        if c >= 2:
                            pe.wait_ge(probT_ready, NCH * t + c - 1)
                        for j, (col, n, _) in enumerate(window(c)[2]):
                            n = P if j == 0 else n
                            mm = nc.tensor.transpose(chip.banks[0:n, TURN_BANK + c % 2, j * P:(j + 1) * P],
                                                     prob[:, c % 2, col:col + n], chip.ident[:])
                        mm.then_inc(probT_full, 1)

                    def output(c):
                        pe.wait_ge(probT_ready, NCH * t + c + 1)
                        if c >= 1:
                            pe.wait_ge(o_read, 2 * (NCH * t + c))
                        parts = window(c)[2]
                        for j, (_, n, v_tile) in enumerate(parts):
                            mm = nc.tensor.matmul(chip.banks[:, OUT_BANK, 0:P], v_tok[0:n, i, v_tile],
                                                  probT[0:n, c % 2, j], start=(j == 0), stop=(j == len(parts) - 1))
                        mm.then_inc(o_full, 1)

                    for c in range(NCH + 2):
                        if c < NCH:
                            scores(c)
                        if c < KT and q_unit is not None:
                            queries(t + 1, *q_unit, c)
                        if OUT_FROM <= c < OUT_FROM + KT and out_unit is not None:
                            out_tile(t - 1, *out_unit, c - OUT_FROM)
                        if 1 <= c <= NCH:
                            turn(c - 1)
                        if c >= 2:
                            output(c - 2)

                q_of = lambda t: (0, 2 * t + 2 * KVP + 1)
                out_of = lambda t: (1, 2 * t + 2 * KVP + 2)
                chunks(0, 0, q_unit=(1, 2 * KVP + 2))
                with pe.Fori(1, GROUP) as t:
                    chunks(t, 0, q_of(t), out_of(t))
                with pe.Fori(GROUP, n_tiles - 1) as t:
                    chunks(t, 1, q_of(t), out_of(t))
                chunks(n_tiles - 1, 1, out_unit=(0, 2 * KVP + 2 * n_tiles - 1))
                for m in range(KT):
                    out_tile(n_tiles - 1, 1, 2 * KVP + 2 * n_tiles, m, True)
                tail.tensor(pe)

            @block.scalar
            def _(act):
                act.sem_inc(o_hi_done, 1)
                norm.scalar(act)
                norm.free(act)
                act.wait_ge(const_in, 48)

                def place_queries(t):
                    act.wait_ge(q_read, t + 1)
                    act.wait_ge(bias_ready, t + 1)
                    if not isinstance(t, int) or t > 0:
                        act.wait_ge(scores_full, NCH * t)
                    nc.scalar.activation(q2[0:CHUNK, :, 0], q_flat[0:CHUNK, 0:T].rearrange("p (c n) -> p c n", n=CHUNK),
                                         ACT.Identity, bias=q_bias[0:CHUNK], scale=scale).then_inc(q_ready, 1)

                for i in range(KVP):
                    act.wait_ge(kv_scaled, 2 * i + 1)
                    k_bias = biases[:, n_tiles + i:n_tiles + i + 1]
                    nc.scalar.activation(kT[:, i, 0:SEQ], q_flat[:, 0:SEQ], ACT.Identity, bias=k_bias).then_inc(kv_read, 1)
                    nc.scalar.activation(kT[:, i, NEW0:KCOLS], q_flat[:, SEQ:T], ACT.Identity, bias=k_bias).then_inc(kv_read, 2)
                    act.wait_ge(kv_scaled, 2 * i + 2)
                    nc.scalar.activation(v_fm[:, i], v_fm[:, i], ACT.Identity,
                                         bias=biases[:, n_tiles + KVP + i:n_tiles + KVP + i + 1]).then_inc(kv_read, 1)
                act.wait_ge(pads_zero, 3)
                for i in range(KVP):
                    for p in range(NPAIR):
                        n = min(P, T - P * p)
                        act.wait_ge(v_turned, NPAIR * i + p + 1)
                        nc.scalar.copy(v_tok[0:n, i, p if p < n_full else n_full + 1],
                                       chip.banks[0:n, 6 + (NPAIR * i + p) % 2, 0:P]).then_inc(v_copied, 1)
                place_queries(0)

                def chunks(t, next_queries):

                    def exps(c):
                        act.wait_ge(maxed, NCH * t + c + 1)
                        if c >= 2:
                            act.wait_ge(probT_full, NCH * t + c - 1)
                        nc.scalar.activation(prob[:, c % 2, prob_cols(c)],
                                             chip.banks[:, SCORE_BANK + c % 2, WIN - window(c)[1]:WIN + 1],
                                             ACT.Exp, bias=neg_max[:, c:c + 1],
                                             accum_out=p_sum[:, c:c + 1]).then_inc(exp_done, 1)

                    def copy_turned(c):
                        parts = window(c)[2]
                        act.wait_ge(probT_full, NCH * t + c + 1)
                        if c >= 2:
                            act.wait_ge(o_full, NCH * t + c - 1)
                        src = chip.banks[:, TURN_BANK + c % 2, 0:2 * P].rearrange("p (j n) -> p j n", j=2)
                        if len(parts) == 1 or parts[0][1] == parts[1][1]:
                            n = parts[0][1]
                            nc.scalar.copy(probT[0:n, c % 2, 0:len(parts)], src[0:n, 0:len(parts)]).then_inc(probT_ready, 1)
                        else:
                            nc.scalar.copy(probT[:, c % 2, 0], src[:, 0])
                            nc.scalar.copy(probT[0:CHUNK, c % 2, 1], src[0:CHUNK, 1]).then_inc(probT_ready, 1)

                    def take_output(c):
                        act.wait_ge(o_full, NCH * t + c + 1)
                        if c == 0 and (not isinstance(t, int) or t > 0):
                            act.wait_ge(o_ready, t)
                        for a in range(2):
                            rows = slice(a * CHUNK, (a + 1) * CHUNK)
                            nc.scalar.copy(o[rows, CHUNK * c:CHUNK * (c + 1)],
                                           chip.banks[rows, OUT_BANK, rows]).then_inc(o_read, 1)

                    for c in range(NCH + 2):
                        if c < NCH:
                            exps(c)
                        if c == NCH - 1 and next_queries:
                            place_queries(t + 1)
                        if 1 <= c <= NCH:
                            copy_turned(c - 1)
                        if c >= 2:
                            take_output(c - 2)
                    act.wait_ge(o_read, 2 * NCH * (t + 1))
                    if not isinstance(t, int) or t > 0:
                        act.wait_ge(out_full, KT * t)
                    nc.scalar.copy(o_hi[:, 0], o[:]).then_inc(o_hi_done, 1)

                chunks(0, True)
                with act.Fori(1, n_tiles - 1) as t:
                    chunks(t, True)
                chunks(n_tiles - 1, False)
                tail.scalar(act)

            @block.vector
            def _(dve):
                dve.sem_inc(y_added, 1)
                norm.vector(dve)
                norm.free(dve)

                def tile_bias(t):
                    at = bass.ds(t, 1) if not isinstance(t, int) else slice(t, t + 1)
                    nc.vector.tensor_scalar(q_bias[:], biases[:, at], scale, None, ALU.mult).then_inc(bias_ready, 1)

                def take_queries(t):
                    dve.wait_ge(q_full, t + 1)
                    if isinstance(t, int):
                        dve.wait_ge(pads_zero, 3)
                    if not isinstance(t, int) or t > 0:
                        dve.wait_ge(q_ready, 2 * t)
                    nc.vector.tensor_tensor(blocks_of(q_flat[:]), chip.psum_set(0), blocks_of(norm.keep[:]),
                                            ALU.mult).then_inc(q_read, 1)

                def place_queries(t):
                    if not isinstance(t, int) or t > 0:
                        dve.wait_ge(scores_full, NCH * t)
                    dve.wait_ge(q_read, t + 1)
                    dve.wait_ge(bias_ready, t + 1)
                    nc.vector.tensor_scalar(q2[CHUNK:P, :, 1], q_flat[CHUNK:P, 0:T].rearrange("p (c n) -> p c n", n=CHUNK),
                                            scale, q_bias[CHUNK:P], ALU.mult, ALU.add).then_inc(q_ready, 1)
                    at = bass.ds(t, 1) if not isinstance(t, int) else slice(t, t + 1)
                    nc.vector.tensor_scalar(sink_col[:], sinks[:, at], 1.0, None, ALU.mult).then_inc(sink_ready, 1)

                norm.kept_ready(dve)
                for i in range(KVP):
                    for n in range(2):
                        dve.wait_ge(kv_full, 2 * i + n + 1)
                        if i and n == 0:
                            dve.wait_ge(kv_read, 3)
                        nc.vector.tensor_tensor(blocks_of(v_fm[:, i] if n else q_flat[:]), chip.psum_set(n),
                                                blocks_of(norm.keep[:]), ALU.mult).then_inc(kv_scaled, 1)
                dve.wait_ge(kv_read, 7)
                dve.wait_ge(const_in, 48)
                dve.wait_ge(y_zero, 1)
                tile_bias(0)
                take_queries(0)
                place_queries(0)
                for k in range(KT):
                    nc.vector.tensor_scalar(chip.y[:, k], chip.y[:, k], out_bias[:, k:k + 1], None, ALU.add).then_inc(y_bias, 1)
                dve.wait_ge(y_bias, KT)

                def add_output(t, m, s=0):
                    dve.wait_ge(out_full, KT * t + m + 1)
                    for b in range(NB):
                        cols = slice(b * BW, (b + 1) * BW)
                        nc.vector.tensor_tensor(chip.y[:, m, cols], chip.banks[:, 3 * s + b, 0:BW], chip.y[:, m, cols],
                                                ALU.add).then_inc(y_added, 1)

                def chunks(t, has_next, has_last):

                    def row_max(c):
                        n = window(c)[1]
                        dve.wait_ge(scores_full, NCH * t + c + 1)
                        nc.vector.tensor_reduce(neg_max[:, c:c + 1], chip.banks[:, SCORE_BANK + c % 2, WIN - n:WIN + 1],
                                                AX_X, ALU.max, negate=True).then_inc(maxed, 1)

                    def normalize(c):
                        cols = prob_cols(c)
                        keys = slice(cols.start, cols.stop - 1)
                        dve.wait_ge(exp_done, NCH * t + c + 1)
                        nc.vector.reciprocal(p_inv[:, c:c + 1], p_sum[:, c:c + 1]).then_inc(inverted, 1)
                        dve.wait_ge(inverted, NCH * t + c + 1)
                        nc.vector.tensor_scalar(prob[:, c % 2, keys], prob[:, c % 2, keys], p_inv[:, c:c + 1], None,
                                                ALU.mult).then_inc(normed, 1)

                    for c in range(NCH + 2):
                        if c < NCH:
                            row_max(c)
                        if 1 <= c < NCH:
                            normalize(c - 1)
                        if c == NCH - 1:
                            normalize(c)
                        if c == KT and has_next:
                            dve.wait_ge(q_ready, 2 * t + 2)
                            tile_bias(t + 1)
                            take_queries(t + 1)
                        if c == NCH - 1 and has_next:
                            place_queries(t + 1)
                        if OUT_FROM <= c < OUT_FROM + KT - 1 and has_last:
                            add_output(t - 1, c - OUT_FROM)
                        if c == OUT_FROM + KT and has_last:
                            add_output(t - 1, KT - 1)
                        if c == 0 and has_last:
                            dve.wait_ge(o_hi_done, t + 1)
                            nc.vector.tensor_tensor(o_lo[:, 0], o[:], o_hi[:, 0].bitcast(F32), ALU.subtract).then_inc(o_ready, 1)

                chunks(0, True, False)
                with dve.Fori(1, n_tiles - 1) as t:
                    chunks(t, True, True)
                chunks(n_tiles - 1, False, True)
                dve.wait_ge(o_hi_done, n_tiles + 1)
                nc.vector.tensor_tensor(o_lo[:, 0], o[:], o_hi[:, 0].bitcast(F32), ALU.subtract).then_inc(o_ready, 1)
                for m in range(KT):
                    add_output(n_tiles - 1, m, m % 2)
                tail.vector(dve)
    tail.close()
    ws.base += 2 * KVP + 2 * n_tiles


def build(nc, ins, outs):
    with ExitStack() as ctx:
        chip = Chip(nc, ctx, ins["units"])
        const_in = chip.sem("const_in")
        with nc.Block() as block:

            @block.sync
            def _(sp):
                sp.dma_start(chip.ones[:], ins["ones"]).then_inc(const_in, 16)
                sp.dma_start(chip.ident[:], ins["ident"]).then_inc(const_in, 16)
                sp.dma_start(chip.gains[:], ins["gains"]).then_inc(const_in, 16)
                sp.wait_ge(const_in, 48)

        everything = dict(ins)
        everything.update(outs)
        x_parts = (ins["x_prompt"], ins["x_sample"])

        norm = Norm(chip, "gla_norm", None, 0, x_parts=x_parts)
        gla(chip, "gla", everything, norm)
        norm.close()
        norm = Norm(chip, "mlp0_norm", 1, 2, x_parts=x_parts)
        mlp(chip, "mlp0", norm, False)
        norm.close()
        norm = Norm(chip, "swa_norm", 3, 4)
        swa(chip, "swa", everything, norm)
        norm.close()
        norm = Norm(chip, "mlp1_norm", 5, 6)
        mlp(chip, "mlp1", norm, True)
        norm.close()
        result(chip, "result", (outs["y_prompt"], outs["y_sample"]))


OUT_SHAPES = {
    "y_prompt": (P, KT, SEQ), "y_sample": (P, KT, DEC),
    "state_prompt": (GH, P, DV), "state_sample": (GH, P, DV),
    "k_prompt": (P, KVP, P), "v_prompt": (P, KVP, P), "k_sample": (P, KVP, P), "v_sample": (P, KVP, P),
}


def features_first(a):
    return np.ascontiguousarray(a.T.reshape(KT, P, -1).transpose(1, 0, 2))


def k_units(w):
    return w.reshape(-1, P, w.shape[1]).transpose(1, 0, 2).reshape(P, -1)


def laid_out(inputs):
    a = {name: np.asarray(value) for name, value in inputs.items()}
    dqk = GH * P
    w_in, w_out = a["gla_w_in"][0], a["gla_w_out"][0]
    gla_units = []
    for h in range(GH):
        q, k = w_in[:, h * P:(h + 1) * P], w_in[:, dqk + h * P:dqk + (h + 1) * P]
        v, r = (w_in[:, s + h * DV:s + (h + 1) * DV] for s in (2 * dqk, 2 * dqk + GH * DV))
        o = w_out[h * DV:(h + 1) * DV]
        gla_units += [k_units(x) for x in (k, q, v[:, :P], v[:, P:], r[:, :P], r[:, P:])]
        gla_units += [k_units(x) for x in (before[:, :512], before[:, 512:])] if h else []
        before = o
    gla_units += [k_units(x) for x in (o[:, :512], o[:, 512:])]

    s_in, s_out, s_b = a["swa_w_in"][0], a["swa_w_out"][0], a["swa_b_in"][0]
    n_q = s_out.shape[0]
    heads = [(8 * i + g, 8 * i + GROUP + g) for i in range(KVP) for g in range(GROUP)]
    rows = [np.concatenate([np.arange(64 * h, 64 * h + 64) for h in pair]) for pair in heads]
    kv = [n_q + np.arange(P * i, P * (i + 1)) for i in range(2 * KVP)]
    q_unit = lambda t: k_units(s_in[:, rows[t]])
    out_unit = lambda t: s_out[rows[t]]
    swa_units = [k_units(s_in[:, kv[n]]) for n in (0, KVP, 1, KVP + 1)] + [q_unit(0), q_unit(1)]
    n_tiles = len(heads)
    for t in range(1, n_tiles - 1):
        swa_units += [q_unit(t + 1), out_unit(t - 1)]
    swa_units += [out_unit(n_tiles - 2), out_unit(n_tiles - 1)]
    mlp_units = []
    for up, down in zip(a["mlp_w_up"], a["mlp_w_down"]):
        for g in range(FF_GROUPS):
            f = slice(g * FF_TILES * P, (g + 1) * FF_TILES * P)
            mlp_units += [k_units(x) for x in np.split(up[:, f], FF_TILES, 1)]
            mlp_units += [k_units(x) for x in np.split(down[f], KT // 2, 1)]

    m, l = np.arange(P)[:, None], np.arange(P)[None, :]
    masks = [(m // (2 * s) == l // (2 * s)) & (m % (2 * s) < s) & (l % (2 * s) >= s) for s in HALVES] + [m == l]
    pack = lambda x: np.ascontiguousarray(x)
    return {
        "ones": np.ones((P, P), np.float32), "ident": np.eye(P, dtype=np.float32),
        "masks": pack(np.stack(masks, 1).astype(np.float32)),
        "gains": pack(a["norm_g"].reshape(8, KT, P).transpose(2, 0, 1)),
        "x_prompt": features_first(a["x_prompt"][0]), "x_sample": features_first(a["x_sample"][0]),
        "units": np.stack(gla_units + mlp_units[:8 * FF_GROUPS] + swa_units + mlp_units[8 * FF_GROUPS:]), "gate_a": pack(a["gla_w_gate_a"][0].reshape(KT, P, RANK).transpose(1, 0, 2)).reshape(P, -1),
        "gate_b": pack(a["gla_w_gate_b"][0].reshape(RANK, GH, P).transpose(1, 0, 2)),
        "gate_bias": pack(a["gla_b_gate"][0].reshape(GH, P, 1)),
        "gla_gain": pack(a["gla_g_onorm"][0].reshape(GH, 2, P).transpose(0, 2, 1)), "state_gla": a["state_gla"][0, 0],
        "swa_bias": pack(s_b[np.stack(rows + kv)].T),
        "swa_out_bias": pack(a["swa_b_out"][0].reshape(KT, P).T),
        "sinks": pack(np.repeat(a["swa_sinks"][0][np.array(heads)], 64, 1).T),
        "cache_k": pack(a["cache_swa_k"][0, 0].reshape(P, KVP, P).transpose(2, 1, 0)),
        "cache_v": pack(a["cache_swa_v"][0, 0].reshape(P, KVP, P)),
    }


def kernel(**inputs):
    import concourse.bacc as bacc
    from concourse.bass_utils import run_bass_kernel_spmd

    nc = bacc.Bacc("TRN2", target_bir_lowering=False, num_devices=1)
    arrays = {f"in_{name}": array for name, array in laid_out(inputs).items()}
    ins = {name[3:]: nc.dram_tensor(name, array.shape, mybir.dt.from_np(array.dtype), kind="ExternalInput").ap()
           for name, array in arrays.items()}
    outs = {name: nc.dram_tensor(f"out_{name}", shape, F32, kind="ExternalOutput").ap()
            for name, shape in OUT_SHAPES.items()}
    build(nc, ins, outs)
    result = run_bass_kernel_spmd(nc, [arrays], core_ids=[0]).results[0]
    got = {name: np.asarray(result[f"out_{name}"]) for name in OUT_SHAPES}

    tokens_first = lambda x: np.ascontiguousarray(x.transpose(1, 0, 2).reshape(D, -1).T)[None]
    keys_first = lambda x: np.ascontiguousarray(x.transpose(2, 1, 0)).reshape(1, 1, P, 2 * KVP, 64)
    return (tokens_first(got["y_prompt"]), tokens_first(got["y_sample"]),
            got["state_prompt"][None, None], got["state_sample"][None, None],
            keys_first(got["k_prompt"]), got["v_prompt"].reshape(1, 1, P, 2 * KVP, 64),
            keys_first(got["k_sample"]), got["v_sample"].reshape(1, 1, P, 2 * KVP, 64))
```
